# Optimizing a Trainium2 kernel written in Bass

```python
import jax, jax.numpy as jnp
from jax import lax
import numpy as np

D_MODEL = 1024
BATCH = 1
SEQ = 256
DEPTH = 2

CHUNK = 64
CONV_CH = 512
CONV_WIDTH = 3
GLA_HEADS = 4
GLA_DK = 64
GLA_DV = 128
GLA_KW = GLA_HEADS * GLA_DK
GLA_VW = GLA_HEADS * GLA_DV
GATE_RANK = 16
GATE_NORMALIZER = 16.0
GATE_LOG_MIN = -1.0
MIX_WIDTH = CONV_CH + GLA_VW
IN_WIDTH = 3 * CONV_CH + 2 * GLA_KW + 2 * GLA_VW + GATE_RANK
IN_SPLITS = (
    CONV_CH,
    2 * CONV_CH,
    3 * CONV_CH,
    3 * CONV_CH + GLA_KW,
    3 * CONV_CH + 2 * GLA_KW,
    3 * CONV_CH + 2 * GLA_KW + GLA_VW,
    3 * CONV_CH + 2 * GLA_KW + 2 * GLA_VW,
)
D_FF = 2816
N_EXPERTS = 8
TOP_K = 2
D_FF_EXPERT = 2816
N_DENSE = (DEPTH + 1) // 2
N_MOE = DEPTH // 2
DEEPNORM_ALPHA = (2.0 * DEPTH) ** 0.25
DEEPNORM_BETA = (8.0 * DEPTH) ** -0.25
LN_EPS = 1e-5
RMS_EPS = 1e-6


def _layernorm(x, g, b):
    xf = x.astype(jnp.float32)
    mu = jnp.mean(xf, axis=-1, keepdims=True)
    var = jnp.mean(jnp.square(xf - mu), axis=-1, keepdims=True)
    return ((xf - mu) * lax.rsqrt(var + LN_EPS) * g.astype(jnp.float32)
            + b.astype(jnp.float32)).astype(x.dtype)

def _causal_depthwise_conv(z, w):
    return lax.conv_general_dilated(
        z, w[:, None, :].astype(z.dtype), window_strides=(1,),
        padding=[(CONV_WIDTH - 1, 0)],
        dimension_numbers=("NWC", "WIO", "NWC"),
        feature_group_count=z.shape[-1])

def _gla_chunked(q, k, v, gk):
    bsz, seq = q.shape[0], q.shape[1]
    n_chunks = seq // CHUNK
    shp_k = (bsz, n_chunks, CHUNK, GLA_HEADS, GLA_DK)
    shp_v = (bsz, n_chunks, CHUNK, GLA_HEADS, GLA_DV)
    q = q.astype(jnp.float32).reshape(shp_k) * (GLA_DK ** -0.5)
    k = k.astype(jnp.float32).reshape(shp_k)
    v = v.astype(jnp.float32).reshape(shp_v)
    b = jnp.cumsum(gk.astype(jnp.float32).reshape(shp_k), axis=2)
    b_last = b[:, :, -1:]
    q_in = q * jnp.exp(b)
    k_in = k * jnp.exp(-b)
    k_out = k * jnp.exp(b_last - b)
    causal = jnp.tril(jnp.ones((CHUNK, CHUNK), dtype=bool))
    scores = jnp.einsum("bnihd,bnjhd->bnhij", q_in, k_in)
    scores = jnp.where(causal, scores, 0.0)
    o_intra = jnp.einsum("bnhij,bnjhv->bnihv", scores, v)
    kv_chunk = jnp.einsum("bnjhd,bnjhv->bnhdv", k_out, v)
    decay_chunk = jnp.exp(b_last[:, :, 0])

    def step(state, inp):
        kv_n, dec_n = inp
        return dec_n[..., None] * state + kv_n, state

    init = jnp.zeros((bsz, GLA_HEADS, GLA_DK, GLA_DV), jnp.float32)
    _, states = lax.scan(step, init, (jnp.swapaxes(kv_chunk, 0, 1), jnp.swapaxes(decay_chunk, 0, 1)))
    states = jnp.swapaxes(states, 0, 1)
    o_inter = jnp.einsum("bnihd,bnhdv->bnihv", q_in, states)
    return (o_intra + o_inter).reshape(bsz, seq, GLA_HEADS, GLA_DV)

def _mixer(u, w_in, conv_w, gk_w2, gk_b, gla_norm_w, w_out):
    bsz, seq, _ = u.shape
    proj = jnp.einsum("bsd,de->bse", u, w_in)
    c_b, c_c, c_h, q, k, v, g, g_low = jnp.split(proj, IN_SPLITS, axis=-1)
    y_conv = c_b * _causal_depthwise_conv(c_c * c_h, conv_w)
    gk = jax.nn.log_sigmoid((jnp.einsum("bsr,rk->bsk", g_low, gk_w2) + gk_b).astype(jnp.float32))
    gk = jnp.maximum(gk / GATE_NORMALIZER, GATE_LOG_MIN)
    o = _gla_chunked(q.reshape(bsz, seq, GLA_HEADS, GLA_DK),
                     k.reshape(bsz, seq, GLA_HEADS, GLA_DK),
                     v.reshape(bsz, seq, GLA_HEADS, GLA_DV),
                     gk.reshape(bsz, seq, GLA_HEADS, GLA_DK))
    o = o * lax.rsqrt(jnp.mean(jnp.square(o), axis=-1, keepdims=True) + RMS_EPS)
    o = o * gla_norm_w.astype(jnp.float32) * jax.nn.silu(
        g.astype(jnp.float32).reshape(bsz, seq, GLA_HEADS, GLA_DV))
    y_gla = o.reshape(bsz, seq, GLA_VW).astype(u.dtype)
    y = jnp.concatenate([y_conv, y_gla], axis=-1)
    return jnp.einsum("bse,ed->bsd", y, w_out)

def _dense_swiglu(u, w_gate, w_up, w_down):
    h = jax.nn.silu(jnp.einsum("bsd,df->bsf", u, w_gate)) * jnp.einsum("bsd,df->bsf", u, w_up)
    return jnp.einsum("bsf,fd->bsd", h, w_down)

def _moe_swiglu(u, w_router, w_gate, w_up, w_down):
    bsz, seq, dm = u.shape
    n_tok = bsz * seq
    xt = u.reshape(n_tok, dm)
    logits = jnp.dot(xt, w_router).astype(jnp.float32)
    top_logits, top_idx = lax.top_k(logits, TOP_K)
    top_w = jax.nn.softmax(top_logits, axis=-1).astype(u.dtype)
    flat_e = top_idx.reshape(-1)
    order = jnp.argsort(flat_e)
    tok = order // TOP_K
    group_sizes = jnp.bincount(flat_e, length=N_EXPERTS).astype(jnp.int32)
    xs = xt[tok]
    h = jax.nn.silu(lax.ragged_dot(xs, w_gate, group_sizes)) * lax.ragged_dot(xs, w_up, group_sizes)
    ys = lax.ragged_dot(h, w_down, group_sizes) * top_w.reshape(-1)[order][:, None]
    out = jax.ops.segment_sum(ys, tok, num_segments=n_tok)
    return out.reshape(bsz, seq, dm)

def first_inputs(seed: int = 0) -> dict:
    key = jax.random.key(seed)
    ks = jax.random.split(key, 24)
    nrm = jax.random.normal
    f32 = jnp.float32
    x = nrm(ks[0], (BATCH, SEQ, D_MODEL), f32)
    c = nrm(ks[1], (BATCH, D_MODEL), f32)
    ada_w = nrm(ks[2], (DEPTH, D_MODEL, 6 * D_MODEL), f32) * (0.1 * D_MODEL ** -0.5)
    ada_b = nrm(ks[3], (DEPTH, 6 * D_MODEL), f32) * 0.02
    w_in = nrm(ks[4], (DEPTH, D_MODEL, IN_WIDTH), f32) * D_MODEL ** -0.5
    conv_w = nrm(ks[5], (DEPTH, CONV_WIDTH, CONV_CH), f32) * CONV_WIDTH ** -0.5
    gk_w2 = nrm(ks[6], (DEPTH, GATE_RANK, GLA_KW), f32) * GATE_RANK ** -0.5
    gk_b = nrm(ks[7], (DEPTH, GLA_KW), f32) * 0.02
    gla_norm_w = 1.0 + 0.02 * nrm(ks[8], (DEPTH, GLA_DV), f32)
    w_out = nrm(ks[9], (DEPTH, MIX_WIDTH, D_MODEL), f32) * (DEEPNORM_BETA * MIX_WIDTH ** -0.5)
    ln1_g = 1.0 + 0.02 * nrm(ks[10], (DEPTH, D_MODEL), f32)
    ln1_b = 0.02 * nrm(ks[11], (DEPTH, D_MODEL), f32)
    ln2_g = 1.0 + 0.02 * nrm(ks[12], (DEPTH, D_MODEL), f32)
    ln2_b = 0.02 * nrm(ks[13], (DEPTH, D_MODEL), f32)
    ffn_w_gate = nrm(ks[14], (N_DENSE, D_MODEL, D_FF), f32) * D_MODEL ** -0.5
    ffn_w_up = nrm(ks[15], (N_DENSE, D_MODEL, D_FF), f32) * D_MODEL ** -0.5
    ffn_w_down = nrm(ks[16], (N_DENSE, D_FF, D_MODEL), f32) * (DEEPNORM_BETA * D_FF ** -0.5)
    router_w = nrm(ks[17], (N_MOE, D_MODEL, N_EXPERTS), f32) * D_MODEL ** -0.5
    moe_w_gate = nrm(ks[18], (N_MOE, N_EXPERTS, D_MODEL, D_FF_EXPERT), f32) * D_MODEL ** -0.5
    moe_w_up = nrm(ks[19], (N_MOE, N_EXPERTS, D_MODEL, D_FF_EXPERT), f32) * D_MODEL ** -0.5
    moe_w_down = nrm(ks[20], (N_MOE, N_EXPERTS, D_FF_EXPERT, D_MODEL), f32) * (DEEPNORM_BETA * D_FF_EXPERT ** -0.5)
    return {"x": x, "c": c, "ada_w": ada_w, "ada_b": ada_b, "w_in": w_in, "conv_w": conv_w,
            "gk_w2": gk_w2, "gk_b": gk_b, "gla_norm_w": gla_norm_w, "w_out": w_out,
            "ln1_g": ln1_g, "ln1_b": ln1_b, "ln2_g": ln2_g, "ln2_b": ln2_b,
            "ffn_w_gate": ffn_w_gate, "ffn_w_up": ffn_w_up, "ffn_w_down": ffn_w_down,
            "router_w": router_w, "moe_w_gate": moe_w_gate, "moe_w_up": moe_w_up,
            "moe_w_down": moe_w_down}

def first_block(x, c, ada_w, ada_b, w_in, conv_w, gk_w2, gk_b, gla_norm_w, w_out,
              ln1_g, ln1_b, ln2_g, ln2_b, ffn_w_gate, ffn_w_up, ffn_w_down,
              router_w, moe_w_gate, moe_w_up, moe_w_down):
    cond = jax.nn.silu(c)
    for layer in range(DEPTH):
        mod = (jnp.dot(cond, ada_w[layer]) + ada_b[layer])[:, None, :]
        sh1, sc1, g1, sh2, sc2, g2 = jnp.split(mod, 6, axis=-1)
        u = x * (1.0 + sc1) + sh1
        mix = _mixer(u, w_in[layer], conv_w[layer], gk_w2[layer], gk_b[layer],
                     gla_norm_w[layer], w_out[layer])
        x = _layernorm(DEEPNORM_ALPHA * x + (1.0 + g1) * mix, ln1_g[layer], ln1_b[layer])
        u = x * (1.0 + sc2) + sh2
        j = layer // 2
        if layer % 2 == 0:
            ff = _dense_swiglu(u, ffn_w_gate[j], ffn_w_up[j], ffn_w_down[j])
        else:
            ff = _moe_swiglu(u, router_w[j], moe_w_gate[j], moe_w_up[j], moe_w_down[j])
        x = _layernorm(DEEPNORM_ALPHA * x + (1.0 + g2) * ff, ln2_g[layer], ln2_b[layer])
    return x


N_A = DEPTH // 2
N_B = DEPTH - N_A
PLE_DIM = 256
FOX_HEADS = 16
FOX_HEAD_DIM = D_MODEL // FOX_HEADS
FOX_IN = 3 * D_MODEL + FOX_HEADS
FOX_GATE_BIAS = 3.0
MLA_HEADS = 16
QK_NOPE_DIM = 128
QK_ROPE_DIM = 64
V_HEAD_DIM = 128
Q_LORA_RANK = 384
KV_LORA_RANK = 256
ROPE_THETA = 10000.0
BLOCK_Q = 128
ALPHA = (2 * DEPTH) ** 0.25
BETA = (8 * DEPTH) ** -0.25


def layer_norm(x, g, b):
    xf = x.astype(jnp.float32)
    mu = jnp.mean(xf, axis=-1, keepdims=True)
    xc = xf - mu
    var = jnp.mean(xc * xc, axis=-1, keepdims=True)
    y = xc * lax.rsqrt(var + LN_EPS) * g.astype(jnp.float32) + b.astype(jnp.float32)
    return y.astype(x.dtype)

def rms_norm(x, g):
    xf = x.astype(jnp.float32)
    y = xf * lax.rsqrt(jnp.mean(xf * xf, axis=-1, keepdims=True) + RMS_EPS) * g.astype(jnp.float32)
    return y.astype(x.dtype)

def post_norm(x, delta, g, b):
    return layer_norm(ALPHA * x + delta, g, b)

def swiglu(x, w_in, w_out):
    h = x @ w_in
    gate, up = h[..., :D_FF], h[..., D_FF:]
    return (jax.nn.silu(gate) * up) @ w_out

def rope_tables(seq_len):
    half = QK_ROPE_DIM // 2
    inv = ROPE_THETA ** (-jnp.arange(half, dtype=jnp.float32) * (2.0 / QK_ROPE_DIM))
    ang = jnp.arange(seq_len, dtype=jnp.float32)[:, None] * inv[None, :]
    return jnp.cos(ang), jnp.sin(ang)

def rope(x, cos, sin):
    half = x.shape[-1] // 2
    xf = x.astype(jnp.float32)
    x1, x2 = xf[..., :half], xf[..., half:]
    return jnp.concatenate([x1 * cos - x2 * sin, x2 * cos + x1 * sin], axis=-1).astype(x.dtype)

def causal_block_attention(score_fn, v):
    B, S, H, Dv = v.shape
    n_blocks = S // BLOCK_Q
    k_pos = jnp.arange(S)

    def one_block(blk):
        start = blk * BLOCK_Q
        s = score_fn(start)
        q_pos = start + jnp.arange(BLOCK_Q)
        s = jnp.where(k_pos[None, :] <= q_pos[:, None], s, -jnp.inf)
        w = jax.nn.softmax(s, axis=-1).astype(v.dtype)
        return jnp.einsum('bhqk,bkhd->bqhd', w, v)

    o = lax.map(one_block, jnp.arange(n_blocks))
    return jnp.moveaxis(o, 0, 1).reshape(B, S, H, Dv)

def fox_mixer(x, w_in, b_f, w_o):
    B, S, _ = x.shape
    h = x @ w_in
    q = h[..., :D_MODEL].reshape(B, S, FOX_HEADS, FOX_HEAD_DIM)
    k = h[..., D_MODEL:2 * D_MODEL].reshape(B, S, FOX_HEADS, FOX_HEAD_DIM)
    v = h[..., 2 * D_MODEL:3 * D_MODEL].reshape(B, S, FOX_HEADS, FOX_HEAD_DIM)
    f_logit = h[..., 3 * D_MODEL:].astype(jnp.float32) + b_f.astype(jnp.float32)
    cum = jnp.cumsum(jax.nn.log_sigmoid(f_logit), axis=1).transpose(0, 2, 1)
    scale = FOX_HEAD_DIM ** -0.5

    def scores(start):
        qb = lax.dynamic_slice_in_dim(q, start, BLOCK_Q, axis=1)
        cb = lax.dynamic_slice_in_dim(cum, start, BLOCK_Q, axis=2)
        s = jnp.einsum('bqhd,bkhd->bhqk', qb, k).astype(jnp.float32) * scale
        return s + cb[:, :, :, None] - cum[:, :, None, :]

    o = causal_block_attention(scores, v)
    return o.reshape(B, S, D_MODEL) @ w_o

def shared_kv(x, w_down, kv_norm, w_up, cos, sin):
    B, S, _ = x.shape
    h = x @ w_down
    c_kv = rms_norm(h[..., :KV_LORA_RANK], kv_norm)
    k_rope = rope(h[..., KV_LORA_RANK:], cos, sin)
    kv = jnp.einsum('bsc,chd->bshd', c_kv, w_up)
    return kv[..., :QK_NOPE_DIM], k_rope, kv[..., QK_NOPE_DIM:]

def mla_mixer(x, w_dq, q_norm, w_uq, w_o, k_nope, k_rope, v, cos, sin):
    B, S, _ = x.shape
    c_q = rms_norm(x @ w_dq, q_norm)
    q = jnp.einsum('bsc,chd->bshd', c_q, w_uq)
    q_nope = q[..., :QK_NOPE_DIM]
    q_rope = rope(q[..., QK_NOPE_DIM:], cos[:, None, :], sin[:, None, :])
    scale = (QK_NOPE_DIM + QK_ROPE_DIM) ** -0.5

    def scores(start):
        qn = lax.dynamic_slice_in_dim(q_nope, start, BLOCK_Q, axis=1)
        qr = lax.dynamic_slice_in_dim(q_rope, start, BLOCK_Q, axis=1)
        s = jnp.einsum('bqhd,bkhd->bhqk', qn, k_nope) + jnp.einsum('bqhr,bkr->bhqk', qr, k_rope)
        return s.astype(jnp.float32) * scale

    o = causal_block_attention(scores, v)
    return o.reshape(B, S, MLA_HEADS * V_HEAD_DIM) @ w_o

def second_inputs(seed: int = 0) -> dict:
    key = jax.random.key(seed)
    ks = iter(jax.random.split(key, 32))
    f32 = jnp.float32

    def nrm(shape, fan_in, scale=1.0):
        return jax.random.normal(next(ks), shape, f32) * (scale * fan_in ** -0.5)

    def gain(shape):
        return 1.0 + 0.02 * jax.random.normal(next(ks), shape, f32)

    def small(shape, s=0.02):
        return s * jax.random.normal(next(ks), shape, f32)

    x = jax.random.normal(next(ks), (BATCH, SEQ, D_MODEL), f32)
    p = jax.random.normal(next(ks), (DEPTH, BATCH, SEQ, PLE_DIM), f32)
    ffn1_w_in = nrm((DEPTH, D_MODEL, 2 * D_FF), D_MODEL)
    ffn1_w_out = nrm((DEPTH, D_FF, D_MODEL), D_FF, BETA)
    ffn2_w_in = nrm((DEPTH, D_MODEL, 2 * D_FF), D_MODEL)
    ffn2_w_out = nrm((DEPTH, D_FF, D_MODEL), D_FF, BETA)
    ln_g = gain((DEPTH, 4, D_MODEL))
    ln_b = small((DEPTH, 4, D_MODEL))
    ple_w_gate = nrm((DEPTH, D_MODEL, D_MODEL), D_MODEL)
    ple_b_gate = small((DEPTH, D_MODEL))
    ple_w_proj = nrm((DEPTH, PLE_DIM, D_MODEL), PLE_DIM, BETA)
    fox_w_in = nrm((N_A, D_MODEL, FOX_IN), D_MODEL)
    fox_w_in = fox_w_in.at[:, :, 2 * D_MODEL:3 * D_MODEL].multiply(BETA)
    fox_b_f = FOX_GATE_BIAS + 0.5 * jax.random.normal(next(ks), (N_A, FOX_HEADS), f32)
    fox_w_o = nrm((N_A, D_MODEL, D_MODEL), D_MODEL, BETA)
    mla_w_dq = nrm((N_B, D_MODEL, Q_LORA_RANK), D_MODEL)
    mla_q_norm = gain((N_B, Q_LORA_RANK))
    mla_w_uq = nrm((N_B, Q_LORA_RANK, MLA_HEADS, QK_NOPE_DIM + QK_ROPE_DIM), Q_LORA_RANK)
    mla_w_o = nrm((N_B, MLA_HEADS * V_HEAD_DIM, D_MODEL), MLA_HEADS * V_HEAD_DIM, BETA)
    kv_w_down = nrm((D_MODEL, KV_LORA_RANK + QK_ROPE_DIM), D_MODEL)
    kv_norm = gain((KV_LORA_RANK,))
    kv_w_up = nrm((KV_LORA_RANK, MLA_HEADS, QK_NOPE_DIM + V_HEAD_DIM), KV_LORA_RANK)
    kv_w_up = kv_w_up.at[:, :, QK_NOPE_DIM:].multiply(BETA)
    return {'x': x, 'p': p,
            'ffn1_w_in': ffn1_w_in, 'ffn1_w_out': ffn1_w_out,
            'ffn2_w_in': ffn2_w_in, 'ffn2_w_out': ffn2_w_out,
            'ln_g': ln_g, 'ln_b': ln_b,
            'ple_w_gate': ple_w_gate, 'ple_b_gate': ple_b_gate, 'ple_w_proj': ple_w_proj,
            'fox_w_in': fox_w_in, 'fox_b_f': fox_b_f, 'fox_w_o': fox_w_o,
            'mla_w_dq': mla_w_dq, 'mla_q_norm': mla_q_norm, 'mla_w_uq': mla_w_uq, 'mla_w_o': mla_w_o,
            'kv_w_down': kv_w_down, 'kv_norm': kv_norm, 'kv_w_up': kv_w_up}

def second_block(x, p, ffn1_w_in, ffn1_w_out, ffn2_w_in, ffn2_w_out, ln_g, ln_b,
              ple_w_gate, ple_b_gate, ple_w_proj, fox_w_in, fox_b_f, fox_w_o,
              mla_w_dq, mla_q_norm, mla_w_uq, mla_w_o, kv_w_down, kv_norm, kv_w_up):
    S = x.shape[1]
    cos, sin = rope_tables(S)
    k_nope = k_rope = v_shared = None
    for i in range(DEPTH):
        if i == N_A:
            k_nope, k_rope, v_shared = shared_kv(x, kv_w_down, kv_norm, kv_w_up, cos, sin)
        x = post_norm(x, 0.5 * swiglu(x, ffn1_w_in[i], ffn1_w_out[i]), ln_g[i, 0], ln_b[i, 0])
        if i < N_A:
            mix = fox_mixer(x, fox_w_in[i], fox_b_f[i], fox_w_o[i])
        else:
            j = i - N_A
            mix = mla_mixer(x, mla_w_dq[j], mla_q_norm[j], mla_w_uq[j], mla_w_o[j],
                            k_nope, k_rope, v_shared, cos, sin)
        x = post_norm(x, mix, ln_g[i, 1], ln_b[i, 1])
        x = post_norm(x, 0.5 * swiglu(x, ffn2_w_in[i], ffn2_w_out[i]), ln_g[i, 2], ln_b[i, 2])
        gate = jax.nn.sigmoid((x @ ple_w_gate[i] + ple_b_gate[i]).astype(jnp.float32)).astype(x.dtype)
        x = post_norm(x, gate * (p[i] @ ple_w_proj[i]), ln_g[i, 3], ln_b[i, 3])
    return x


def setup_inputs(seed=0):
    out = dict(first_inputs(seed))
    for name, value in second_inputs(seed + 1).items():
        if name != "x":
            out[name + "_2"] = value
    return out


def reference(
    x, c, ada_w, ada_b, w_in, conv_w, gk_w2, gk_b, gla_norm_w, w_out, ln1_g, ln1_b, ln2_g,
    ln2_b, ffn_w_gate, ffn_w_up, ffn_w_down, router_w, moe_w_gate, moe_w_up, moe_w_down, p_2,
    ffn1_w_in_2, ffn1_w_out_2, ffn2_w_in_2, ffn2_w_out_2, ln_g_2, ln_b_2, ple_w_gate_2,
    ple_b_gate_2, ple_w_proj_2, fox_w_in_2, fox_b_f_2, fox_w_o_2, mla_w_dq_2, mla_q_norm_2,
    mla_w_uq_2, mla_w_o_2, kv_w_down_2, kv_norm_2, kv_w_up_2,
):
    x = first_block(
        x, c, ada_w, ada_b, w_in, conv_w, gk_w2, gk_b, gla_norm_w, w_out, ln1_g, ln1_b, ln2_g,
        ln2_b, ffn_w_gate, ffn_w_up, ffn_w_down, router_w, moe_w_gate, moe_w_up, moe_w_down,
    )
    return second_block(
        x, p_2, ffn1_w_in_2, ffn1_w_out_2, ffn2_w_in_2, ffn2_w_out_2, ln_g_2, ln_b_2,
        ple_w_gate_2, ple_b_gate_2, ple_w_proj_2, fox_w_in_2, fox_b_f_2, fox_w_o_2, mla_w_dq_2,
        mla_q_norm_2, mla_w_uq_2, mla_w_o_2, kv_w_down_2, kv_norm_2, kv_w_up_2,
    )


_drawn_inputs = setup_inputs


def setup_inputs(seed=0):
    import zlib

    import numpy as np

    out = dict(_drawn_inputs(seed))
    spreads = {}
    factors = {'gk_b': 8.0,
     'gla_norm_w': 5.828,
     'ple_b_gate_2': 8.0,
     'fox_b_f_2': 44.576,
     'mla_q_norm_2': 8.0,
     'kv_norm_2': 8.0}
    for name, (base, spread) in spreads.items():
        noise = np.random.default_rng([zlib.crc32(name.encode()), seed]).standard_normal(out[name].shape)
        drawn = base * np.exp(spread * noise) if base else spread * noise
        out[name] = __import__('jax').numpy.asarray(drawn.astype(out[name].dtype))
    for name, factor in factors.items():
        out[name] = (out[name] * factor).astype(out[name].dtype)
    return out
```

```python
from contextlib import ExitStack

import numpy as np

import concourse.bass as bass
from concourse import mybir

F32 = mybir.dt.float32
U32 = mybir.dt.uint32
ALU = mybir.AluOpType
ACT = mybir.ActivationFunctionType
AX = mybir.AxisListType

P = 128
S = 256
T = S // P
D = 1024
KD = D // P
DEPTH = 2
CONV = 512
WIDTH = 3
HEADS = 4
DK = 64
DV = 128
CHUNK = 64
KW = HEADS * DK
VW = HEADS * DV
RANK = 16
C_B, C_C, C_H = 0, CONV, 2 * CONV
C_Q = 3 * CONV
C_K = C_Q + KW
C_V = C_K + KW
C_G = C_V + VW
C_LOW = C_G + VW
FF = 2816
FU = 256
NU = FF // FU
EXPERTS = 8
ALPHA = (2.0 * DEPTH) ** 0.25
LN_EPS = 1e-5
RMS_EPS = 1e-6
FOX_H = 16
FOX_D = 64
MLA_H = 16
NOPE = 128
ROPE = 64
VH = 128
QLORA = 384
KVLORA = 256
THETA = 10000.0
MASKED = -1e30

RW = 4
RD = 2
WSLOT = 4096
DSLOT = 2048
NEED_WIDE = 32

CONST_COLS = {}
_col = 0
for _name, _w in (("ident", P), ("shift1", P), ("shift2", P), ("cross1", P), ("cross2", P), ("cum", P),
                  ("suffix", P), ("tri", P), ("ones", P), ("causal", P), ("chunks", 2), ("experts", EXPERTS),
                  ("cos", T * ROPE // 2), ("sin", T * ROPE // 2), ("minushalf", T * HEADS)):
    CONST_COLS[_name] = (_col, _col + _w)
    _col += _w
NCONST = _col


def constants():
    c = np.zeros((P, NCONST), np.float32)
    j, i = np.meshgrid(np.arange(P), np.arange(P), indexing="ij")
    same = j // CHUNK == i // CHUNK

    def put(name, value):
        a, b = CONST_COLS[name]
        c[:, a:b] = value

    put("ident", j == i)
    put("shift1", j == i - 1)
    put("shift2", j == i - 2)
    put("cross1", j == i - 1 + P)
    put("cross2", j == i - 2 + P)
    put("cum", same & (j <= i))
    put("suffix", same & (j > i))
    put("tri", j <= i)
    put("ones", 1.0)
    put("causal", np.where(i <= j, 0.0, MASKED))
    put("chunks", np.arange(P)[:, None] // CHUNK == np.arange(2)[None, :])
    put("experts", np.arange(EXPERTS)[None, :])
    half = ROPE // 2
    inv = np.float32(THETA) ** (-np.arange(half, dtype=np.float32) * np.float32(2.0 / ROPE))
    ang = np.arange(S, dtype=np.float32)[:, None] * inv[None, :].astype(np.float32)
    put("cos", np.cos(ang).reshape(T, P, half).transpose(1, 0, 2).reshape(P, T * half))
    put("sin", np.sin(ang).reshape(T, P, half).transpose(1, 0, 2).reshape(P, T * half))
    put("minushalf", -0.5)
    return c


class Tally:
    DELTA = {
        "start": dict(act=1, dve=1),
        "ada": dict(g=12, w=12),
        "mod": dict(src=1),
        "tr8": dict(tg=4),
        "tr16": dict(tg=8),
        "gla": dict(g=22, tg=4, w=7, act=8, dve=6, pool=2, acc=1, free=1, src=1),
        "out1": dict(w=2, acc=2),
        "out2": dict(w=4, acc=4),
        "ln": dict(dve=2, pool=2, free=1, src=1, ln=1),
        "ffn": dict(g=2 * NU, tg=NU, w=NU, d=NU, act=2 * NU),
        "moe": dict(g=2 * NU * EXPERTS, tg=NU * EXPERTS, w=NU * EXPERTS, d=NU * EXPERTS, act=2 * NU * EXPERTS),
        "router": dict(g=2, act=1, dve=1),
        "kvdown": dict(g=2, tg=2, w=1, act=2, dve=3, pool=2),
        "fox": dict(g=24 + 32, tg=1 + 32, w=7, act=2 + 32, dve=2, acc=1, free=1, src=1),
        "mla": dict(g=2 + 24 + 24 + 32, tg=2 + 4 + 32, w=7, act=2 + 32, dve=3, pool=2, acc=2, free=2, src=1),
        "ple": dict(g=4, tg=1, w=3, act=2, acc=1),
    }
    FIELDS = ("g", "tg", "w", "d", "act", "dve", "pool", "acc", "free", "src", "ln")

    def __init__(self):
        self.g = self.tg = self.w = self.d = self.act = self.dve = 0
        self.pool = self.acc = self.free = self.src = self.ln = 0

    def after(self, kind):
        new = Tally()
        e = dict(self.DELTA[kind])
        new.g, new.tg = self.g + e.pop("g", 0), self.tg + e.pop("tg", 0)
        new.w, new.d = self.w + e.pop("w", 0), self.d + e.pop("d", 0)
        new.act, new.dve = self.act + e.pop("act", 0), self.dve + e.pop("dve", 0)
        new.pool, new.acc = self.pool + e.pop("pool", 0), self.acc + e.pop("acc", 0)
        new.free, new.src = self.free + e.pop("free", 0), self.src + e.pop("src", 0)
        new.ln = self.ln + e.pop("ln", 0)
        return new


def stages():
    plan = [("start", 0)]
    for l in range(DEPTH):
        plan += [("ada", l), ("mod", 0), ("tr8", "src"), ("gla", l), ("tr8", "src"), ("out1", ("w_out", l)),
                 ("ln", ("mod", 2)), ("mod", 3), ("tr8", "src")]
        plan += [("ffn", "dense")] if l % 2 == 0 else [("router", 0), ("moe", 0)]
        plan += [("ln", ("mod", 5))]
    for i in range(DEPTH):
        plan += [("tr8", "x")]
        if i:
            plan += [("kvdown", 0)]
        plan += [("ffn", ("ffn1", i)), ("ln", ("half", 0)), ("tr8", "x")]
        plan += [("mla", 0), ("tr16", "src"), ("out2", ("mla", 0))] if i else \
                [("fox", 0), ("tr8", "src"), ("out1", ("fox", 0))]
        plan += [("ln", ("plain", 0)), ("tr8", "x"), ("ffn", ("ffn2", i)), ("ln", ("half", 0)),
                 ("tr8", "x"), ("ple", i), ("ln", ("gate", 0))]
    return plan


def build(nc, I, out):
    plan = stages()
    tallies = [Tally()]
    for kind, _ in plan:
        tallies.append(tallies[-1].after(kind))
    steps = [(kind, arg, t, plan[max(i - 1, 0)][0]) for i, ((kind, arg), t) in enumerate(zip(plan, tallies))]

    with ExitStack() as ctx:
        def sb(name, cols, dt=F32, rows=P):
            return ctx.enter_context(nc.sbuf_tensor(name, [rows, cols], dt))

        def sem(name):
            return ctx.enter_context(nc.semaphore(name))

        G = ctx.enter_context(nc.psum_tensor("G", [P, 2, 512], F32))
        TB = ctx.enter_context(nc.psum_tensor("TB", [P, 2, 512], F32))
        A = ctx.enter_context(nc.psum_tensor("A", [P, 4, 512], F32))

        wide = [sb(f"wide{i}", WSLOT) for i in range(RW)]
        down = [sb(f"down{i}", DSLOT) for i in range(RD)]
        xs = sb("x_tok", T * D)
        x = xs[:, :].rearrange("p (t c) -> p t c", t=T)
        lnp = sb("ln_params", 2 * D)
        con = sb("con", NCONST)
        sg = sb("silu_gate", T * FU)
        hbuf = sb("hidden", 2 * T * FU)
        hT = sb("hidden_T", 2 * 2 * S)
        small = sb("small", 256)
        idx8 = sb("expert_idx", T * 8, U32)
        routw = sb("router_w", KD * EXPERTS)
        BIG = 2 * 4096
        arena = sb("arena", BIG + 15360)

        def C(name):
            a, b = CONST_COLS[name]
            return con[:, a:b]

        ident, ones = C("ident"), C("ones")

        def area(at, *shape):
            size = 1
            for s in shape:
                size *= s
            v = arena[:, at:at + size]
            if len(shape) == 2:
                v = v.rearrange("p (a b) -> p a b", a=shape[0])
            if len(shape) == 3:
                v = v.rearrange("p (a b c) -> p a b c", a=shape[0], b=shape[1])
            return v

        uT = area(0, 16, S)
        src = area(4096, T, D)
        src2 = area(4096, T, 2 * D)
        z1 = area(2048, T, CONV)
        gqT = area(2048, 2, S)
        gkT = area(2560, 2, S)
        stm = area(3072, 2, 2 * T, P)
        e3 = area(6144, T, 3 * KW)
        lsg = area(6144, T, KW)
        state = area(6144, 3, 2, 2 * DV)
        gk = area(7680, T, KW)
        mod = area(BIG, 6, D)
        proj = area(BIG + 6144, T, 3088)
        convw = area(BIG + 12320, WIDTH, CONV)
        gnw = area(BIG + 13856, DV)
        glowT = area(BIG + 13984, S)
        gkw2 = area(BIG + 14240, KW)
        gkb = area(BIG + 14496, KW)
        cqT = area(2048, 3, S)
        ckvT = area(2816, 2, S)
        krT = area(3328, S)
        qnT = area(BIG, MLA_H, S)
        knT = area(BIG + 4096, MLA_H, S)
        vtok = area(BIG + 8192, T, 2 * D)
        qrT = area(BIG + 12288, MLA_H // 2, S)
        cq = area(BIG, T, QLORA)
        ckv = area(BIG, T, KVLORA)
        krd = area(BIG + 512, T, 2 * ROPE)
        qr_raw = area(4096, T, MLA_H, ROPE)
        qr_rot = area(6144, T, MLA_H, ROPE)
        ropetmp = area(BIG + 4096, MLA_H, ROPE // 2)
        fqT = area(BIG, KD, S)
        fkT = area(BIG + 2048, KD, S)
        fv = area(BIG + 4096, T, D)
        ncT = area(BIG + 14336, S)
        cumf = area(BIG + 14592, T, FOX_H)
        fls = area(BIG + 14624, T, FOX_H)
        flt = area(BIG + 14656, T, FOX_H)
        qnw = area(BIG + 14688, QLORA)
        kvnw = area(BIG + 15072, KVLORA)
        bfrow = area(BIG + 15328, FOX_H)
        gt = area(BIG, T, D)
        bgate = area(BIG + 2048, D)
        ptok = area(BIG + 3072, T, S)
        pT = area(BIG + 3584, 2, S)
        scores = hbuf[:, 0:2 * S].rearrange("p (b s) -> p b s", b=2)
        probs = hbuf[:, 2 * S:4 * S].rearrange("p (b s) -> p b s", b=2)
        pbT = hT[:, 0:4 * P].rearrange("p (b s q) -> p b s q", b=2, s=2)
        hid = hbuf[:, :].rearrange("p (b t f) -> p b t f", b=2, t=T)
        hidT = hT[:, :].rearrange("p (b f s) -> p b f s", b=2, f=2)
        sgt = sg[:, :].rearrange("p (t f) -> p t f", t=T)

        stats = small[:, 0:24].rearrange("p (t c s) -> p t c s", t=T, c=2)
        mv = small[:, 24:28].rearrange("p (t c) -> p t c", t=T)
        ve = small[:, 28:36].rearrange("p (t h) -> p t h", t=T)
        rstd = small[:, 36:44].rearrange("p (t h) -> p t h", t=T)
        ssq = small[:, 44:52].rearrange("p (t h) -> p t h", t=T)
        dec = small[:, 52:60].rearrange("p (t a c) -> p t a c", t=T, a=2)
        condT = small[:, 60:68]
        cT = small[:, 68:76]
        nmax = small[:, 76:78]
        rsum = small[:, 80:112].rearrange("p (t h) -> p t h", t=T)
        rinv = small[:, 112:144].rearrange("p (t h) -> p t h", t=T)
        logit = small[:, 144:160].rearrange("p (t e) -> p t e", t=T)
        top8 = small[:, 160:176].rearrange("p (t e) -> p t e", t=T)
        gap = small[:, 176:178]
        e2 = small[:, 178:180]
        w1 = small[:, 180:182]
        w2 = small[:, 182:184]
        idxf = small[:, 184:200].rearrange("p (t e) -> p t e", t=T)
        route = small[:, 200:216].rearrange("p (t e) -> p t e", t=T)
        rtmp = small[:, 216:232].rearrange("p (t e) -> p t e", t=T)
        condB = area(4096, KD, P)

        g_done = sem("g_done")
        g_read = sem("g_read")
        t_done = sem("t_done")
        t_evac = sem("t_evac")
        acc_done = sem("acc_done")
        acc_free = sem("acc_free")
        down_used = sem("down_used")
        act_ready = sem("act_ready")
        dve_ready = sem("dve_ready")
        pool_ready = sem("pool_ready")
        src_ready = sem("src_ready")
        dve_step = sem("dve_step")
        act_step = sem("act_step")
        wide_full = [sem(f"wide_full{i}") for i in range(RW)]
        down_full = [sem(f"down_full{i}") for i in range(RD)]
        s_con = sem("con_loaded")
        s_x = sem("x_loaded")
        s_c = sem("c_loaded")
        s_rout = sem("router_loaded")
        s_ada = sem("ada_bias_loaded")
        s_gla = sem("gla_params_loaded")
        s_ln = sem("ln_params_loaded")
        s_attn = sem("attn_params_loaded")
        s_ple = sem("ple_params_loaded")
        s_out = sem("out_stored")

        cond_again = sem("cond_again")

        def ring_count(base, n, depth, need):
            return base * (need // depth) + need * (n // depth + 1)

        def flat(ap):
            return {2: lambda a: a, 3: lambda a: a.rearrange("p a b -> p (a b)")}[len(ap.shape)](ap)

        def swiglu(arg):
            if arg == "dense":
                return I["ffn_w_gate"][0], I["ffn_w_up"][0], I["ffn_w_down"][0]
            name, i = arg
            w = I[f"{name}_w_in_2"][i]
            return w[:, 0:FF], w[:, FF:2 * FF], I[f"{name}_w_out_2"][i]

        block = ctx.enter_context(nc.Block())

        @block.sync
        def _(sp):
            released = []
            state_w = {"w": 0}

            def wait_slot():
                w = state_w["w"]
                if w >= RW:
                    s, v = released[w - RW]
                    sp.wait_ge(s, v)

            def fill(view_k, kt, cols, freed_by):
                wait_slot()
                w = state_w["w"]
                dst = wide[w % RW][:, 0:kt * cols].rearrange("p (k c) -> p k c", k=kt)
                cut = (kt + 1) // 2
                for a, b in ((0, cut), (cut, kt)):
                    sp.dma_start(dst[:, a:b], view_k[:, a:b]).then_inc(wide_full[w % RW], 16)
                released.append(freed_by)
                state_w["w"] = w + 1

            def kview(w_ap):
                return w_ap.rearrange("(k p) c -> p k c", p=P)

            def unit(slot, dslot, gate, up, dn, at):
                gv = wide[slot][:, :].rearrange("p (k h f) -> p k h f", k=KD, h=2)
                sp.dma_start(gv[:, :, 0], kview(gate)[:, :, bass.ds(at, FU)]).then_inc(wide_full[slot], 16)
                sp.dma_start(gv[:, :, 1], kview(up)[:, :, bass.ds(at, FU)]).then_inc(wide_full[slot], 16)
                return (down[dslot][:, :].rearrange("p (f c) -> p f c", f=2),
                        dn[bass.ds(at, FU), :].rearrange("(f p) c -> p f c", p=P))

            sp.dma_start(con[:, :], I["con"]).then_inc(s_con, 16)
            for kind, arg, n, _ in steps:
                if kind == "ada":
                    v = kview(I["ada_w"][arg])
                    for c in range(12):
                        fill(v[:, :, c * 512:(c + 1) * 512], KD, 512, (g_done, n.g + c + 1))
                elif kind == "gla":
                    v = kview(I["w_in"][arg])
                    for c in range(6):
                        fill(v[:, :, c * 512:(c + 1) * 512], KD, 512, (g_done, n.g + 2 * c + 2))
                    fill(v[:, :, C_LOW:C_LOW + RANK], KD, RANK, (t_done, n.tg + 1))
                elif kind in ("out1", "out2"):
                    name, i = arg
                    w_ap = {"w_out": I["w_out"], "fox": I["fox_w_o_2"], "mla": I["mla_w_o_2"]}[name][i]
                    v, kt = kview(w_ap), (KD if kind == "out1" else 2 * KD)
                    cols = WSLOT // kt
                    for c in range(D // cols):
                        fill(v[:, :, c * cols:(c + 1) * cols], kt, cols, (acc_done, n.acc + c + 1))
                elif kind == "ffn":
                    gate, up, dn = swiglu(arg)

                    def ffn_unit(j, c):
                        dst, dsrc = unit((n.w + j) % RW, (n.d + j) % RD, gate, up, dn, c * FU)
                        sp.wait_ge(down_used, n.d - RD + 1 + c) if n.d or j >= RD else None
                        sp.dma_start(dst, dsrc).then_inc(down_full[(n.d + j) % RD], 16)

                    peel = NU % RW
                    for c in range(peel):
                        wait_slot()
                        ffn_unit(c, c)
                        released.append((g_done, n.g + 2 * c + 2))
                        state_w["w"] += 1
                    wait_slot()
                    with sp.Fori(0, NU // RW) as i:
                        for j in range(RW):
                            sp.wait_ge(g_done, i * (2 * RW) + (n.g + 2 * (peel + j - RW + 1)))
                            ffn_unit(peel + j, i * RW + (peel + j))
                    for c in range(peel, NU):
                        released.append((g_done, n.g + 2 * c + 2))
                    state_w["w"] += NU - peel
                elif kind == "moe":
                    gates, ups, dns = I["moe_w_gate"][0], I["moe_w_up"][0], I["moe_w_down"][0]

                    def moe_unit(e, at, u):
                        dst, dsrc = unit((n.w + e) % RW, (n.d + e) % RD, gates[e], ups[e], dns[e], at)
                        sp.wait_ge(down_used, u + (n.d - RD + 1))
                        sp.dma_start(dst, dsrc).then_inc(down_full[(n.d + e) % RD], 16)

                    for e in range(EXPERTS):
                        wait_slot()
                        moe_unit(e, 0, e)
                        released.append((g_done, n.g + 2 * e + 2))
                        state_w["w"] += 1
                    with sp.Fori(1, NU) as i:
                        for e in range(EXPERTS):
                            sp.wait_ge(g_done, i * (2 * EXPERTS) + (n.g + 2 * (e - RW + 1)))
                            moe_unit(e, i * FU, i * EXPERTS + e)
                    for u in range(EXPERTS, NU * EXPERTS):
                        released.append((g_done, n.g + 2 * u + 2))
                    state_w["w"] += (NU - 1) * EXPERTS
                elif kind == "kvdown":
                    fill(kview(I["kv_w_down_2"]), KD, KVLORA + ROPE, (g_done, n.g + 2))
                elif kind == "fox":
                    v = kview(I["fox_w_in_2"][0])
                    for c in range(6):
                        last = n.g + (4 * c + 4 if c < 4 else 16 + 2 * (c - 4) + 2)
                        fill(v[:, :, c * 512:(c + 1) * 512], KD, 512, (g_done, last))
                    fill(v[:, :, 3 * D:3 * D + FOX_H], KD, FOX_H, (g_done, n.g + 22))
                elif kind == "mla":
                    fill(kview(I["mla_w_dq_2"][0]), KD, QLORA, (g_done, n.g + 2))
                    v = I["mla_w_uq_2"][0].rearrange("(k p) h d -> p k (h d)", p=P)
                    cols = 4 * (NOPE + ROPE)
                    for c in range(4):
                        fill(v[:, :, c * cols:(c + 1) * cols], 3, cols, (g_done, n.g + 2 + 6 * c + 6))
                    v = I["kv_w_up_2"].rearrange("(k p) h d -> p k (h d)", p=P)
                    for c in range(2):
                        fill(v[:, :, c * 2048:(c + 1) * 2048], 2, 2048, (g_done, n.g + 26 + 12 * c + 12))
                elif kind == "ple":
                    v = kview(I["ple_w_gate_2"][arg])
                    for c in range(2):
                        fill(v[:, :, c * 512:(c + 1) * 512], KD, 512, (g_done, n.g + 2 * c + 2))
                    fill(kview(I["ple_w_proj_2"][arg]), 2, D, (acc_done, n.acc + 1))
            sp.wait_ge(src_ready, tallies[-1].src)
            sp.dma_start(out[0].rearrange("(t p) c -> p t c", p=P), x).then_inc(s_out, 16)
            sp.wait_ge(s_out, 16)

        @block.tensor
        def _(pe):
            def open_g(g):
                if not isinstance(g, int) or g >= 2:
                    pe.wait_ge(g_read, g - 1)

            def open_t(tg):
                if not isinstance(tg, int) or tg >= 2:
                    pe.wait_ge(t_evac, tg - 1)

            def wide_ready(w):
                pe.wait_ge(wide_full[w % RW], NEED_WIDE * (w // RW + 1))

            def slot(w, kt, cols):
                return wide[w % RW][:, 0:kt * cols].rearrange("p (k c) -> p k c", k=kt)

            def mm(o, lhsT, rhs, start, stop):
                return nc.tensor.matmul(o, lhsT, rhs, start=start, stop=stop, skip_group_check=True)

            def tok(t):
                return slice(t * P, (t + 1) * P)

            def project(g, t, aT, kt, rhs_of, cols):
                open_g(g)
                for k in range(kt):
                    last = mm(G[:, g % 2, 0:cols], aT[:, k, tok(t)], rhs_of(k), k == 0, k == kt - 1)
                return last.then_inc(g_done, 1)

            def project_T(g, lhs_of, aT, kt):
                open_g(g)
                for k in range(kt):
                    last = mm(G[:, g % 2, 0:S], lhs_of(k), aT[:, k, :], k == 0, k == kt - 1)
                return last.then_inc(g_done, 1)

            def transposes(tg, blocks):
                open_t(tg)
                for b, block_in in enumerate(blocks):
                    last = nc.tensor.transpose(TB[:, tg % 2, b * P:(b + 1) * P], block_in, ident)
                return last.then_inc(t_done, 1)

            def attention(n, g0, tg0, act0, heads, rows, scores_of, vcols, free0):
                todo = [(t, h) for t in range(T) for h in range(heads)]
                per_t = len(todo) // T
                for i in range(len(todo) + 2):
                    if i < len(todo):
                        t, h = todo[i]
                        open_g(g0 + i)
                        scores_of(G[:, (g0 + i) % 2, 0:P * (t + 1)], t, h).then_inc(g_done, 1)
                    if 1 <= i <= len(todo):
                        t, h = todo[i - 1]
                        pe.wait_ge(act_ready, act0 + i)
                        transposes(tg0 + i - 1, [probs[:, (i - 1) % 2, tok(b)] for b in range(t + 1)])
                    if i >= 2:
                        t, h = todo[i - 2]
                        pe.wait_ge(t_evac, tg0 + i - 1)
                        if i == 2:
                            pe.wait_ge(acc_free, free0)
                        if vcols == VH and t and h == 0:
                            pe.wait_ge(acc_free, free0 + 1)
                        if vcols == VH:
                            o = A[:, h // 4, (h % 4) * VH:(h % 4 + 1) * VH]
                            v = vtok
                        else:
                            o = A[:, 2 * t + h // 8, (h % 8) * FOX_D:(h % 8 + 1) * FOX_D]
                            v = fv
                        for b in range(t + 1):
                            last = mm(o, pbT[:, i % 2, b, :], v[:, b, h * vcols:(h + 1) * vcols], b == 0, b == t)
                        if (i - 2) % per_t == per_t - 1 and (vcols == VH or t == T - 1):
                            last.then_inc(acc_done, 1)

            def up_half(g, w, t, sl):
                open_g(g)
                wv = wide[sl][:, :].rearrange("p (k c) -> p k c", k=KD)
                for k in range(KD):
                    last = mm(G[:, t, :], uT[:, k, tok(t)], wv[:, k, :], k == 0, k == KD - 1)
                last.then_inc(g_done, 1)

            def turn_hidden(tg, par, g_after):
                pe.wait_ge(g_read, g_after)
                open_t(tg)
                for f in range(2):
                    for t in range(T):
                        last = nc.tensor.transpose(TB[:, par, f * S + t * P:f * S + (t + 1) * P],
                                                   hid[:, par, t, tok(f)], ident)
                last.then_inc(t_done, 1)

            def down_half(tg, par, dsl, full, first, final):
                pe.wait_ge(t_evac, tg + 1)
                pe.wait_ge(down_full[dsl], full)
                dv = down[dsl][:, :].rearrange("p (f c) -> p f c", f=2)
                for t in range(T):
                    for f in range(2):
                        for half in range(2):
                            last = mm(A[:, 2 * t + half, :], hidT[:, par, f, tok(t)],
                                      dv[:, f, half * 512:(half + 1) * 512], first and f == 0, final and f == 1)
                last.then_inc(down_used, 1)

            def ffn(n, total, body, peel):
                def up_and_down(j, c, first):
                    wr = n.w + j
                    base = (c - j)
                    pe.wait_ge(wide_full[wr % RW], ring_count(base, wr, RW, NEED_WIDE))
                    up_half(c * 2 + n.g, wr, 0, wr % RW)
                    if not first:
                        turn_hidden(c + (n.tg - 1), (n.tg + j - 1) % 2, c * 2 + n.g)
                    up_half(c * 2 + (n.g + 1), wr, 1, wr % RW)
                    if not first:
                        down_at(j - 1, c - 1, isinstance(c, int) and c == 1, False)

                def down_at(j, c, opening, final):
                    d = n.d + j
                    down_half(c + n.tg, (n.tg + j) % 2, d % RD, ring_count(c - j, d, RD, 16), opening, final)

                assert n.g % 2 == 0
                for c in range(peel):
                    if c == 1:
                        pe.wait_ge(acc_free, n.free)
                    up_and_down(c, c, c == 0)
                with pe.Fori(0, (total - peel) // body) as i:
                    for j in range(body):
                        up_and_down(peel + j, i * body + (peel + j), False)
                turn_hidden(n.tg + total - 1, (n.tg + total - 1) % 2, n.g + 2 * total)
                down_at(total - 1, total - 1, False, True)

            pe.wait_ge(s_con, 16)
            for kind, arg, n, before in steps:
                if kind == "ada":
                    if arg == 0:
                        pe.wait_ge(dve_ready, 1)
                    else:
                        pe.wait_ge(cond_again, 1)
                    for c in range(12):
                        g = n.g + c
                        wide_ready(n.w + c)
                        open_g(g)
                        wv = slot(n.w + c, KD, 512)
                        for k in range(KD):
                            last = mm(G[:, g % 2, :], condB[:, k, :], wv[:, k, :], k == 0, k == KD - 1)
                        last.then_inc(g_done, 1)
                elif kind in ("tr8", "tr16"):
                    pe.wait_ge(src_ready, n.src)
                    kt = int(kind[2:])
                    view = x if arg == "x" else (src if kt == 8 else src2)
                    for j in range(kt // 2):
                        transposes(n.tg + j, [view[:, t, tok(2 * j + k)] for k in range(2) for t in range(T)])
                elif kind == "gla":
                    pe.wait_ge(t_evac, n.tg)
                    for c in range(6):
                        wide_ready(n.w + c)
                        wv = slot(n.w + c, KD, 512)
                        for t in range(T):
                            project(n.g + 2 * c + t, t, uT, KD, lambda k: wv[:, k, :], 512)
                    wide_ready(n.w + 6)
                    wv6 = slot(n.w + 6, KD, RANK)
                    open_t(n.tg)
                    for k in range(KD):
                        last = mm(TB[0:RANK, n.tg % 2, 0:S], wv6[:, k, :], uT[:, k, :], k == 0, k == KD - 1)
                    last.then_inc(t_done, 1)
                    pe.wait_ge(s_gla, 64 * (arg + 1))
                    pe.wait_ge(t_evac, n.tg + 1)
                    for t in range(T):
                        g = n.g + 12 + t
                        open_g(g)
                        mm(G[:, g % 2, 0:KW], ones[0:1, :], gkb[0:1, :], True, False)
                        mm(G[:, g % 2, 0:KW], glowT[0:RANK, tok(t)], gkw2[0:RANK, :], False, True) \
                            .then_inc(g_done, 1)
                    pe.wait_ge(dve_ready, n.dve + 1)
                    for t in range(T):
                        g = n.g + 14 + t
                        open_g(g)
                        o = G[:, g % 2, :]
                        mm(o, ident, proj[:, t, C_C:C_C + CONV], True, False)
                        mm(o, C("shift1"), z1[:, t, :], False, False)
                        if t:
                            mm(o, C("cross1"), z1[:, t - 1, :], False, False)
                            mm(o, C("cross2"), proj[:, t - 1, C_H:C_H + CONV], False, False)
                        mm(o, C("shift2"), proj[:, t, C_H:C_H + CONV], False, True).then_inc(g_done, 1)
                    for t in range(T):
                        g = n.g + 16 + t
                        pe.wait_ge(dve_ready, n.dve + 2 + t)
                        open_g(g)
                        mm(G[:, g % 2, 0:KW], C("cum"), gk[:, t, :], True, True)
                        mm(G[:, g % 2, KW:2 * KW], C("suffix"), gk[:, t, :], True, True).then_inc(g_done, 1)
                    open_t(n.tg + 1)
                    for t in range(T):
                        for a in range(2):
                            last = mm(TB[:, (n.tg + 1) % 2, t * 4 + a * 2:t * 4 + a * 2 + 2],
                                      gk[:, t, tok(a)], C("chunks"), True, True)
                    last.then_inc(t_done, 1)
                    pe.wait_ge(g_read, n.g + 18)
                    transposes(n.tg + 2, [proj[:, t, C_Q + a * P:C_Q + (a + 1) * P] for a in range(2)
                                          for t in range(T)])
                    transposes(n.tg + 3, [proj[:, t, C_C + a * P:C_C + (a + 1) * P] for a in range(2)
                                          for t in range(T)])
                    pe.wait_ge(acc_free, n.free) if n.free else None
                    for c in range(3):
                        t, r = c // 2, slice(CHUNK * (c % 2), CHUNK * (c % 2) + CHUNK)
                        for a in range(2):
                            last = mm(A[:, c, a * KW:(a + 1) * KW], proj[r, t, C_K + a * P:C_K + (a + 1) * P],
                                      proj[r, t, C_V + a * KW:C_V + (a + 1) * KW], True, True)
                    last.then_inc(acc_done, 1)
                    pe.wait_ge(t_evac, n.tg + 4)
                    for f in range(2):
                        g = n.g + 18 + f
                        r = slice(DK * f, DK * f + DK)
                        open_g(g)
                        for j in range(2 * T):
                            a, t = divmod(j, T)
                            last = mm(G[:, g % 2, tok(j)], gkT[r, a, tok(t)], gqT[r, a, tok(t)], True, True)
                        last.then_inc(g_done, 1)
                    pe.wait_ge(g_read, n.g + 20)
                    pe.wait_ge(dve_ready, n.dve + 4)
                    for t in range(T):
                        g = n.g + 20 + t
                        open_g(g)
                        for h in range(HEADS):
                            mm(G[:, g % 2, tok(h)], stm[:, h % 2, T * (h // 2) + t, :],
                               proj[:, t, C_V + h * DV:C_V + (h + 1) * DV], h == 0, False)
                        for f in range(2):
                            c = 2 * t + f
                            if c:
                                q = slice(CHUNK * f, CHUNK * f + CHUNK)
                                for a in range(2):
                                    last = mm(G[q, g % 2, a * KW:(a + 1) * KW],
                                              gqT[:, a, t * P + CHUNK * f:t * P + CHUNK * f + CHUNK],
                                              state[:, c - 1, a, :], False, True)
                        last.then_inc(g_done, 1)
                elif kind in ("out1", "out2"):
                    pe.wait_ge(t_evac, n.tg)
                    pe.wait_ge(acc_free, n.free)
                    kt = KD if kind == "out1" else 2 * KD
                    cols = WSLOT // kt
                    for c in range(D // cols):
                        wide_ready(n.w + c)
                        wv = slot(n.w + c, kt, cols)
                        half, at = divmod(c * cols, 512)
                        for t in range(T):
                            for k in range(kt):
                                last = mm(A[:, 2 * t + half, at:at + cols], uT[:, k, tok(t)], wv[:, k, :],
                                          k == 0, k == kt - 1)
                        last.then_inc(acc_done, 1)
                elif kind == "ffn":
                    pe.wait_ge(t_evac, n.tg)
                    ffn(n, NU, RW, NU % RW)
                elif kind == "moe":
                    pe.wait_ge(t_evac, n.tg)
                    ffn(n, NU * EXPERTS, EXPERTS, EXPERTS)
                elif kind == "router":
                    pe.wait_ge(t_evac, n.tg)
                    pe.wait_ge(s_rout, 16)
                    rv = routw[:, :].rearrange("p (k e) -> p k e", k=KD)
                    for t in range(T):
                        project(n.g + t, t, uT, KD, lambda k: rv[:, k, :], EXPERTS)
                elif kind == "kvdown":
                    pe.wait_ge(t_evac, n.tg)
                    wide_ready(n.w)
                    wv = slot(n.w, KD, KVLORA + ROPE)
                    for t in range(T):
                        project(n.g + t, t, uT, KD, lambda k: wv[:, k, :], KVLORA + ROPE)
                    pe.wait_ge(dve_ready, n.dve + 3)
                    transposes(n.tg, [ckv[:, t, tok(k)] for k in range(2) for t in range(T)])
                    transposes(n.tg + 1, [krd[:, t, :] for t in range(T)])
                elif kind == "fox":
                    pe.wait_ge(t_evac, n.tg)
                    for c in range(4):
                        wide_ready(n.w + c)
                        wv = slot(n.w + c, KD, 512)
                        for f in range(4):
                            project_T(n.g + 4 * c + f, lambda k: wv[:, k, tok(f)], uT, KD)
                    for c in range(4, 6):
                        wide_ready(n.w + c)
                        wv = slot(n.w + c, KD, 512)
                        for t in range(T):
                            project(n.g + 16 + 2 * (c - 4) + t, t, uT, KD, lambda k: wv[:, k, :], 512)
                    wide_ready(n.w + 6)
                    pe.wait_ge(s_attn, 48)
                    wv6 = slot(n.w + 6, KD, FOX_H)
                    for t in range(T):
                        g = n.g + 20 + t
                        open_g(g)
                        mm(G[:, g % 2, 0:FOX_H], ones[0:1, :], bfrow[0:1, :], True, False)
                        for k in range(KD):
                            last = mm(G[:, g % 2, 0:FOX_H], uT[:, k, tok(t)], wv6[:, k, :], False, k == KD - 1)
                        last.then_inc(g_done, 1)
                    pe.wait_ge(dve_ready, n.dve + 2)
                    for t in range(T):
                        g = n.g + 22 + t
                        open_g(g)
                        last = mm(G[:, g % 2, 0:FOX_H], C("tri"), fls[:, t, :], True, t == 0)
                        if t:
                            last = mm(G[:, g % 2, 0:FOX_H], ones, fls[:, 0, :], False, True)
                        last.then_inc(g_done, 1)
                    open_t(n.tg)
                    for t in range(T):
                        o = TB[0:FOX_H, n.tg % 2, tok(t)]
                        last = mm(o, fls[:, t, :], C("tri"), True, t == 0)
                        if t:
                            last = mm(o, fls[:, 0, :], ones, False, True)
                    last.then_inc(t_done, 1)
                    pe.wait_ge(t_evac, n.tg + 1)
                    pe.wait_ge(g_read, n.g + 24)

                    def fox_scores(o, t, h):
                        r = slice(FOX_D * (h % 2), FOX_D * (h % 2) + FOX_D)
                        mm(o, fqT[r, h // 2, tok(t)], fkT[r, h // 2, 0:P * (t + 1)], True, False)
                        return mm(o, ident[0:FOX_H, h:h + 1].to_broadcast([FOX_H, P]), ncT[0:FOX_H, 0:P * (t + 1)],
                                  False, True)

                    attention(n, n.g + 24, n.tg + 1, n.act + 2, FOX_H, None, fox_scores, FOX_D, n.free)
                elif kind == "mla":
                    pe.wait_ge(t_evac, n.tg)
                    wide_ready(n.w)
                    wv = slot(n.w, KD, QLORA)
                    for t in range(T):
                        project(n.g + t, t, uT, KD, lambda k: wv[:, k, :], QLORA)
                    pe.wait_ge(g_read, n.g + 2)
                    transposes(n.tg, [cq[:, t, tok(k)] for k in range(2) for t in range(T)])
                    transposes(n.tg + 1, [cq[:, t, tok(2)] for t in range(T)])
                    pe.wait_ge(t_evac, n.tg + 2)
                    for c in range(4):
                        wide_ready(n.w + 1 + c)
                        wv = slot(n.w + 1 + c, 3, 4 * (NOPE + ROPE))
                        wr = wide[(n.w + 1 + c) % RW][:, 0:12 * (NOPE + ROPE)].rearrange(
                            "p (k h d) -> p k h d", k=3, h=4)
                        g = n.g + 2 + 6 * c
                        for h in range(4):
                            project_T(g + h, lambda k: wr[:, k, h, 0:NOPE], cqT, 3)
                        for t in range(T):
                            project(g + 4 + t, t, cqT, 3, lambda k: wr[:, k, :, NOPE:NOPE + ROPE], 4 * ROPE)
                    pe.wait_ge(dve_ready, n.dve + 3)
                    for j in range(4):
                        transposes(n.tg + 2 + j, [qr_rot[:, t, 4 * j + 2 * a:4 * j + 2 * a + 2, :].rearrange(
                            "p h d -> p (h d)") for a in range(2) for t in range(T)])
                    for c in range(2):
                        wide_ready(n.w + 5 + c)
                        wr2 = wide[(n.w + 5 + c) % RW][:, :].rearrange("p (k h d) -> p k h d", k=2, h=8)
                        g = n.g + 26 + 12 * c
                        for h in range(8):
                            project_T(g + h, lambda k: wr2[:, k, h, 0:NOPE], ckvT, 2)
                        for q in range(2):
                            for t in range(T):
                                project(g + 8 + 2 * q + t, t, ckvT, 2,
                                        lambda k: wr2[:, k, 4 * q:4 * q + 4, NOPE:NOPE + VH], 4 * VH)
                    pe.wait_ge(t_evac, n.tg + 6)
                    pe.wait_ge(g_read, n.g + 50)

                    def mla_scores(o, t, h):
                        r = slice(ROPE * (h % 2), ROPE * (h % 2) + ROPE)
                        mm(o, qnT[:, h, tok(t)], knT[:, h, 0:P * (t + 1)], True, False)
                        return mm(o, qrT[r, h // 2, tok(t)], krT[r, 0:P * (t + 1)], False, True)

                    attention(n, n.g + 50, n.tg + 6, n.act + 2, MLA_H, None, mla_scores, VH, n.free)
                elif kind == "ple":
                    pe.wait_ge(t_evac, n.tg)
                    for c in range(2):
                        wide_ready(n.w + c)
                        wv = slot(n.w + c, KD, 512)
                        for t in range(T):
                            project(n.g + 2 * c + t, t, uT, KD, lambda k: wv[:, k, :], 512)
                    pe.wait_ge(s_ple, 32 * (arg + 1))
                    transposes(n.tg, [ptok[:, t, tok(k)] for k in range(2) for t in range(T)])
                    pe.wait_ge(t_evac, n.tg + 1)
                    pe.wait_ge(acc_free, n.free)
                    wide_ready(n.w + 2)
                    wv = slot(n.w + 2, 2, D)
                    for t in range(T):
                        for half in range(2):
                            for k in range(2):
                                last = mm(A[:, 2 * t + half, :], pT[:, k, tok(t)],
                                          wv[:, k, half * 512:(half + 1) * 512], k == 0, k == 1)
                    last.then_inc(acc_done, 1)

        @block.scalar
        def _(act):
            act.dma_start(x, I["x"][0].rearrange("(t p) c -> p t c", p=P)).then_inc(s_x, 16)
            act.dma_start(cT, I["c"].rearrange("a (k p) -> p (a k)", p=P),
                          allow_slow_non_contiguous=True).then_inc(s_c, 16)
            step = [0]

            def link(ins):
                step[0] += 1
                ins.then_inc(act_step, 1)
                act.wait_ge(act_step, step[0])

            def evac(tg, dst, cols=4 * P, rows=P, func=ACT.Copy, scale=1.0):
                act.wait_ge(t_done, tg + 1)
                nc.scalar.activation(flat(dst), TB[0:rows, tg % 2, 0:cols], func, scale=scale).then_inc(t_evac, 1)

            def log_gate(g, dst, cols):
                act.wait_ge(g_done, g + 1)
                link(nc.scalar.activation(dst, G[:, g % 2, 0:cols], ACT.Abs))
                link(nc.scalar.activation(dst, dst, ACT.Exp, scale=-1.0))
                nc.scalar.activation(dst, dst, ACT.Ln, bias=1.0).then_inc(act_ready, 1)

            def sum_squares(g, t, h, cols, junk, signal):
                ins = nc.scalar.activation(junk, G[:, g % 2, h * cols:(h + 1) * cols], ACT.Square,
                                           accum_out=ssq[:, t, h:h + 1])
                if signal:
                    ins.then_inc(act_ready, 1)

            def attention(n, g0, tg0, act0):
                for i in range(33):
                    if i < 32:
                        t, h = divmod(i, 16)
                        act.wait_ge(g_read, g0 + i + 1)
                        nc.scalar.activation(probs[:, i % 2, 0:P * (t + 1)], scores[:, i % 2, 0:P * (t + 1)], ACT.Exp,
                                             bias=nmax[:, i % 2:i % 2 + 1], accum_out=rsum[:, t, h:h + 1]) \
                            .then_inc(act_ready, 1)
                    if i >= 1:
                        t = (i - 1) // 16
                        evac(tg0 + i - 1, pbT[:, (i - 1) % 2, 0:t + 1, :], P * (t + 1))

            def ffn(n, total, body, peel):
                def silu(c2, t):
                    act.wait_ge(g_done, c2 + (n.g + t + 1))
                    nc.scalar.activation(sgt[:, t, :], G[:, t, 0:FU], ACT.Silu).then_inc(act_ready, 1)

                def turn(c, par):
                    act.wait_ge(t_done, c + (n.tg + 1))
                    nc.scalar.activation(hidT[:, par].rearrange("p f s -> p (f s)"), TB[:, par, :], ACT.Copy) \
                        .then_inc(t_evac, 1)

                def unit(j, c, first):
                    silu(c * 2, 0)
                    if not first:
                        turn(c - 1, (n.tg + j - 1) % 2)
                    silu(c * 2, 1)

                for c in range(peel):
                    unit(c, c, c == 0)
                with act.Fori(0, (total - peel) // body) as i:
                    for j in range(body):
                        unit(peel + j, i * body + (peel + j), False)
                turn(total - 1, (n.tg + total - 1) % 2)

            for kind, arg, n, before in steps:
                if kind == "start":
                    act.wait_ge(s_c, 16)
                    nc.scalar.activation(condT, cT, ACT.Silu).then_inc(act_ready, 1)
                elif kind in ("tr8", "tr16"):
                    for j in range(int(kind[2:]) // 2):
                        evac(n.tg + j, uT[:, 2 * j:2 * j + 2, :])
                elif kind == "gla":
                    evac(n.tg, glowT[0:RANK, :], S, RANK)
                    for t in range(T):
                        log_gate(n.g + 12 + t, lsg[:, t, :], KW)
                    evac(n.tg + 1, small[:, 52:60], 8, P, ACT.Exp)
                    act.wait_ge(dve_ready, n.dve + 3)
                    for t in range(T):
                        g = n.g + 16 + t
                        act.wait_ge(g_done, g + 1)
                        nc.scalar.activation(e3[:, t, 0:2 * KW], G[:, g % 2, 0:2 * KW], ACT.Exp)
                        nc.scalar.activation(e3[:, t, 2 * KW:3 * KW], G[:, g % 2, 0:KW], ACT.Exp, scale=-1.0) \
                            .then_inc(act_ready, 1)
                    evac(n.tg + 2, gqT)
                    evac(n.tg + 3, gkT)
                    for t in range(T):
                        act.wait_ge(g_read, n.g + 16)
                        nc.scalar.activation(proj[:, t, C_H:C_H + VW], proj[:, t, C_G:C_G + VW], ACT.Silu) \
                            .then_inc(act_ready, 1)
                    for t in range(T):
                        g = n.g + 20 + t
                        act.wait_ge(g_done, g + 1)
                        for h in range(HEADS):
                            sum_squares(g, t, h, DV, hbuf[:, t * VW + h * DV:t * VW + (h + 1) * DV], h == HEADS - 1)
                elif kind == "ffn":
                    ffn(n, NU, RW, NU % RW)
                elif kind == "moe":
                    ffn(n, NU * EXPERTS, EXPERTS, EXPERTS)
                elif kind == "router":
                    act.wait_ge(dve_ready, n.dve + 1)
                    nc.scalar.activation(e2, gap, ACT.Exp).then_inc(act_ready, 1)
                elif kind == "kvdown":
                    for t in range(T):
                        act.wait_ge(g_done, n.g + t + 1)
                        sum_squares(n.g + t, t, 0, KVLORA, sg[:, t * KVLORA:(t + 1) * KVLORA], True)
                    evac(n.tg, ckvT)
                    evac(n.tg + 1, krT, S)
                elif kind == "fox":
                    for t in range(T):
                        log_gate(n.g + 20 + t, flt[:, t, :], FOX_H)
                    evac(n.tg, ncT[0:FOX_H, :], S, FOX_H, ACT.Copy, -1.0)
                    attention(n, n.g + 24, n.tg + 1, n.act + 2)
                elif kind == "mla":
                    for t in range(T):
                        act.wait_ge(g_done, n.g + t + 1)
                        sum_squares(n.g + t, t, 0, QLORA, hbuf[:, t * QLORA:(t + 1) * QLORA], True)
                    evac(n.tg, cqT[:, 0:2, :])
                    evac(n.tg + 1, cqT[:, 2, :], S)
                    for j in range(4):
                        evac(n.tg + 2 + j, qrT[:, 2 * j:2 * j + 2, :])
                    attention(n, n.g + 50, n.tg + 6, n.act + 2)
                elif kind == "ple":
                    evac(n.tg, pT)
                    for t in range(T):
                        act.wait_ge(g_read, n.g + 3 + t)
                        nc.scalar.activation(gt[:, t, :], gt[:, t, :], ACT.Sigmoid).then_inc(act_ready, 1)

        @block.gpsimd
        def _(pool):
            def bc(row):
                return row.partition_broadcast(P)

            def load_ln(s):
                if s < 2 * DEPTH:
                    name = ("ln1", "ln2")[s % 2]
                    rows = I[f"{name}_g"][s // 2], I[f"{name}_b"][s // 2]
                elif s < 6 * DEPTH:
                    i, j = divmod(s - 2 * DEPTH, 4)
                    rows = I["ln_g_2"][i, j], I["ln_b_2"][i, j]
                else:
                    return
                for half, row in enumerate(rows):
                    pool.dma_start(lnp[:, half * D:(half + 1) * D], bc(row)).then_inc(s_ln, 16)

            def load_gla(l):
                pool.dma_start(convw, bc(I["conv_w"][l])).then_inc(s_gla, 16)
                pool.dma_start(gnw, bc(I["gla_norm_w"][l])).then_inc(s_gla, 16)
                pool.dma_start(gkw2[0:RANK, :], I["gk_w2"][l]).then_inc(s_gla, 16)
                pool.dma_start(gkb[0:1, :], I["gk_b"][l:l + 1]).then_inc(s_gla, 16)

            def load_ada(l):
                pool.dma_start(area(BIG, 6 * D), bc(I["ada_b"][l])).then_inc(s_ada, 16)

            def load_ple(i):
                pool.dma_start(bgate, bc(I["ple_b_gate_2"][i])).then_inc(s_ple, 16)
                pool.dma_start(ptok, I["p_2"][i, 0].rearrange("(t p) c -> p t c", p=P)).then_inc(s_ple, 16)

            def root(dve, width):
                a = CONST_COLS["minushalf"][0]
                for t in range(T):
                    pool.wait_ge(dve_ready, dve + t + 1)
                    nc.gpsimd.tensor_tensor(rstd[:, t, 0:width], ve[:, t, 0:width], con[:, a:a + width],
                                            ALU.pow).then_inc(pool_ready, 1)

            load_ada(0)
            load_gla(0)
            load_ln(0)
            pool.dma_start(routw[:, :].rearrange("p (k e) -> p k e", k=KD),
                           I["router_w"][0].rearrange("(k p) e -> p k e", p=P)).then_inc(s_rout, 16)
            pool.wait_ge(s_con, 16)
            for kind, arg, n, _ in steps:
                if kind == "gla":
                    root(n.dve + 4, HEADS)
                elif kind in ("kvdown", "mla"):
                    root(n.dve, 1)
                elif kind == "ln":
                    root(n.dve, 1)
                    pool.wait_ge(src_ready, n.src + 1)
                    load_ln(n.ln + 1)
                    if n.ln == 0:
                        load_gla(1)
                    if n.ln == 1:
                        load_ada(1)
                    if n.ln == 2 * DEPTH - 1:
                        pool.dma_start(qnw, bc(I["mla_q_norm_2"][0])).then_inc(s_attn, 16)
                        pool.dma_start(kvnw, bc(I["kv_norm_2"])).then_inc(s_attn, 16)
                        pool.dma_start(bfrow[0:1, :], I["fox_b_f_2"]).then_inc(s_attn, 16)
                    if arg[0] == "plain":
                        load_ple((n.ln - 2 * DEPTH) // 4)

        @block.vector
        def _(dve):
            V = nc.vector
            step = [0]

            def link(ins):
                step[0] += 1
                ins.then_inc(dve_step, 1)
                dve.wait_ge(dve_step, step[0])

            def copy_out(g, dst, cols, scale=None):
                dve.wait_ge(g_done, g + 1)
                if scale is None:
                    V.tensor_copy(flat(dst), G[:, g % 2, 0:cols]).then_inc(g_read, 1)
                else:
                    V.tensor_scalar(dst, G[:, g % 2, 0:cols], scale, None, ALU.mult).then_inc(g_read, 1)

            def log_sigmoid(g, scratch, cols, a):
                dve.wait_ge(act_ready, a)
                V.scalar_tensor_tensor(out=scratch, in0=G[:, g % 2, 0:cols], scalar=0.0, in1=scratch,
                                       op0=ALU.min, op1=ALU.subtract).then_inc(g_read, 1)
                dve.wait_ge(g_read, g + 1)

            def mean_eps(t, width, size, a):
                dve.wait_ge(act_ready, a)
                V.tensor_scalar(ve[:, t, 0:width], ssq[:, t, 0:width], 1.0 / size, RMS_EPS,
                                ALU.mult, ALU.add).then_inc(dve_ready, 1)

            def rope(dst, lo, hi, cos, sin, t1):
                half = ROPE // 2
                link(V.tensor_tensor(t1, hi, sin, ALU.mult))
                link(V.tensor_tensor(dst[0], lo, cos, ALU.mult))
                link(V.tensor_tensor(dst[0], dst[0], t1, ALU.subtract))
                link(V.tensor_tensor(t1, lo, sin, ALU.mult))
                link(V.tensor_tensor(dst[1], hi, cos, ALU.mult))
                return V.tensor_tensor(dst[1], dst[1], t1, ALU.add)

            def attention(n, g0, fox):
                for i in range(32):
                    t, h = divmod(i, 16)
                    g, cols = g0 + i, P * (t + 1)
                    dve.wait_ge(g_done, g + 1)
                    sc = scores[:, i % 2, 0:cols]
                    if i >= 2:
                        dve.wait_ge(act_ready, n.act + 2 + i - 1)
                    if fox:
                        scalar, op = cumf[:, t, h:h + 1], ALU.add
                    else:
                        scalar, op = float((NOPE + ROPE) ** -0.5), ALU.mult
                    if t:
                        link(V.tensor_scalar(sc[:, 0:P], G[:, g % 2, 0:P], scalar, None, op))
                    link(V.scalar_tensor_tensor(out=sc[:, t * P:cols], in0=G[:, g % 2, t * P:cols], scalar=scalar,
                                                in1=C("causal"), op0=op, op1=ALU.add))
                    V.tensor_reduce(nmax[:, i % 2:i % 2 + 1], sc, AX.X, ALU.max, negate=True).then_inc(g_read, 1)
                    if i == 31:
                        weighted(n, 1, fox)
                    elif i == 17 and not fox:
                        weighted(n, 0, fox)

            def weighted(n, t, fox):
                dve.wait_ge(acc_done, n.acc + (1 if fox or t == 0 else 2))
                dve.wait_ge(act_ready, n.act + 2 + 16 * (t + 1))
                if fox:
                    link(V.reciprocal(rinv[:, :, :], rsum[:, :, :]))
                    for b in range(4):
                        tt, half = divmod(b, 2)
                        last = V.tensor_tensor(
                            src[:, tt, half * 512:(half + 1) * 512].rearrange("p (h d) -> p h d", h=8),
                            A[:, b, :].rearrange("p (h d) -> p h d", h=8),
                            rinv[:, tt, half * 8:half * 8 + 8].unsqueeze(2).to_broadcast([P, 8, FOX_D]), ALU.mult)
                    last.then_inc(acc_free, 1)
                    dve.wait_ge(acc_free, n.free + 1)
                else:
                    link(V.reciprocal(rinv[:, t, :], rsum[:, t, :]))
                    for b in range(4):
                        last = V.tensor_tensor(
                            src2[:, t, b * 512:(b + 1) * 512].rearrange("p (h d) -> p h d", h=4),
                            A[:, b, :].rearrange("p (h d) -> p h d", h=4),
                            rinv[:, t, b * 4:b * 4 + 4].unsqueeze(2).to_broadcast([P, 4, VH]), ALU.mult)
                    last.then_inc(acc_free, 1)
                    dve.wait_ge(acc_free, n.free + 1 + t)

            def ffn(n, total, body, peel, weighted_units):
                def unit(j, c):
                    par = (n.tg + j) % 2
                    for t in range(T):
                        dve.wait_ge(act_ready, c * 2 + (n.act + t + 1))
                        if weighted_units:
                            ins = V.scalar_tensor_tensor(out=hid[:, par, t, :], in0=sgt[:, t, :],
                                                         scalar=route[:, t, j % EXPERTS:j % EXPERTS + 1],
                                                         in1=G[:, t, FU:2 * FU], op0=ALU.mult, op1=ALU.mult)
                        else:
                            ins = V.tensor_tensor(hid[:, par, t, :], sgt[:, t, :], G[:, t, FU:2 * FU], ALU.mult)
                        ins.then_inc(g_read, 1)

                for c in range(peel):
                    unit(c, c)
                with dve.Fori(0, (total - peel) // body) as i:
                    for j in range(body):
                        unit(peel + j, i * body + (peel + j))

            for kind, arg, n, before in steps:
                if kind == "start":
                    dve.wait_ge(s_con, 16)
                    dve.wait_ge(act_ready, 1)
                    V.tensor_copy(condB, condT.unsqueeze(2).to_broadcast([P, KD, P])).then_inc(dve_ready, 1)
                    dve.wait_ge(s_x, 16)
                elif kind == "ada":
                    if arg:
                        V.tensor_copy(condB, condT.unsqueeze(2).to_broadcast([P, KD, P])).then_inc(cond_again, 1)
                    dve.wait_ge(s_ada, 16 * (arg + 1))
                    for c in range(12):
                        g = n.g + c
                        dst = mod[:, c // 2, (c % 2) * 512:(c % 2 + 1) * 512]
                        dve.wait_ge(g_done, g + 1)
                        V.tensor_tensor(dst, G[:, g % 2, :], dst, ALU.add).then_inc(g_read, 1)
                    dve.wait_ge(g_read, n.g + 12)
                elif kind == "mod":
                    for t in range(T):
                        link(V.scalar_tensor_tensor(out=src[:, t, :], in0=mod[:, arg + 1, :], scalar=1.0, in1=x[:, t, :],
                                                    op0=ALU.add, op1=ALU.mult))
                        last = V.tensor_tensor(src[:, t, :], src[:, t, :], mod[:, arg, :], ALU.add)
                    last.then_inc(src_ready, 1)
                elif kind == "gla":
                    for c in range(6):
                        for t in range(T):
                            copy_out(n.g + 2 * c + t, proj[:, t, c * 512:(c + 1) * 512], 512)
                    dve.wait_ge(g_read, n.g + 12)
                    dve.wait_ge(s_gla, 64 * (arg + 1))
                    for t in range(T):
                        zc = proj[:, t, C_C:C_C + CONV]
                        link(V.tensor_tensor(zc, zc, proj[:, t, C_H:C_H + CONV], ALU.mult))
                        link(V.tensor_tensor(proj[:, t, C_H:C_H + CONV], zc, convw[:, 0, :], ALU.mult))
                        link(V.tensor_tensor(z1[:, t, :], zc, convw[:, 1, :], ALU.mult))
                        last = V.tensor_tensor(zc, zc, convw[:, 2, :], ALU.mult)
                    last.then_inc(dve_ready, 1)
                    for t in range(T):
                        log_sigmoid(n.g + 12 + t, lsg[:, t, :], KW, n.act + 1 + t)
                        V.tensor_scalar(gk[:, t, :], lsg[:, t, :], 1.0 / 16.0, -1.0, ALU.mult, ALU.max) \
                            .then_inc(dve_ready, 1)
                    for t in range(T):
                        g = n.g + 14 + t
                        dve.wait_ge(g_done, g + 1)
                        V.tensor_tensor(src[:, t, 0:CONV], G[:, g % 2, :], proj[:, t, C_B:C_B + CONV], ALU.mult) \
                            .then_inc(g_read, 1)
                    for t in range(T):
                        g = n.g + 16 + t
                        dve.wait_ge(act_ready, n.act + 3 + t)
                        q, k = proj[:, t, C_Q:C_Q + KW], proj[:, t, C_K:C_K + KW]
                        V.scalar_tensor_tensor(out=q, in0=q, scalar=DK ** -0.5, in1=e3[:, t, 0:KW],
                                               op0=ALU.mult, op1=ALU.mult)
                        link(V.tensor_tensor(proj[:, t, C_C:C_C + KW], k, e3[:, t, 2 * KW:3 * KW], ALU.mult))
                        V.tensor_tensor(k, k, e3[:, t, KW:2 * KW], ALU.mult).then_inc(g_read, 1)
                    dve.wait_ge(g_read, n.g + 18)
                    link(V.memset(state, 0.0))
                    dve.wait_ge(acc_done, n.acc + 1)
                    dve.wait_ge(t_evac, n.tg + 2)
                    for c in range(3):
                        for f in range(2):
                            r = slice(DK * f, DK * f + DK)
                            for a in range(2):
                                kv = A[r, c, a * KW + f * DV:a * KW + (f + 1) * DV]
                                if c == 0:
                                    last = V.tensor_copy(state[r, 0, a, f * DV:(f + 1) * DV], kv)
                                else:
                                    last = V.scalar_tensor_tensor(out=state[r, c, a, f * DV:(f + 1) * DV],
                                                                  in0=state[r, c - 1, a, f * DV:(f + 1) * DV],
                                                                  scalar=dec[r, c // 2, a, c % 2:c % 2 + 1], in1=kv,
                                                                  op0=ALU.mult, op1=ALU.add)
                        if c < 2:
                            link(last)
                    last.then_inc(dve_ready, 1)
                    V.tensor_copy(ve[0:1, 0, 0:1], A[0:1, 0, 0:1]).then_inc(acc_free, 1)
                    for f in range(2):
                        g = n.g + 18 + f
                        dve.wait_ge(g_done, g + 1)
                        V.tensor_tensor(stm[:, f], G[:, g % 2, :].rearrange("p (h i) -> p h i", h=HEADS),
                                        C("cum").unsqueeze(1).to_broadcast([P, HEADS, P]), ALU.mult).then_inc(g_read, 1)
                    dve.wait_ge(acc_free, n.free + 1)
                    for t in range(T):
                        mean_eps(t, HEADS, DV, n.act + 7 + t)
                    for t in range(T):
                        g = n.g + 20 + t
                        dve.wait_ge(pool_ready, n.pool + t + 1)
                        y = src[:, t, CONV:CONV + VW]
                        for h in range(HEADS):
                            last = V.scalar_tensor_tensor(out=y[:, h * DV:(h + 1) * DV], in0=G[:, g % 2, h * DV:(h + 1) * DV],
                                                          scalar=rstd[:, t, h:h + 1], in1=gnw, op0=ALU.mult, op1=ALU.mult)
                        last.then_inc(g_read, 1)
                        dve.wait_ge(g_read, g + 1)
                        last = V.tensor_tensor(y, y, proj[:, t, C_H:C_H + VW], ALU.mult)
                    last.then_inc(src_ready, 1)
                elif kind == "ln":
                    how, which = arg
                    if before == "ffn" or before == "moe":
                        dve.wait_ge(down_used, n.d)
                    else:
                        dve.wait_ge(acc_done, n.acc)
                    for t in range(T):
                        acc = A[:, 2 * t:2 * t + 2, :].rearrange("p h c -> p (h c)")
                        xt = x[:, t, :]
                        if how in ("mod", "gate"):
                            delta = src[:, t, :]
                            if how == "mod":
                                link(V.scalar_tensor_tensor(out=delta, in0=mod[:, which, :], scalar=1.0, in1=acc,
                                                            op0=ALU.add, op1=ALU.mult))
                            else:
                                dve.wait_ge(act_ready, n.act - 1 + t)
                                link(V.tensor_tensor(delta, gt[:, t, :], acc, ALU.mult))
                            link(V.scalar_tensor_tensor(out=xt, in0=xt, scalar=ALPHA, in1=delta, op0=ALU.mult, op1=ALU.add))
                        elif how == "half":
                            link(V.tensor_scalar(xt, xt, ALPHA, None, ALU.mult))
                            link(V.scalar_tensor_tensor(out=xt, in0=acc, scalar=0.5, in1=xt, op0=ALU.mult, op1=ALU.add))
                        else:
                            link(V.scalar_tensor_tensor(out=xt, in0=xt, scalar=ALPHA, in1=acc, op0=ALU.mult, op1=ALU.add))
                        for half in range(2):
                            last = V.bn_stats(stats[:, t, half, :], x[:, t, half * 512:(half + 1) * 512])
                        link(last)
                        link(V.bn_aggr(mv[:, t, :], stats[:, t].rearrange("p c s -> p (c s)")))
                        V.tensor_scalar(ve[:, t, 0:1], mv[:, t, 1:2], LN_EPS, None, ALU.add).then_inc(dve_ready, 1)
                    V.tensor_copy(nmax[0:1, 0:1], mv[0:1, 0, 0:1]).then_inc(acc_free, 1)
                    dve.wait_ge(s_ln, 32 * (n.ln + 1))
                    for t in range(T):
                        xt = x[:, t, :]
                        link(V.scalar_tensor_tensor(out=xt, in0=xt, scalar=mv[:, t, 0:1], in1=lnp[:, 0:D],
                                                    op0=ALU.subtract, op1=ALU.mult))
                        dve.wait_ge(pool_ready, n.pool + t + 1)
                        last = V.scalar_tensor_tensor(out=xt, in0=xt, scalar=rstd[:, t, 0:1], in1=lnp[:, D:2 * D],
                                                      op0=ALU.mult, op1=ALU.add)
                    last.then_inc(src_ready, 1)
                    dve.wait_ge(src_ready, n.src + 1)
                elif kind == "ffn":
                    ffn(n, NU, RW, NU % RW, False)
                elif kind == "moe":
                    ffn(n, NU * EXPERTS, EXPERTS, EXPERTS, True)
                elif kind == "router":
                    for t in range(T):
                        copy_out(n.g + t, logit[:, t, :], EXPERTS)
                    dve.wait_ge(g_read, n.g + 2)
                    for t in range(T):
                        link(V.max(top8[:, t, :], logit[:, t, :]))
                        link(V.max_index(idx8[:, t * 8:(t + 1) * 8], top8[:, t, :], logit[:, t, :]))
                        link(V.tensor_copy(idxf[:, t, :], idx8[:, t * 8:(t + 1) * 8]))
                        last = V.tensor_tensor(gap[:, t:t + 1], top8[:, t, 1:2], top8[:, t, 0:1], ALU.subtract)
                    last.then_inc(dve_ready, 1)
                    dve.wait_ge(act_ready, n.act + 1)
                    link(V.tensor_scalar(w1, e2, 1.0, None, ALU.add))
                    link(V.reciprocal(w1, w1))
                    link(V.tensor_tensor(w2, e2, w1, ALU.mult))
                    for t in range(T):
                        link(V.tensor_scalar(rtmp[:, t, :], C("experts"), idxf[:, t, 0:1], w1[:, t:t + 1],
                                             ALU.is_equal, ALU.mult))
                        link(V.tensor_scalar(route[:, t, :], C("experts"), idxf[:, t, 1:2], w2[:, t:t + 1],
                                             ALU.is_equal, ALU.mult))
                        link(V.tensor_tensor(route[:, t, :], route[:, t, :], rtmp[:, t, :], ALU.add))
                elif kind == "kvdown":
                    dve.wait_ge(s_attn, 48)
                    for t in range(T):
                        mean_eps(t, 1, KVLORA, n.act + 1 + t)
                    half = ROPE // 2
                    for t in range(T):
                        g = n.g + t
                        cos = C("cos").rearrange("p (t c) -> p t c", t=T)[:, t, :]
                        sin = C("sin").rearrange("p (t c) -> p t c", t=T)[:, t, :]
                        link(rope((krd[:, t, 0:half], krd[:, t, half:ROPE]), G[:, g % 2, KVLORA:KVLORA + half],
                                  G[:, g % 2, KVLORA + half:KVLORA + ROPE], cos, sin, rinv[:, :, :].rearrange("p a b -> p (a b)")))
                        link(V.tensor_copy(krd[:, t, ROPE:2 * ROPE], krd[:, t, 0:ROPE]))
                        dve.wait_ge(pool_ready, n.pool + t + 1)
                        V.scalar_tensor_tensor(out=ckv[:, t, :], in0=G[:, g % 2, 0:KVLORA], scalar=rstd[:, t, 0:1], in1=kvnw,
                                               op0=ALU.mult, op1=ALU.mult).then_inc(g_read, 1)
                    V.tensor_copy(nmax[0:1, 0:1], rstd[0:1, 0, 0:1]).then_inc(dve_ready, 1)
                elif kind == "fox":
                    for c in range(4):
                        for f in range(4):
                            dst = fqT if c < 2 else fkT
                            copy_out(n.g + 4 * c + f, dst[:, 4 * (c % 2) + f, :], S, FOX_D ** -0.5 if c < 2 else None)
                    for c in range(2):
                        for t in range(T):
                            copy_out(n.g + 16 + 2 * c + t, fv[:, t, c * 512:(c + 1) * 512], 512)
                    for t in range(T):
                        log_sigmoid(n.g + 20 + t, flt[:, t, :], FOX_H, n.act + 1 + t)
                        V.tensor_copy(fls[:, t, :], flt[:, t, :]).then_inc(dve_ready, 1)
                    for t in range(T):
                        copy_out(n.g + 22 + t, cumf[:, t, :], FOX_H)
                    dve.wait_ge(g_read, n.g + 24)
                    attention(n, n.g + 24, True)
                    V.tensor_copy(nmax[0:1, 0:1], rinv[0:1, 0, 0:1]).then_inc(src_ready, 1)
                elif kind == "mla":
                    for t in range(T):
                        mean_eps(t, 1, QLORA, n.act + 1 + t)
                    for t in range(T):
                        g = n.g + t
                        dve.wait_ge(pool_ready, n.pool + t + 1)
                        V.scalar_tensor_tensor(out=cq[:, t, :], in0=G[:, g % 2, 0:QLORA], scalar=rstd[:, t, 0:1], in1=qnw,
                                               op0=ALU.mult, op1=ALU.mult).then_inc(g_read, 1)
                    for c in range(4):
                        g = n.g + 2 + 6 * c
                        for h in range(4):
                            copy_out(g + h, qnT[:, 4 * c + h, :], S)
                        for t in range(T):
                            copy_out(g + 4 + t, qr_raw[:, t, 4 * c:4 * c + 4, :], 4 * ROPE)
                    dve.wait_ge(g_read, n.g + 26)
                    half = ROPE // 2
                    for t in range(T):
                        cos = C("cos").rearrange("p (t c) -> p t c", t=T)[:, t:t + 1, :].to_broadcast([P, MLA_H, half])
                        sin = C("sin").rearrange("p (t c) -> p t c", t=T)[:, t:t + 1, :].to_broadcast([P, MLA_H, half])
                        link(rope((qr_rot[:, t, :, 0:half], qr_rot[:, t, :, half:ROPE]), qr_raw[:, t, :, 0:half],
                                  qr_raw[:, t, :, half:ROPE], cos, sin, ropetmp))
                    V.tensor_copy(nmax[0:1, 0:1], rstd[0:1, 0, 0:1]).then_inc(dve_ready, 1)
                    for c in range(2):
                        g = n.g + 26 + 12 * c
                        for h in range(8):
                            copy_out(g + h, knT[:, 8 * c + h, :], S)
                        for q in range(2):
                            for t in range(T):
                                copy_out(g + 8 + 2 * q + t, vtok[:, t, (2 * c + q) * 512:(2 * c + q + 1) * 512], 512)
                    dve.wait_ge(g_read, n.g + 50)
                    attention(n, n.g + 50, False)
                    V.tensor_copy(nmax[0:1, 0:1], rinv[0:1, 0, 0:1]).then_inc(src_ready, 1)
                elif kind == "ple":
                    dve.wait_ge(s_ple, 32 * (arg + 1))
                    for c in range(2):
                        for t in range(T):
                            g = n.g + 2 * c + t
                            dve.wait_ge(g_done, g + 1)
                            V.tensor_tensor(gt[:, t, c * 512:(c + 1) * 512], G[:, g % 2, :], bgate[:, c * 512:(c + 1) * 512],
                                            ALU.add).then_inc(g_read, 1)


NAMES = ["x", "c", "ada_w", "ada_b", "w_in", "conv_w", "gk_w2", "gk_b", "gla_norm_w", "w_out", "ln1_g", "ln1_b",
         "ln2_g", "ln2_b", "ffn_w_gate", "ffn_w_up", "ffn_w_down", "router_w", "moe_w_gate", "moe_w_up",
         "moe_w_down", "p_2", "ffn1_w_in_2", "ffn1_w_out_2", "ffn2_w_in_2", "ffn2_w_out_2", "ln_g_2", "ln_b_2",
         "ple_w_gate_2", "ple_b_gate_2", "ple_w_proj_2", "fox_w_in_2", "fox_b_f_2", "fox_w_o_2", "mla_w_dq_2",
         "mla_q_norm_2", "mla_w_uq_2", "mla_w_o_2", "kv_w_down_2", "kv_norm_2", "kv_w_up_2"]


def kernel(**inputs):
    import concourse.bacc as bacc
    from concourse.bass_utils import run_bass_kernel_spmd

    nc = bacc.Bacc("TRN2", target_bir_lowering=False, num_devices=1)
    arrays, aps = {}, {}
    for name in NAMES:
        a = np.ascontiguousarray(inputs[name])
        arrays[f"in_{name}"] = a
        aps[name] = nc.dram_tensor(f"in_{name}", a.shape, mybir.dt.from_np(a.dtype), kind="ExternalInput").ap()
    arrays["in_con"] = constants()
    aps["con"] = nc.dram_tensor("in_con", (P, NCONST), F32, kind="ExternalInput").ap()
    out = nc.dram_tensor("out_x", (1, S, D), F32, kind="ExternalOutput").ap()
    build(nc, aps, out)
    r = run_bass_kernel_spmd(nc, [arrays], core_ids=[0])
    return r.results[0]["out_x"]
```

```python
from contextlib import ExitStack

import numpy as np

import concourse.bass as bass
from concourse import mybir

F32 = mybir.dt.float32
F32R = mybir.dt.float32r
U32 = mybir.dt.uint32
ALU = mybir.AluOpType
ACT = mybir.ActivationFunctionType
AX = mybir.AxisListType

P = 128
S = 256
T = S // P
D = 1024
KD = D // P
DEPTH = 2
CONV = 512
WIDTH = 3
HEADS = 4
DK = 64
DV = 128
CHUNK = 64
KW = HEADS * DK
VW = HEADS * DV
RANK = 16
C_B, C_C, C_H = 0, CONV, 2 * CONV
C_Q = 3 * CONV
C_K = C_Q + KW
C_V = C_K + KW
C_G = C_V + VW
C_LOW = C_G + VW
FF = 2816
FU = 256
NU = FF // FU
EXPERTS = 8
ALPHA = (2.0 * DEPTH) ** 0.25
LN_EPS = 1e-5
RMS_EPS = 1e-6
FOX_H = 16
FOX_D = 64
MLA_H = 16
NOPE = 128
ROPE = 64
VH = 128
QLORA = 384
KVLORA = 256
THETA = 10000.0
MASKED = -1e30

RW = 2
RD = 2
WSLOT = 4096
DSLOT = 2048
PAIR = 2 * NU
NEED_WIDE = 32

CONST_COLS = {}
_col = 0
for _name, _w in (("ident", P), ("shift1", P), ("shift2", P), ("cross1", P), ("cross2", P), ("cum", P),
                  ("suffix", P), ("tri", P), ("ones", P), ("causal", P), ("slots", P), ("chunks", 2), ("experts", EXPERTS),
                  ("cos", T * ROPE // 2), ("sin", T * ROPE // 2), ("minushalf", T * HEADS)):
    CONST_COLS[_name] = (_col, _col + _w)
    _col += _w
NCONST = _col


def constants():
    c = np.zeros((P, NCONST), np.float32)
    j, i = np.meshgrid(np.arange(P), np.arange(P), indexing="ij")
    same = j // CHUNK == i // CHUNK

    def put(name, value):
        a, b = CONST_COLS[name]
        c[:, a:b] = value

    put("ident", j == i)
    put("shift1", j == i - 1)
    put("shift2", j == i - 2)
    put("cross1", j == i - 1 + P)
    put("cross2", j == i - 2 + P)
    put("cum", same & (j <= i))
    put("suffix", same & (j > i))
    put("tri", j <= i)
    put("ones", 1.0)
    put("causal", np.where(i <= j, 0.0, MASKED))
    put("chunks", np.arange(P)[:, None] // CHUNK == np.arange(2)[None, :])
    put("slots", np.arange(P)[None, :])
    put("experts", np.arange(EXPERTS)[None, :])
    half = ROPE // 2
    inv = np.float32(THETA) ** (-np.arange(half, dtype=np.float32) * np.float32(2.0 / ROPE))
    ang = np.arange(S, dtype=np.float32)[:, None] * inv[None, :].astype(np.float32)
    put("cos", np.cos(ang).reshape(T, P, half).transpose(1, 0, 2).reshape(P, T * half))
    put("sin", np.sin(ang).reshape(T, P, half).transpose(1, 0, 2).reshape(P, T * half))
    put("minushalf", -0.5)
    return c


class Tally:
    DELTA = {
        "start": dict(act=1, dve=1),
        "ada": dict(g=12, w=12),
        "mod": dict(src=1),
        "tr8": dict(tg=4),
        "tr16": dict(tg=8),
        "gla": dict(g=22, tg=4, w=7, act=8, dve=6, pool=2, acc=1, free=1, src=1),
        "out1": dict(w=2, acc=2),
        "out2": dict(w=4, acc=4),
        "ln": dict(dve=2, pool=2, free=1, src=1, ln=1),
        "trs8": dict(tg=4, act=4),
        "ffn": dict(g=2 * NU, tg=NU, w=NU, d=NU, act=3 * NU, lo=6 * NU),
        "moe": dict(g=2 * NU * EXPERTS, tg=NU * EXPERTS, w=NU * EXPERTS, d=NU * EXPERTS, act=3 * NU * EXPERTS,
                    lo=6 * NU * EXPERTS, free=EXPERTS),
        "router": dict(g=4, act=1, dve=3),
        "kvdown": dict(g=2, tg=2, w=1, act=2, dve=3, pool=2),
        "fox": dict(g=24 + 32, tg=1 + 32, w=7, act=2 + 32, dve=2, acc=1, free=1, src=1),
        "mla": dict(g=2 + 24 + 24 + 32, tg=2 + 4 + 32, w=7, act=2 + 32, dve=3, pool=2, acc=2, free=2, src=1),
        "ple": dict(g=4, tg=1, w=3, act=2, acc=1),
    }
    def __init__(self):
        self.g = self.tg = self.w = self.d = self.act = self.dve = 0
        self.pool = self.acc = self.free = self.src = self.ln = self.lo = 0

    def after(self, kind):
        new = Tally()
        e = self.DELTA[kind]
        new.g, new.tg = self.g + e.get("g", 0), self.tg + e.get("tg", 0)
        new.w, new.d = self.w + e.get("w", 0), self.d + e.get("d", 0)
        new.act, new.dve = self.act + e.get("act", 0), self.dve + e.get("dve", 0)
        new.pool, new.acc = self.pool + e.get("pool", 0), self.acc + e.get("acc", 0)
        new.free, new.src = self.free + e.get("free", 0), self.src + e.get("src", 0)
        new.ln, new.lo = self.ln + e.get("ln", 0), self.lo + e.get("lo", 0)
        return new


def stages():
    plan = [("start", 0)]
    for l in range(DEPTH):
        plan += [("ada", l), ("mod", 0), ("tr8", "src"), ("gla", l), ("tr8", "src"), ("out1", ("w_out", l)),
                 ("ln", ("mod", 2)), ("mod", 3), ("trs8", "src")]
        plan += [("ffn", "dense")] if l % 2 == 0 else [("router", 0), ("moe", 0)]
        plan += [("ln", ("mod", 5))]
    for i in range(DEPTH):
        if i:
            plan += [("tr8", "x"), ("kvdown", 0)]
        plan += [("trs8", "x"), ("ffn", ("ffn1", i)), ("ln", ("half", 0)), ("tr8", "x")]
        plan += [("mla", 0), ("tr16", "src"), ("out2", ("mla", 0))] if i else \
                [("fox", 0), ("tr8", "src"), ("out1", ("fox", 0))]
        plan += [("ln", ("plain", 0)), ("trs8", "x"), ("ffn", ("ffn2", i)), ("ln", ("half", 0)),
                 ("tr8", "x"), ("ple", i), ("ln", ("gate", 0))]
    return plan


def build(nc, I, out):
    plan = stages()
    tallies = [Tally()]
    for kind, _ in plan:
        tallies.append(tallies[-1].after(kind))
    steps = [(kind, arg, t, plan[max(i - 1, 0)][0]) for i, ((kind, arg), t) in enumerate(zip(plan, tallies))]

    with ExitStack() as ctx:
        def sb(name, cols, dt=F32, rows=P):
            return ctx.enter_context(nc.sbuf_tensor(name, [rows, cols], dt))

        def sem(name):
            return ctx.enter_context(nc.semaphore(name))

        G = ctx.enter_context(nc.psum_tensor("G", [P, 2, 512], F32))
        TB = ctx.enter_context(nc.psum_tensor("TB", [P, 2, 512], F32))
        A = ctx.enter_context(nc.psum_tensor("A", [P, 4, 512], F32))

        wide = [sb(f"wide{i}", WSLOT) for i in range(RW)]
        down = [sb(f"down{i}", DSLOT) for i in range(RD)]
        xs = sb("x_tok", T * D)
        x = xs[:, :].rearrange("p (t c) -> p t c", t=T)
        lnp = sb("ln_params", 2 * D)
        con = sb("con", NCONST)
        sg = sb("silu_gate", T * FU)
        hbuf = sb("hidden", 2 * T * FU)
        hT = sb("hidden_T", 2 * 2 * S)
        hT_at = nc.sbuf_base - 4 * 4 * S
        small = sb("small", 256)
        idx8 = sb("expert_idx", T * 8, U32)
        routw = sb("router_w", KD * EXPERTS)
        crowded = sb("crowded", 1, U32)
        pack = sb("pack", 2048)
        pick = pack[:, 0:256].rearrange("p (t s) -> p t s", t=T)
        pick_w = pack[:, 256:512].rearrange("p (t s) -> p t s", t=T)
        put_back = pack[:, 512:1024].rearrange("p (e s) -> p e s", e=2)
        packed_out = pack[:, 1024:2048]
        BIG = 2 * 4096
        ARENA = BIG + 15360 + 768
        arena = sb("arena", ARENA)
        arena_at = nc.sbuf_base - 4 * ARENA

        def split_tensor(name, cols, at):
            return nc.alloc_sbuf_tensor_at(name, [P, cols], F32R, offset=at)

        uh = split_tensor("u_hi", KD * S, arena_at)
        ul = split_tensor("u_lo", KD * S, arena_at + 4 * 2048)
        hth = split_tensor("hidden_hi", 2 * S, hT_at)
        htl = split_tensor("hidden_lo", 2 * S, hT_at + 4 * 2 * S)
        piece_at = [arena_at + 4 * (BIG + 1024 * j) for j in (0, 1, 2, 3, 4, 6, 7, 8, 9, 10, 11, 12)]
        w_hi = [split_tensor(f"w_hi{j}", 1024, piece_at[2 * j]) for j in range(6)]
        w_lo = [split_tensor(f"w_lo{j}", 1024, piece_at[2 * j + 1]) for j in range(6)]

        def C(name):
            a, b = CONST_COLS[name]
            return con[:, a:b]

        ident, ones = C("ident"), C("ones")

        def area(at, *shape):
            size = 1
            for s in shape:
                size *= s
            v = arena[:, at:at + size]
            if len(shape) == 2:
                v = v.rearrange("p (a b) -> p a b", a=shape[0])
            if len(shape) == 3:
                v = v.rearrange("p (a b c) -> p a b c", a=shape[0], b=shape[1])
            return v

        uT = area(0, 16, S)
        src = area(4096, T, D)
        src2 = area(4096, T, 2 * D)
        z1 = area(2048, T, CONV)
        gqT = area(2048, 2, S)
        gkT = area(2560, 2, S)
        stm = area(3072, 2, 2 * T, P)
        e3 = area(6144, T, 3 * KW)
        lsg = area(6144, T, KW)
        state = area(6144, 3, 2, 2 * DV)
        gk = area(7680, T, KW)
        mod = area(BIG, 6, D)
        proj = area(BIG + 6144, T, 3088)
        convw = area(BIG + 12320, WIDTH, CONV)
        gnw = area(BIG + 13856, DV)
        glowT = area(BIG + 13984, S)
        gkw2 = area(BIG + 14240, KW)
        gkb = area(BIG + 14496, KW)
        cqT = area(2048, 3, S)
        ckvT = area(BIG + 15360, 2, S)
        krT = area(BIG + 15872, S)
        moe_sum = area(BIG + 13312, T, D)
        qnT = area(BIG, MLA_H, S)
        knT = area(BIG + 4096, MLA_H, S)
        vtok = area(BIG + 8192, T, 2 * D)
        qrT = area(BIG + 12288, MLA_H // 2, S)
        cq = area(BIG, T, QLORA)
        ckv = area(BIG, T, KVLORA)
        krd = area(BIG + 512, T, 2 * ROPE)
        qr_raw = area(4096, T, MLA_H, ROPE)
        qr_rot = area(6144, T, MLA_H, ROPE)
        ropetmp = area(BIG + 4096, MLA_H, ROPE // 2)
        fqT = area(BIG, KD, S)
        fkT = area(BIG + 2048, KD, S)
        fv = area(BIG + 4096, T, D)
        ncT = area(BIG + 14336, S)
        cumf = area(BIG + 14592, T, FOX_H)
        fls = area(BIG + 14624, T, FOX_H)
        flt = area(BIG + 14656, T, FOX_H)
        qnw = area(BIG + 14688, QLORA)
        kvnw = area(BIG + 15072, KVLORA)
        bfrow = area(BIG + 15328, FOX_H)
        gt = area(BIG, T, D)
        bgate = area(BIG + 2048, D)
        ptok = area(BIG + 3072, T, S)
        pT = area(BIG + 3584, 2, S)
        scores = hbuf[:, 0:2 * S].rearrange("p (b s) -> p b s", b=2)
        probs = hbuf[:, 2 * S:4 * S].rearrange("p (b s) -> p b s", b=2)
        pbT = hT[:, 0:4 * P].rearrange("p (b s q) -> p b s q", b=2, s=2)
        hid = hbuf[:, :].rearrange("p (b t f) -> p b t f", b=2, t=T)
        hidT = hT[:, :].rearrange("p (b f s) -> p b f s", b=2, f=2)
        sgt = sg[:, :].rearrange("p (t f) -> p t f", t=T)

        stats = small[:, 0:24].rearrange("p (t c s) -> p t c s", t=T, c=2)
        mv = small[:, 24:28].rearrange("p (t c) -> p t c", t=T)
        ve = small[:, 28:36].rearrange("p (t h) -> p t h", t=T)
        rstd = small[:, 36:44].rearrange("p (t h) -> p t h", t=T)
        ssq = small[:, 44:52].rearrange("p (t h) -> p t h", t=T)
        dec = small[:, 52:60].rearrange("p (t a c) -> p t a c", t=T, a=2)
        condT = small[:, 60:68]
        cT = small[:, 68:76]
        nmax = small[:, 76:78]
        rsum = small[:, 80:112].rearrange("p (t h) -> p t h", t=T)
        rinv = small[:, 112:144].rearrange("p (t h) -> p t h", t=T)
        logit = small[:, 144:160].rearrange("p (t e) -> p t e", t=T)
        top8 = small[:, 160:176].rearrange("p (t e) -> p t e", t=T)
        gap = small[:, 176:178]
        e2 = small[:, 178:180]
        w1 = small[:, 180:182]
        w2 = small[:, 182:184]
        idxf = small[:, 184:200].rearrange("p (t e) -> p t e", t=T)
        route = small[:, 200:216].rearrange("p (t e) -> p t e", t=T)
        rtmp = small[:, 216:232].rearrange("p (t e) -> p t e", t=T)
        slotid = rtmp
        member = small[:, 232:248].rearrange("p (t e) -> p t e", t=T)
        condB = area(4096, KD, P)

        g_done = sem("g_done")
        g_read = sem("g_read")
        t_done = sem("t_done")
        t_evac = sem("t_evac")
        acc_done = sem("acc_done")
        acc_free = sem("acc_free")
        down_used = sem("down_used")
        act_ready = sem("act_ready")
        dve_ready = sem("dve_ready")
        pool_ready = sem("pool_ready")
        src_ready = sem("src_ready")
        dve_step = sem("dve_step")
        act_step = sem("act_step")
        wide_full = [sem(f"wide_full{i}") for i in range(RW)]
        down_full = [sem(f"down_full{i}") for i in range(RD)]
        s_con = sem("con_loaded")
        s_x = sem("x_loaded")
        s_c = sem("c_loaded")
        s_rout = sem("router_loaded")
        s_ada = sem("ada_bias_loaded")
        s_gla = sem("gla_params_loaded")
        s_ln = sem("ln_params_loaded")
        s_attn = sem("attn_params_loaded")
        s_ple = sem("ple_params_loaded")
        s_out = sem("out_stored")

        hi_ready = sem("hi_ready")
        lo_ready = sem("lo_ready")
        up_used = sem("up_used")
        down0_used = sem("down0_used")
        pick_ready = sem("pick_ready")
        scat_done = sem("scat_done")
        scat_read = sem("scat_read")
        cond_again = sem("cond_again")

        def ring_count(base, n, depth, need):
            return base * (need // depth) + need * (n // depth + 1)

        def up_pieces(c, j):
            if isinstance(c, int) and c == 0:
                return j + 1
            return c * 6 + (j - 1)

        def down_pieces(c, f, units):
            if isinstance(c, int) and c == units - 1:
                return 6 * units - 1 + f
            return c * 6 + (9 + f)

        def roll(eng, units, step):
            step(0, 0)
            step(1, 1)
            with eng.Fori(0, (units - 3) // 2) as i:
                for j in (2, 3):
                    step(j, i * 2 + j)
            step(units - 1, units - 1)

        def straight(eng, units, step):
            for c in range(units):
                step(c, c)

        PREP_AT = 4
        G_PAIR = PAIR + 6
        ACT_PAIR = 2 * PAIR + 6

        def g_unit(c):
            return c + 3 if c <= PREP_AT else c + 6

        def g_prep(e):
            return (PREP_AT + 4) * e

        def a_silu(c):
            return 2 * c + 3 + (2 if c > PREP_AT else 0) + (1 if c > NU else 0)

        def a_prep(e, half):
            return 1 + half + (2 + 2 * (PREP_AT + 1)) * e

        def a_out(e):
            return a_silu(NU) + 2 if e == 0 else ACT_PAIR

        def flat(ap):
            return {2: lambda a: a, 3: lambda a: a.rearrange("p a b -> p (a b)")}[len(ap.shape)](ap)

        def swiglu(arg):
            if arg == "dense":
                return I["ffn_w_gate"][0], I["ffn_w_up"][0], I["ffn_w_down"][0]
            name, i = arg
            w = I[f"{name}_w_in_2"][i]
            return w[:, 0:FF], w[:, FF:2 * FF], I[f"{name}_w_out_2"][i]

        block = ctx.enter_context(nc.Block())

        @block.sync
        def _(sp):
            released = []
            state_w = {"w": 0}

            def wait_slot():
                w = state_w["w"]
                if w >= RW:
                    s, v = released[w - RW]
                    sp.wait_ge(s, v)

            def fill(view_k, kt, cols, freed_by):
                wait_slot()
                w = state_w["w"]
                dst = wide[w % RW][:, 0:kt * cols].rearrange("p (k c) -> p k c", k=kt)
                cut = (kt + 1) // 2
                for a, b in ((0, cut), (cut, kt)):
                    sp.dma_start(dst[:, a:b], view_k[:, a:b]).then_inc(wide_full[w % RW], 16)
                released.append(freed_by)
                state_w["w"] = w + 1

            def kview(w_ap):
                return w_ap.rearrange("(k p) c -> p k c", p=P)

            def load_up(slot, gate, up, at):
                gv = wide[slot][:, :].rearrange("p (k h f) -> p k h f", k=KD, h=2)
                sp.dma_start(gv[:, :, 0], kview(gate)[:, :, bass.ds(at, FU)]).then_inc(wide_full[slot], 16)
                sp.dma_start(gv[:, :, 1], kview(up)[:, :, bass.ds(at, FU)]).then_inc(wide_full[slot], 16)

            def load_down(dslot, dn, at):
                sp.dma_start(down[dslot][:, :].rearrange("p (f c) -> p f c", f=2),
                             dn[bass.ds(at, FU), :].rearrange("(f p) c -> p f c", p=P)).then_inc(down_full[dslot], 16)

            sp.dma_start(con[:, :], I["con"]).then_inc(s_con, 16)
            for kind, arg, n, _ in steps:
                if kind == "ada":
                    v = kview(I["ada_w"][arg])
                    for c in range(12):
                        fill(v[:, :, c * 512:(c + 1) * 512], KD, 512, (g_done, n.g + c + 1))
                elif kind == "gla":
                    v = kview(I["w_in"][arg])
                    for c in range(6):
                        fill(v[:, :, c * 512:(c + 1) * 512], KD, 512, (g_done, n.g + 2 * c + 2))
                    fill(v[:, :, C_LOW:C_LOW + RANK], KD, RANK, (t_done, n.tg + 1))
                elif kind in ("out1", "out2"):
                    name, i = arg
                    w_ap = {"w_out": I["w_out"], "fox": I["fox_w_o_2"], "mla": I["mla_w_o_2"]}[name][i]
                    v, kt = kview(w_ap), (KD if kind == "out1" else 2 * KD)
                    cols = WSLOT // kt
                    for c in range(D // cols):
                        fill(v[:, :, c * cols:(c + 1) * cols], kt, cols, (acc_done, n.acc + c + 1))
                elif kind == "ffn":
                    gate, up, dn = swiglu(arg)

                    def step_in(j, c):
                        if j >= RW:
                            sp.wait_ge(lo_ready, up_pieces(c - RW, 3) + n.lo)
                        load_up((n.w + j) % RW, gate, up, c * FU)
                        if j:
                            down_in(j - 1, c - 1)

                    def down_in(j, c):
                        if j >= RD:
                            sp.wait_ge(lo_ready, down_pieces(c - RD, 1, NU) + n.lo)
                        elif n.lo:
                            sp.wait_ge(lo_ready, n.lo)
                        load_down((n.d + j) % RD, dn, c * FU)

                    for c in range(3):
                        if c < RW:
                            wait_slot()
                            state_w["w"] += 1
                            released.append((lo_ready, n.lo + up_pieces(c, 3)))
                        step_in(c, c)
                    with sp.Fori(0, (NU - 3) // 2) as i:
                        for j in (3, 4):
                            step_in(j, i * 2 + j)
                    down_in(NU - 1, NU - 1)
                    for c in range(RW, NU):
                        released.append((lo_ready, n.lo + up_pieces(c, 3)))
                    state_w["w"] += NU - RW
                elif kind == "moe":
                    gates, ups, dns = I["moe_w_gate"][0], I["moe_w_up"][0], I["moe_w_down"][0]
                    for _ in range(RW):
                        wait_slot()
                        state_w["w"] += 1
                        released.append(None)
                    with sp.Fori(0, EXPERTS // 2) as i:
                        lo0 = i * (6 * PAIR) + n.lo
                        for c in range(PAIR):
                            sp.wait_ge(lo_ready, lo0 + up_pieces(c - RW, 3) if c >= RW else lo0)
                            gate = gates[bass.ds(i * 2 + c // NU, 1)].rearrange("e d f -> (e d) f")
                            up = ups[bass.ds(i * 2 + c // NU, 1)].rearrange("e d f -> (e d) f")
                            load_up((n.w + c) % RW, gate, up, (c % NU) * FU)
                            for b in ([c - 1] if c else []) + ([c] if c == PAIR - 1 else []):
                                if b >= RD:
                                    sp.wait_ge(lo_ready, lo0 + down_pieces(b - RD, 1, PAIR))
                                dn = dns[bass.ds(i * 2 + b // NU, 1)].rearrange("e d f -> (e d) f")
                                load_down((n.d + b) % RD, dn, (b % NU) * FU)
                    for c in range(RW, NU * EXPERTS):
                        in_last = c - (EXPERTS // 2 - 1) * PAIR
                        released.append((lo_ready, n.lo + (EXPERTS // 2 - 1) * 6 * PAIR + up_pieces(in_last, 3))
                                        if in_last >= 0 else None)
                    state_w["w"] += NU * EXPERTS - RW
                elif kind == "kvdown":
                    fill(kview(I["kv_w_down_2"]), KD, KVLORA + ROPE, (g_done, n.g + 2))
                elif kind == "fox":
                    v = kview(I["fox_w_in_2"][0])
                    for c in range(6):
                        last = n.g + (4 * c + 4 if c < 4 else 16 + 2 * (c - 4) + 2)
                        fill(v[:, :, c * 512:(c + 1) * 512], KD, 512, (g_done, last))
                    fill(v[:, :, 3 * D:3 * D + FOX_H], KD, FOX_H, (g_done, n.g + 22))
                elif kind == "mla":
                    fill(kview(I["mla_w_dq_2"][0]), KD, QLORA, (g_done, n.g + 2))
                    v = I["mla_w_uq_2"][0].rearrange("(k p) h d -> p k (h d)", p=P)
                    cols = 4 * (NOPE + ROPE)
                    for c in range(4):
                        fill(v[:, :, c * cols:(c + 1) * cols], 3, cols, (g_done, n.g + 2 + 6 * c + 6))
                    v = I["kv_w_up_2"].rearrange("(k p) h d -> p k (h d)", p=P)
                    for c in range(2):
                        fill(v[:, :, c * 2048:(c + 1) * 2048], 2, 2048, (g_done, n.g + 26 + 12 * c + 12))
                elif kind == "ple":
                    v = kview(I["ple_w_gate_2"][arg])
                    for c in range(2):
                        fill(v[:, :, c * 512:(c + 1) * 512], KD, 512, (g_done, n.g + 2 * c + 2))
                    fill(kview(I["ple_w_proj_2"][arg]), 2, D, (acc_done, n.acc + 1))
            sp.wait_ge(src_ready, tallies[-1].src)
            sp.dma_start(out[0].rearrange("(t p) c -> p t c", p=P), x).then_inc(s_out, 16)
            sp.wait_ge(s_out, 16)

        @block.tensor
        def _(pe):
            def open_g(g):
                if not isinstance(g, int) or g >= 2:
                    pe.wait_ge(g_read, g - 1)

            def open_t(tg):
                if not isinstance(tg, int) or tg >= 2:
                    pe.wait_ge(t_evac, tg - 1)

            def wide_ready(w):
                pe.wait_ge(wide_full[w % RW], NEED_WIDE * (w // RW + 1))

            def slot(w, kt, cols):
                return wide[w % RW][:, 0:kt * cols].rearrange("p (k c) -> p k c", k=kt)

            def mm(o, lhsT, rhs, start, stop):
                return nc.tensor.matmul(o, lhsT, rhs, start=start, stop=stop, skip_group_check=True)

            def tok(t):
                return slice(t * P, (t + 1) * P)

            def project(g, t, aT, kt, rhs_of, cols):
                open_g(g)
                for k in range(kt):
                    last = mm(G[:, g % 2, 0:cols], aT[:, k, tok(t)], rhs_of(k), k == 0, k == kt - 1)
                return last.then_inc(g_done, 1)

            def project_T(g, lhs_of, aT, kt):
                open_g(g)
                for k in range(kt):
                    last = mm(G[:, g % 2, 0:S], lhs_of(k), aT[:, k, :], k == 0, k == kt - 1)
                return last.then_inc(g_done, 1)

            def transposes(tg, blocks):
                open_t(tg)
                for b, block_in in enumerate(blocks):
                    last = nc.tensor.transpose(TB[:, tg % 2, b * P:(b + 1) * P], block_in, ident)
                return last.then_inc(t_done, 1)

            def attention(n, g0, tg0, act0, heads, rows, scores_of, vcols, free0):
                todo = [(t, h) for t in range(T) for h in range(heads)]
                per_t = len(todo) // T
                for i in range(len(todo) + 2):
                    if i < len(todo):
                        t, h = todo[i]
                        open_g(g0 + i)
                        scores_of(G[:, (g0 + i) % 2, 0:P * (t + 1)], t, h).then_inc(g_done, 1)
                    if 1 <= i <= len(todo):
                        t, h = todo[i - 1]
                        pe.wait_ge(act_ready, act0 + i)
                        transposes(tg0 + i - 1, [probs[:, (i - 1) % 2, tok(b)] for b in range(t + 1)])
                    if i >= 2:
                        t, h = todo[i - 2]
                        pe.wait_ge(t_evac, tg0 + i - 1)
                        if i == 2:
                            pe.wait_ge(acc_free, free0)
                        if vcols == VH and t and h == 0:
                            pe.wait_ge(acc_free, free0 + 1)
                        if vcols == VH:
                            o = A[:, h // 4, (h % 4) * VH:(h % 4 + 1) * VH]
                            v = vtok
                        else:
                            o = A[:, 2 * t + h // 8, (h % 8) * FOX_D:(h % 8 + 1) * FOX_D]
                            v = fv
                        for b in range(t + 1):
                            last = mm(o, pbT[:, i % 2, b, :], v[:, b, h * vcols:(h + 1) * vcols], b == 0, b == t)
                        if (i - 2) % per_t == per_t - 1 and (vcols == VH or t == T - 1):
                            last.then_inc(acc_done, 1)

            uhv = uh[:, :].rearrange("p (k s) -> p k s", k=KD)
            ulv = ul[:, :].rearrange("p (k s) -> p k s", k=KD)
            hthv = hth[:, :].rearrange("p (f s) -> p f s", f=2)
            htlv = htl[:, :].rearrange("p (f s) -> p f s", f=2)

            def mm3(o, a_hi, a_lo, b_hi, b_lo, start, stop):
                mm(o, a_hi, b_hi, start, False)
                mm(o, a_hi, b_lo, False, False)
                return mm(o, a_lo, b_hi, False, stop)

            def run(n, units, walk, past, first_of, last_of, fresh_acc):
                def up(j, c):
                    for q in range(4):
                        pe.wait_ge(lo_ready, past * 6 + up_pieces(c, q) + n.lo)
                        if q == 0:
                            open_g((c + past) * 2 + (n.g + 1))
                        hi = w_hi[q][:, :].rearrange("p (k c) -> p k c", k=2)
                        lo = w_lo[q][:, :].rearrange("p (k c) -> p k c", k=2)
                        for kk in range(2):
                            k = 2 * q + kk
                            for t in range(T):
                                last = mm3(G[:, t, :], uhv[:, k, tok(t)], ulv[:, k, tok(t)], hi[:, kk, :], lo[:, kk, :],
                                           k == 0, k == KD - 1)
                                if k == KD - 1:
                                    last.then_inc(g_done, 1)
                        if q < 3:
                            last.then_inc(up_used, 1)

                def down_product(j, c):
                    if j in first_of:
                        pe.wait_ge(acc_free, fresh_acc(j))
                    for f in range(2):
                        pe.wait_ge(lo_ready, past * 6 + down_pieces(c, f, units) + n.lo)
                        hi, lo = w_hi[4 + f], w_lo[4 + f]
                        for t in range(T):
                            for half in range(2):
                                cols = slice(half * 512, half * 512 + 512)
                                last = mm3(A[:, 2 * t + half, :], hthv[:, f, tok(t)], htlv[:, f, tok(t)],
                                           hi[:, cols], lo[:, cols], j in first_of and f == 0, j in last_of and f == 1)
                        last.then_inc(down_used if f else down0_used, 1)

                def turn(j, c):
                    tg = (c + past) + n.tg
                    pe.wait_ge(g_read, (c + past) * 2 + (n.g + 2))
                    open_t(tg)
                    for f in range(2):
                        for t in range(T):
                            last = nc.tensor.transpose(TB[:, (n.tg + j) % 2, f * S + t * P:f * S + (t + 1) * P],
                                                       hid[:, 0, t, tok(f)], ident)
                    last.then_inc(t_done, 1)

                def step(j, c):
                    up(j, c)
                    if j:
                        pe.wait_ge(t_evac, (c + past) + n.tg)
                        down_product(j - 1, c - 1)
                    turn(j, c)

                walk(pe, units, step)
                pe.wait_ge(t_evac, past + (n.tg + units))
                down_product(units - 1, units - 1)

            def run_packed(n, i):
                past = i * PAIR
                g0, a0 = i * G_PAIR + n.g, i * ACT_PAIR + n.act

                def prepare(e):
                    pe.wait_ge(pick_ready, i * 2 + (e + 1))
                    b = (n.g + g_prep(e)) % 2
                    pe.wait_ge(g_read, g0 + (g_prep(e) - 1))
                    for t in range(T):
                        last = nc.tensor.transpose(G[:, b, tok(t)], pick_w[:, t, :], ident)
                    last.then_inc(g_done, 1)
                    for half in range(2):
                        b = (n.g + g_prep(e) + 1 + half) % 2
                        pe.wait_ge(g_read, g0 + (g_prep(e) + half))
                        for kk in range(4):
                            for t in range(T):
                                last = mm(G[:, b, tok(kk)], src[:, t, tok(4 * half + kk)], pick[:, t, :], t == 0, t == 1)
                        last.then_inc(g_done, 1)

                def up(c):
                    e, b = c // NU, (n.g + g_unit(c)) % 2
                    if c % NU == 0:
                        pe.wait_ge(g_read, g0 + (g_prep(e) + 3))
                    for q in range(4):
                        pe.wait_ge(lo_ready, past * 6 + (up_pieces(c, q) + n.lo))
                        if q == 0:
                            pe.wait_ge(g_read, g0 + (g_unit(c) - 1))
                        for kk in range(2):
                            k = 2 * q + kk
                            at = e * 1024 + k * P
                            last = mm3(G[:, b, :], uh[:, at:at + P], ul[:, at:at + P],
                                       w_hi[q][:, kk * 512:(kk + 1) * 512], w_lo[q][:, kk * 512:(kk + 1) * 512],
                                       k == 0, k == KD - 1)
                        last.then_inc(up_used if q < 3 else g_done, 1)

                def down_product(c):
                    e = c // NU
                    if c == 0:
                        pe.wait_ge(acc_free, i * 2 + n.free)
                    for f in range(2):
                        pe.wait_ge(lo_ready, past * 6 + (down_pieces(c, f, PAIR) + n.lo))
                        for half in range(2):
                            cols = slice(half * 512, half * 512 + 512)
                            last = mm3(A[:, 2 * e + half, :], hth[:, tok(f)], htl[:, tok(f)], w_hi[4 + f][:, cols],
                                       w_lo[4 + f][:, cols], c % NU == 0 and f == 0, c % NU == NU - 1 and f == 1)
                        last.then_inc(down_used if f else down0_used, 1)

                def turn(c):
                    pe.wait_ge(g_read, g0 + (g_unit(c) + 1))
                    tg = past + (c + n.tg)
                    open_t(tg)
                    for f in range(2):
                        last = nc.tensor.transpose(TB[:, (n.tg + c) % 2, tok(f)], hid[:, 0, 0, tok(f)], ident)
                    last.then_inc(t_done, 1)

                def scatter(e, t, banks):
                    for half in range(2):
                        last = mm(A[:, banks + half, :], put_back[:, e, tok(t)],
                                  packed_out[:, half * 512:(half + 1) * 512], True, True)
                    last.then_inc(scat_done, 1)

                prepare(0)
                for c in range(PAIR):
                    up(c)
                    if c:
                        pe.wait_ge(t_evac, past + (c + n.tg))
                        down_product(c - 1)
                    turn(c)
                    if c == PREP_AT:
                        prepare(1)
                    if c == NU + 1:
                        pe.wait_ge(act_ready, a0 + a_out(0))
                        scatter(0, 0, 0)
                    if c == NU + 2:
                        pe.wait_ge(scat_read, i * 2 + 1)
                        scatter(0, 1, 0)
                pe.wait_ge(t_evac, past + (n.tg + PAIR))
                down_product(PAIR - 1)
                pe.wait_ge(act_ready, a0 + a_out(1))
                scatter(1, 0, 2)
                pe.wait_ge(acc_free, i * 2 + (n.free + 1))
                scatter(1, 1, 0)

            pe.wait_ge(s_con, 16)
            for kind, arg, n, before in steps:
                if kind == "ada":
                    if arg == 0:
                        pe.wait_ge(dve_ready, 1)
                    else:
                        pe.wait_ge(cond_again, 1)
                    for c in range(12):
                        g = n.g + c
                        wide_ready(n.w + c)
                        open_g(g)
                        wv = slot(n.w + c, KD, 512)
                        for k in range(KD):
                            last = mm(G[:, g % 2, :], condB[:, k, :], wv[:, k, :], k == 0, k == KD - 1)
                        last.then_inc(g_done, 1)
                elif kind in ("tr8", "tr16", "trs8"):
                    pe.wait_ge(src_ready, n.src)
                    if kind == "trs8":
                        pe.wait_ge(t_evac, n.tg)
                    kt = 16 if kind == "tr16" else 8
                    view = x if arg == "x" else (src if kt == 8 else src2)
                    for j in range(kt // 2):
                        transposes(n.tg + j, [view[:, t, tok(2 * j + k)] for k in range(2) for t in range(T)])
                elif kind == "gla":
                    pe.wait_ge(t_evac, n.tg)
                    for c in range(6):
                        wide_ready(n.w + c)
                        wv = slot(n.w + c, KD, 512)
                        for t in range(T):
                            project(n.g + 2 * c + t, t, uT, KD, lambda k: wv[:, k, :], 512)
                    wide_ready(n.w + 6)
                    wv6 = slot(n.w + 6, KD, RANK)
                    open_t(n.tg)
                    for k in range(KD):
                        last = mm(TB[0:RANK, n.tg % 2, 0:S], wv6[:, k, :], uT[:, k, :], k == 0, k == KD - 1)
                    last.then_inc(t_done, 1)
                    pe.wait_ge(s_gla, 64 * (arg + 1))
                    pe.wait_ge(t_evac, n.tg + 1)
                    for t in range(T):
                        g = n.g + 12 + t
                        open_g(g)
                        mm(G[:, g % 2, 0:KW], ones[0:1, :], gkb[0:1, :], True, False)
                        mm(G[:, g % 2, 0:KW], glowT[0:RANK, tok(t)], gkw2[0:RANK, :], False, True) \
                            .then_inc(g_done, 1)
                    pe.wait_ge(dve_ready, n.dve + 1)
                    for t in range(T):
                        g = n.g + 14 + t
                        open_g(g)
                        o = G[:, g % 2, :]
                        mm(o, ident, proj[:, t, C_C:C_C + CONV], True, False)
                        mm(o, C("shift1"), z1[:, t, :], False, False)
                        if t:
                            mm(o, C("cross1"), z1[:, t - 1, :], False, False)
                            mm(o, C("cross2"), proj[:, t - 1, C_H:C_H + CONV], False, False)
                        mm(o, C("shift2"), proj[:, t, C_H:C_H + CONV], False, True).then_inc(g_done, 1)
                    for t in range(T):
                        g = n.g + 16 + t
                        pe.wait_ge(dve_ready, n.dve + 2 + t)
                        open_g(g)
                        mm(G[:, g % 2, 0:KW], C("cum"), gk[:, t, :], True, True)
                        mm(G[:, g % 2, KW:2 * KW], C("suffix"), gk[:, t, :], True, True).then_inc(g_done, 1)
                    open_t(n.tg + 1)
                    for t in range(T):
                        for a in range(2):
                            last = mm(TB[:, (n.tg + 1) % 2, t * 4 + a * 2:t * 4 + a * 2 + 2],
                                      gk[:, t, tok(a)], C("chunks"), True, True)
                    last.then_inc(t_done, 1)
                    pe.wait_ge(g_read, n.g + 18)
                    transposes(n.tg + 2, [proj[:, t, C_Q + a * P:C_Q + (a + 1) * P] for a in range(2)
                                          for t in range(T)])
                    transposes(n.tg + 3, [proj[:, t, C_C + a * P:C_C + (a + 1) * P] for a in range(2)
                                          for t in range(T)])
                    pe.wait_ge(acc_free, n.free) if n.free else None
                    for c in range(3):
                        t, r = c // 2, slice(CHUNK * (c % 2), CHUNK * (c % 2) + CHUNK)
                        for a in range(2):
                            last = mm(A[:, c, a * KW:(a + 1) * KW], proj[r, t, C_K + a * P:C_K + (a + 1) * P],
                                      proj[r, t, C_V + a * KW:C_V + (a + 1) * KW], True, True)
                    last.then_inc(acc_done, 1)
                    pe.wait_ge(t_evac, n.tg + 4)
                    for f in range(2):
                        g = n.g + 18 + f
                        r = slice(DK * f, DK * f + DK)
                        open_g(g)
                        for j in range(2 * T):
                            a, t = divmod(j, T)
                            last = mm(G[:, g % 2, tok(j)], gkT[r, a, tok(t)], gqT[r, a, tok(t)], True, True)
                        last.then_inc(g_done, 1)
                    pe.wait_ge(g_read, n.g + 20)
                    pe.wait_ge(dve_ready, n.dve + 4)
                    for t in range(T):
                        g = n.g + 20 + t
                        open_g(g)
                        for h in range(HEADS):
                            mm(G[:, g % 2, tok(h)], stm[:, h % 2, T * (h // 2) + t, :],
                               proj[:, t, C_V + h * DV:C_V + (h + 1) * DV], h == 0, False)
                        for f in range(2):
                            c = 2 * t + f
                            if c:
                                q = slice(CHUNK * f, CHUNK * f + CHUNK)
                                for a in range(2):
                                    last = mm(G[q, g % 2, a * KW:(a + 1) * KW],
                                              gqT[:, a, t * P + CHUNK * f:t * P + CHUNK * f + CHUNK],
                                              state[:, c - 1, a, :], False, True)
                        last.then_inc(g_done, 1)
                elif kind in ("out1", "out2"):
                    pe.wait_ge(t_evac, n.tg)
                    pe.wait_ge(acc_free, n.free)
                    kt = KD if kind == "out1" else 2 * KD
                    cols = WSLOT // kt
                    for c in range(D // cols):
                        wide_ready(n.w + c)
                        wv = slot(n.w + c, kt, cols)
                        half, at = divmod(c * cols, 512)
                        for t in range(T):
                            for k in range(kt):
                                last = mm(A[:, 2 * t + half, at:at + cols], uT[:, k, tok(t)], wv[:, k, :],
                                          k == 0, k == kt - 1)
                        last.then_inc(acc_done, 1)
                elif kind == "ffn":
                    pe.wait_ge(t_evac, n.tg)
                    run(n, NU, roll, 0, (0,), (NU - 1,), lambda j: n.free)
                elif kind == "moe":
                    pe.wait_ge(t_evac, n.tg)
                    pe.wait_ge(dve_ready, n.dve)
                    full = pe.value_load(crowded[0:1, 0:1], min_val=0, max_val=1)
                    with pe.If(full == 0):
                        with pe.Fori(0, EXPERTS // 2) as i:
                            run_packed(n, i)
                        pe.drain().then_inc(g_done, 2 * NU * EXPERTS - G_PAIR * (EXPERTS // 2))
                    with pe.Else():
                        with pe.Fori(0, EXPERTS // 2) as i:
                            run(n, PAIR, straight, i * PAIR, (0, NU), (NU - 1, PAIR - 1),
                                lambda j: i * 2 + (n.free + j // NU))
                elif kind == "router":
                    pe.wait_ge(t_evac, n.tg)
                    pe.wait_ge(s_rout, 16)
                    rv = routw[:, :].rearrange("p (k e) -> p k e", k=KD)
                    for t in range(T):
                        g = n.g + t
                        open_g(g)
                        for k in range(KD):
                            mm(G[:, g % 2, 0:EXPERTS], uhv[:, k, tok(t)].bitcast(F32), rv[:, k, :], k == 0, False)
                            last = mm(G[:, g % 2, 0:EXPERTS], ulv[:, k, tok(t)].bitcast(F32), rv[:, k, :],
                                      False, k == KD - 1)
                        last.then_inc(g_done, 1)
                    pe.wait_ge(dve_ready, n.dve + 2)
                    for t in range(T):
                        g = n.g + 2 + t
                        open_g(g)
                        last = mm(G[:, g % 2, 0:EXPERTS], C("tri"), member[:, t, :], True, t == 0)
                        if t:
                            mm(G[:, g % 2, 0:EXPERTS], ones, member[:, 0, :], False, True)
                            mm(G[:, g % 2, EXPERTS:2 * EXPERTS], ones, member[:, 0, :], True, False)
                            last = mm(G[:, g % 2, EXPERTS:2 * EXPERTS], ones, member[:, 1, :], False, True)
                        last.then_inc(g_done, 1)
                elif kind == "kvdown":
                    pe.wait_ge(t_evac, n.tg)
                    wide_ready(n.w)
                    wv = slot(n.w, KD, KVLORA + ROPE)
                    for t in range(T):
                        project(n.g + t, t, uT, KD, lambda k: wv[:, k, :], KVLORA + ROPE)
                    pe.wait_ge(dve_ready, n.dve + 3)
                    transposes(n.tg, [ckv[:, t, tok(k)] for k in range(2) for t in range(T)])
                    transposes(n.tg + 1, [krd[:, t, :] for t in range(T)])
                elif kind == "fox":
                    pe.wait_ge(t_evac, n.tg)
                    for c in range(4):
                        wide_ready(n.w + c)
                        wv = slot(n.w + c, KD, 512)
                        for f in range(4):
                            project_T(n.g + 4 * c + f, lambda k: wv[:, k, tok(f)], uT, KD)
                    for c in range(4, 6):
                        wide_ready(n.w + c)
                        wv = slot(n.w + c, KD, 512)
                        for t in range(T):
                            project(n.g + 16 + 2 * (c - 4) + t, t, uT, KD, lambda k: wv[:, k, :], 512)
                    wide_ready(n.w + 6)
                    pe.wait_ge(s_attn, 48)
                    wv6 = slot(n.w + 6, KD, FOX_H)
                    for t in range(T):
                        g = n.g + 20 + t
                        open_g(g)
                        mm(G[:, g % 2, 0:FOX_H], ones[0:1, :], bfrow[0:1, :], True, False)
                        for k in range(KD):
                            last = mm(G[:, g % 2, 0:FOX_H], uT[:, k, tok(t)], wv6[:, k, :], False, k == KD - 1)
                        last.then_inc(g_done, 1)
                    pe.wait_ge(dve_ready, n.dve + 2)
                    for t in range(T):
                        g = n.g + 22 + t
                        open_g(g)
                        last = mm(G[:, g % 2, 0:FOX_H], C("tri"), fls[:, t, :], True, t == 0)
                        if t:
                            last = mm(G[:, g % 2, 0:FOX_H], ones, fls[:, 0, :], False, True)
                        last.then_inc(g_done, 1)
                    open_t(n.tg)
                    for t in range(T):
                        o = TB[0:FOX_H, n.tg % 2, tok(t)]
                        last = mm(o, fls[:, t, :], C("tri"), True, t == 0)
                        if t:
                            last = mm(o, fls[:, 0, :], ones, False, True)
                    last.then_inc(t_done, 1)
                    pe.wait_ge(t_evac, n.tg + 1)
                    pe.wait_ge(g_read, n.g + 24)

                    def fox_scores(o, t, h):
                        r = slice(FOX_D * (h % 2), FOX_D * (h % 2) + FOX_D)
                        mm(o, fqT[r, h // 2, tok(t)], fkT[r, h // 2, 0:P * (t + 1)], True, False)
                        return mm(o, ident[0:FOX_H, h:h + 1].to_broadcast([FOX_H, P]), ncT[0:FOX_H, 0:P * (t + 1)],
                                  False, True)

                    attention(n, n.g + 24, n.tg + 1, n.act + 2, FOX_H, None, fox_scores, FOX_D, n.free)
                elif kind == "mla":
                    pe.wait_ge(t_evac, n.tg)
                    wide_ready(n.w)
                    wv = slot(n.w, KD, QLORA)
                    for t in range(T):
                        project(n.g + t, t, uT, KD, lambda k: wv[:, k, :], QLORA)
                    pe.wait_ge(g_read, n.g + 2)
                    transposes(n.tg, [cq[:, t, tok(k)] for k in range(2) for t in range(T)])
                    transposes(n.tg + 1, [cq[:, t, tok(2)] for t in range(T)])
                    pe.wait_ge(t_evac, n.tg + 2)
                    for c in range(4):
                        wide_ready(n.w + 1 + c)
                        wv = slot(n.w + 1 + c, 3, 4 * (NOPE + ROPE))
                        wr = wide[(n.w + 1 + c) % RW][:, 0:12 * (NOPE + ROPE)].rearrange(
                            "p (k h d) -> p k h d", k=3, h=4)
                        g = n.g + 2 + 6 * c
                        for h in range(4):
                            project_T(g + h, lambda k: wr[:, k, h, 0:NOPE], cqT, 3)
                        for t in range(T):
                            project(g + 4 + t, t, cqT, 3, lambda k: wr[:, k, :, NOPE:NOPE + ROPE], 4 * ROPE)
                    pe.wait_ge(dve_ready, n.dve + 3)
                    for j in range(4):
                        transposes(n.tg + 2 + j, [qr_rot[:, t, 4 * j + 2 * a:4 * j + 2 * a + 2, :].rearrange(
                            "p h d -> p (h d)") for a in range(2) for t in range(T)])
                    for c in range(2):
                        wide_ready(n.w + 5 + c)
                        wr2 = wide[(n.w + 5 + c) % RW][:, :].rearrange("p (k h d) -> p k h d", k=2, h=8)
                        g = n.g + 26 + 12 * c
                        for h in range(8):
                            project_T(g + h, lambda k: wr2[:, k, h, 0:NOPE], ckvT, 2)
                        for q in range(2):
                            for t in range(T):
                                project(g + 8 + 2 * q + t, t, ckvT, 2,
                                        lambda k: wr2[:, k, 4 * q:4 * q + 4, NOPE:NOPE + VH], 4 * VH)
                    pe.wait_ge(t_evac, n.tg + 6)
                    pe.wait_ge(g_read, n.g + 50)

                    def mla_scores(o, t, h):
                        r = slice(ROPE * (h % 2), ROPE * (h % 2) + ROPE)
                        mm(o, qnT[:, h, tok(t)], knT[:, h, 0:P * (t + 1)], True, False)
                        return mm(o, qrT[r, h // 2, tok(t)], krT[r, 0:P * (t + 1)], False, True)

                    attention(n, n.g + 50, n.tg + 6, n.act + 2, MLA_H, None, mla_scores, VH, n.free)
                elif kind == "ple":
                    pe.wait_ge(t_evac, n.tg)
                    for c in range(2):
                        wide_ready(n.w + c)
                        wv = slot(n.w + c, KD, 512)
                        for t in range(T):
                            project(n.g + 2 * c + t, t, uT, KD, lambda k: wv[:, k, :], 512)
                    pe.wait_ge(s_ple, 32 * (arg + 1))
                    transposes(n.tg, [ptok[:, t, tok(k)] for k in range(2) for t in range(T)])
                    pe.wait_ge(t_evac, n.tg + 1)
                    pe.wait_ge(acc_free, n.free)
                    wide_ready(n.w + 2)
                    wv = slot(n.w + 2, 2, D)
                    for t in range(T):
                        for half in range(2):
                            for k in range(2):
                                last = mm(A[:, 2 * t + half, :], pT[:, k, tok(t)],
                                          wv[:, k, half * 512:(half + 1) * 512], k == 0, k == 1)
                    last.then_inc(acc_done, 1)

        @block.scalar
        def _(act):
            act.dma_start(x, I["x"][0].rearrange("(t p) c -> p t c", p=P)).then_inc(s_x, 16)
            act.dma_start(cT, I["c"].rearrange("a (k p) -> p (a k)", p=P),
                          allow_slow_non_contiguous=True).then_inc(s_c, 16)
            step = [0]

            def link(ins):
                step[0] += 1
                ins.then_inc(act_step, 1)
                act.wait_ge(act_step, step[0])

            def evac(tg, dst, cols=4 * P, rows=P, func=ACT.Copy, scale=1.0):
                act.wait_ge(t_done, tg + 1)
                nc.scalar.activation(flat(dst), TB[0:rows, tg % 2, 0:cols], func, scale=scale).then_inc(t_evac, 1)

            def log_gate(g, dst, cols):
                act.wait_ge(g_done, g + 1)
                link(nc.scalar.activation(dst, G[:, g % 2, 0:cols], ACT.Abs))
                link(nc.scalar.activation(dst, dst, ACT.Exp, scale=-1.0))
                nc.scalar.activation(dst, dst, ACT.Ln, bias=1.0).then_inc(act_ready, 1)

            def sum_squares(g, t, h, cols, junk, signal):
                ins = nc.scalar.activation(junk, G[:, g % 2, h * cols:(h + 1) * cols], ACT.Square,
                                           accum_out=ssq[:, t, h:h + 1])
                if signal:
                    ins.then_inc(act_ready, 1)

            def attention(n, g0, tg0, act0):
                for i in range(33):
                    if i < 32:
                        t, h = divmod(i, 16)
                        act.wait_ge(g_read, g0 + i + 1)
                        nc.scalar.activation(probs[:, i % 2, 0:P * (t + 1)], scores[:, i % 2, 0:P * (t + 1)], ACT.Exp,
                                             bias=nmax[:, i % 2:i % 2 + 1], accum_out=rsum[:, t, h:h + 1]) \
                            .then_inc(act_ready, 1)
                    if i >= 1:
                        t = (i - 1) // 16
                        evac(tg0 + i - 1, pbT[:, (i - 1) % 2, 0:t + 1, :], P * (t + 1))

            def rounder(n, past, third_free):
                def piece(j, c, q):
                    if q < 4:
                        w = n.w + j
                        act.wait_ge(wide_full[w % RW], ring_count((c - j) + past, w, RW, NEED_WIDE))
                        raw = wide[w % RW][:, q * 1024:(q + 1) * 1024]
                        if q < 3:
                            act.wait_ge(up_used, (c + past) * 3 + (3 * n.d - 2 + q)) if j or n.d else None
                        else:
                            third_free(j, c)
                    else:
                        d = n.d + j
                        act.wait_ge(down_full[d % RD], ring_count((c - j) + past, d, RD, 16))
                        raw = down[d % RD][:, (q - 4) * 1024:(q - 3) * 1024]
                        if n.d or j:
                            act.wait_ge(down_used if q == 5 else down0_used, (c + past) + n.d)
                    nc.scalar.activation(w_hi[q][:, :], raw, ACT.Copy).then_inc(hi_ready, 1)

                return piece

            def run_packed(n, i):
                past = i * PAIR
                g0 = i * G_PAIR + n.g

                def third_free(j, c):
                    act.wait_ge(g_done, g0 + (g_unit(j - 1) + 1 if j else 0))

                piece = rounder(n, past, third_free)

                def prepare(e):
                    for half in range(2):
                        g = g_prep(e) + 1 + half
                        act.wait_ge(g_done, g0 + (g + 1))
                        at = e * 1024 + half * 512
                        nc.scalar.activation(uh[:, at:at + 512], G[:, (n.g + g) % 2, :], ACT.Copy).then_inc(act_ready, 1)

                def outputs(e, c):
                    act.wait_ge(down_used, past + (n.d + c + 1))
                    if e:
                        act.wait_ge(scat_done, i * 4 + 2)
                    nc.scalar.activation(packed_out, A[:, 2 * e:2 * e + 2, :].rearrange("p h c -> p (h c)"), ACT.Copy) \
                        .then_inc(act_ready, 1)

                piece(0, 0, 0)
                piece(0, 0, 1)
                prepare(0)
                for c in range(PAIR):
                    piece(c, c, 2)
                    piece(c, c, 3)
                    if c:
                        piece(c - 1, c - 1, 4)
                        piece(c - 1, c - 1, 5)
                    if c < PAIR - 1:
                        piece(c + 1, c + 1, 0)
                        piece(c + 1, c + 1, 1)
                    act.wait_ge(g_done, g0 + (g_unit(c) + 1))
                    nc.scalar.activation(sgt[:, 0, :], G[:, (n.g + g_unit(c)) % 2, 0:FU], ACT.Silu).then_inc(act_ready, 1)
                    act.wait_ge(t_done, past + (c + n.tg + 1))
                    nc.scalar.activation(hth[:, 0:2 * P], TB[:, (n.tg + c) % 2, 0:2 * P], ACT.Copy).then_inc(act_ready, 1)
                    if c == PREP_AT:
                        prepare(1)
                    if c == NU:
                        outputs(0, NU - 1)
                piece(PAIR - 1, PAIR - 1, 4)
                piece(PAIR - 1, PAIR - 1, 5)
                outputs(1, PAIR - 1)

            def run(n, units, walk, past):
                piece = rounder(n, past, lambda j, c: act.wait_ge(g_done, (c + past) * 2 + n.g))

                def step(j, c):
                    if j == 0:
                        piece(0, c, 0)
                        piece(0, c, 1)
                    piece(j, c, 2)
                    piece(j, c, 3)
                    if j:
                        piece(j - 1, c - 1, 4)
                        piece(j - 1, c - 1, 5)
                    if j < units - 1:
                        piece(j + 1, c + 1, 0)
                        piece(j + 1, c + 1, 1)
                    for t in range(T):
                        act.wait_ge(g_done, (c + past) * 2 + (n.g + t + 1))
                        nc.scalar.activation(sgt[:, t, :], G[:, t, 0:FU], ACT.Silu).then_inc(act_ready, 1)
                    act.wait_ge(t_done, (c + past) + (n.tg + 1))
                    nc.scalar.activation(hth[:, :], TB[:, (n.tg + j) % 2, :], ACT.Copy).then_inc(act_ready, 1)

                walk(act, units, step)
                piece(units - 1, units - 1, 4)
                piece(units - 1, units - 1, 5)

            for kind, arg, n, before in steps:
                if kind == "start":
                    act.wait_ge(s_c, 16)
                    nc.scalar.activation(condT, cT, ACT.Silu).then_inc(act_ready, 1)
                elif kind == "trs8":
                    for j in range(4):
                        tg = n.tg + j
                        act.wait_ge(t_done, tg + 1)
                        nc.scalar.activation(uh[:, j * 512:(j + 1) * 512], TB[:, tg % 2, :], ACT.Copy) \
                            .then_inc(act_ready, 1)
                elif kind in ("tr8", "tr16"):
                    for j in range(int(kind[2:]) // 2):
                        evac(n.tg + j, uT[:, 2 * j:2 * j + 2, :])
                elif kind == "gla":
                    evac(n.tg, glowT[0:RANK, :], S, RANK)
                    for t in range(T):
                        log_gate(n.g + 12 + t, lsg[:, t, :], KW)
                    evac(n.tg + 1, small[:, 52:60], 8, P, ACT.Exp)
                    act.wait_ge(dve_ready, n.dve + 3)
                    for t in range(T):
                        g = n.g + 16 + t
                        act.wait_ge(g_done, g + 1)
                        nc.scalar.activation(e3[:, t, 0:2 * KW], G[:, g % 2, 0:2 * KW], ACT.Exp)
                        nc.scalar.activation(e3[:, t, 2 * KW:3 * KW], G[:, g % 2, 0:KW], ACT.Exp, scale=-1.0) \
                            .then_inc(act_ready, 1)
                    evac(n.tg + 2, gqT)
                    evac(n.tg + 3, gkT)
                    for t in range(T):
                        act.wait_ge(g_read, n.g + 16)
                        nc.scalar.activation(proj[:, t, C_H:C_H + VW], proj[:, t, C_G:C_G + VW], ACT.Silu) \
                            .then_inc(act_ready, 1)
                    for t in range(T):
                        g = n.g + 20 + t
                        act.wait_ge(g_done, g + 1)
                        for h in range(HEADS):
                            sum_squares(g, t, h, DV, hbuf[:, t * VW + h * DV:t * VW + (h + 1) * DV], h == HEADS - 1)
                elif kind == "ffn":
                    run(n, NU, roll, 0)
                elif kind == "moe":
                    act.wait_ge(dve_ready, n.dve)
                    full = act.value_load(crowded[0:1, 0:1], min_val=0, max_val=1)
                    with act.If(full == 0):
                        with act.Fori(0, EXPERTS // 2) as i:
                            run_packed(n, i)
                        act.drain().then_inc(act_ready, 3 * NU * EXPERTS - ACT_PAIR * (EXPERTS // 2))
                    with act.Else():
                        with act.Fori(0, EXPERTS // 2) as i:
                            run(n, PAIR, straight, i * PAIR)
                elif kind == "router":
                    act.wait_ge(dve_ready, n.dve + 1)
                    nc.scalar.activation(e2, gap, ACT.Exp).then_inc(act_ready, 1)
                elif kind == "kvdown":
                    for t in range(T):
                        act.wait_ge(g_done, n.g + t + 1)
                        sum_squares(n.g + t, t, 0, KVLORA, sg[:, t * KVLORA:(t + 1) * KVLORA], True)
                    evac(n.tg, ckvT)
                    evac(n.tg + 1, krT, S)
                elif kind == "fox":
                    for t in range(T):
                        log_gate(n.g + 20 + t, flt[:, t, :], FOX_H)
                    evac(n.tg, ncT[0:FOX_H, :], S, FOX_H, ACT.Copy, -1.0)
                    attention(n, n.g + 24, n.tg + 1, n.act + 2)
                elif kind == "mla":
                    for t in range(T):
                        act.wait_ge(g_done, n.g + t + 1)
                        sum_squares(n.g + t, t, 0, QLORA, hbuf[:, t * QLORA:(t + 1) * QLORA], True)
                    evac(n.tg, cqT[:, 0:2, :])
                    evac(n.tg + 1, cqT[:, 2, :], S)
                    for j in range(4):
                        evac(n.tg + 2 + j, qrT[:, 2 * j:2 * j + 2, :])
                    attention(n, n.g + 50, n.tg + 6, n.act + 2)
                elif kind == "ple":
                    evac(n.tg, pT)
                    for t in range(T):
                        act.wait_ge(g_read, n.g + 3 + t)
                        nc.scalar.activation(gt[:, t, :], gt[:, t, :], ACT.Sigmoid).then_inc(act_ready, 1)

        @block.gpsimd
        def _(pool):
            def bc(row):
                return row.partition_broadcast(P)

            def load_ln(s):
                if s < 2 * DEPTH:
                    name = ("ln1", "ln2")[s % 2]
                    rows = I[f"{name}_g"][s // 2], I[f"{name}_b"][s // 2]
                elif s < 6 * DEPTH:
                    i, j = divmod(s - 2 * DEPTH, 4)
                    rows = I["ln_g_2"][i, j], I["ln_b_2"][i, j]
                else:
                    return
                for half, row in enumerate(rows):
                    pool.dma_start(lnp[:, half * D:(half + 1) * D], bc(row)).then_inc(s_ln, 16)

            def load_gla(l):
                pool.dma_start(convw, bc(I["conv_w"][l])).then_inc(s_gla, 16)
                pool.dma_start(gnw, bc(I["gla_norm_w"][l])).then_inc(s_gla, 16)
                pool.dma_start(gkw2[0:RANK, :], I["gk_w2"][l]).then_inc(s_gla, 16)
                pool.dma_start(gkb[0:1, :], I["gk_b"][l:l + 1]).then_inc(s_gla, 16)

            def load_ada(l):
                pool.dma_start(area(BIG, 6 * D), bc(I["ada_b"][l])).then_inc(s_ada, 16)

            def load_ple(i):
                pool.dma_start(bgate, bc(I["ple_b_gate_2"][i])).then_inc(s_ple, 16)
                pool.dma_start(ptok, I["p_2"][i, 0].rearrange("(t p) c -> p t c", p=P)).then_inc(s_ple, 16)

            def root(dve, width):
                a = CONST_COLS["minushalf"][0]
                for t in range(T):
                    pool.wait_ge(dve_ready, dve + t + 1)
                    nc.gpsimd.tensor_tensor(rstd[:, t, 0:width], ve[:, t, 0:width], con[:, a:a + width],
                                            ALU.pow).then_inc(pool_ready, 1)

            load_ada(0)
            load_gla(0)
            load_ln(0)
            pool.dma_start(routw[:, :].rearrange("p (k e) -> p k e", k=KD),
                           I["router_w"][0].rearrange("(k p) e -> p k e", p=P)).then_inc(s_rout, 16)
            pool.wait_ge(s_con, 16)
            for kind, arg, n, _ in steps:
                if kind == "gla":
                    root(n.dve + 4, HEADS)
                elif kind in ("kvdown", "mla"):
                    root(n.dve, 1)
                elif kind == "ln":
                    root(n.dve, 1)
                    pool.wait_ge(src_ready, n.src + 1)
                    load_ln(n.ln + 1)
                    if n.ln == 1:
                        load_gla(1)
                        load_ada(1)
                    if n.ln == 2 * DEPTH - 1:
                        pool.dma_start(qnw, bc(I["mla_q_norm_2"][0])).then_inc(s_attn, 16)
                        pool.dma_start(kvnw, bc(I["kv_norm_2"])).then_inc(s_attn, 16)
                        pool.dma_start(bfrow[0:1, :], I["fox_b_f_2"]).then_inc(s_attn, 16)
                    if n.ln >= 2 * DEPTH and n.ln % 4 == 2:
                        load_ple((n.ln - 2 * DEPTH) // 4)

        @block.vector
        def _(dve):
            V = nc.vector
            step = [0]

            def link(ins):
                step[0] += 1
                ins.then_inc(dve_step, 1)
                dve.wait_ge(dve_step, step[0])

            def copy_out(g, dst, cols, scale=None):
                dve.wait_ge(g_done, g + 1)
                if scale is None:
                    V.tensor_copy(flat(dst), G[:, g % 2, 0:cols]).then_inc(g_read, 1)
                else:
                    V.tensor_scalar(dst, G[:, g % 2, 0:cols], scale, None, ALU.mult).then_inc(g_read, 1)

            def log_sigmoid(g, scratch, cols, a):
                dve.wait_ge(act_ready, a)
                V.scalar_tensor_tensor(out=scratch, in0=G[:, g % 2, 0:cols], scalar=0.0, in1=scratch,
                                       op0=ALU.min, op1=ALU.subtract).then_inc(g_read, 1)
                dve.wait_ge(g_read, g + 1)

            def mean_eps(t, width, size, a):
                dve.wait_ge(act_ready, a)
                V.tensor_scalar(ve[:, t, 0:width], ssq[:, t, 0:width], 1.0 / size, RMS_EPS,
                                ALU.mult, ALU.add).then_inc(dve_ready, 1)

            def rope(dst, lo, hi, cos, sin, t1):
                half = ROPE // 2
                link(V.tensor_tensor(t1, hi, sin, ALU.mult))
                link(V.tensor_tensor(dst[0], lo, cos, ALU.mult))
                link(V.tensor_tensor(dst[0], dst[0], t1, ALU.subtract))
                link(V.tensor_tensor(t1, lo, sin, ALU.mult))
                link(V.tensor_tensor(dst[1], hi, cos, ALU.mult))
                return V.tensor_tensor(dst[1], dst[1], t1, ALU.add)

            def attention(n, g0, fox):
                for i in range(32):
                    t, h = divmod(i, 16)
                    g, cols = g0 + i, P * (t + 1)
                    dve.wait_ge(g_done, g + 1)
                    sc = scores[:, i % 2, 0:cols]
                    if i >= 2:
                        dve.wait_ge(act_ready, n.act + 2 + i - 1)
                    if fox:
                        scalar, op = cumf[:, t, h:h + 1], ALU.add
                    else:
                        scalar, op = float((NOPE + ROPE) ** -0.5), ALU.mult
                    if t:
                        link(V.tensor_scalar(sc[:, 0:P], G[:, g % 2, 0:P], scalar, None, op))
                    link(V.scalar_tensor_tensor(out=sc[:, t * P:cols], in0=G[:, g % 2, t * P:cols], scalar=scalar,
                                                in1=C("causal"), op0=op, op1=ALU.add))
                    V.tensor_reduce(nmax[:, i % 2:i % 2 + 1], sc, AX.X, ALU.max, negate=True).then_inc(g_read, 1)
                    if i == 31:
                        weighted(n, 1, fox)
                    elif i == 17 and not fox:
                        weighted(n, 0, fox)

            def weighted(n, t, fox):
                dve.wait_ge(acc_done, n.acc + (1 if fox or t == 0 else 2))
                dve.wait_ge(act_ready, n.act + 2 + 16 * (t + 1))
                if fox:
                    link(V.reciprocal(rinv[:, :, :], rsum[:, :, :]))
                    for b in range(4):
                        tt, half = divmod(b, 2)
                        last = V.tensor_tensor(
                            src[:, tt, half * 512:(half + 1) * 512].rearrange("p (h d) -> p h d", h=8),
                            A[:, b, :].rearrange("p (h d) -> p h d", h=8),
                            rinv[:, tt, half * 8:half * 8 + 8].unsqueeze(2).to_broadcast([P, 8, FOX_D]), ALU.mult)
                    last.then_inc(acc_free, 1)
                    dve.wait_ge(acc_free, n.free + 1)
                else:
                    link(V.reciprocal(rinv[:, t, :], rsum[:, t, :]))
                    for b in range(4):
                        last = V.tensor_tensor(
                            src2[:, t, b * 512:(b + 1) * 512].rearrange("p (h d) -> p h d", h=4),
                            A[:, b, :].rearrange("p (h d) -> p h d", h=4),
                            rinv[:, t, b * 4:b * 4 + 4].unsqueeze(2).to_broadcast([P, 4, VH]), ALU.mult)
                    last.then_inc(acc_free, 1)
                    dve.wait_ge(acc_free, n.free + 1 + t)

            def resters(n, units, past):
                def piece(j, c, q):
                    if q < 4:
                        raw = wide[(n.w + j) % RW][:, q * 1024:(q + 1) * 1024]
                        count = up_pieces(c, q)
                    else:
                        raw = down[(n.d + j) % RD][:, (q - 4) * 1024:(q - 3) * 1024]
                        count = down_pieces(c, q - 4, units)
                    dve.wait_ge(hi_ready, past * 6 + count + n.lo)
                    V.tensor_tensor(w_lo[q][:, :], raw, w_hi[q][:, :].bitcast(F32), ALU.subtract).then_inc(lo_ready, 1)

                return piece

            def run_packed(n, i):
                past = i * PAIR
                g0, a0 = i * G_PAIR + n.g, i * ACT_PAIR + n.act
                piece = resters(n, PAIR, past)

                def one_hots(e):
                    col = bass.ds(i * 2 + e, 1)
                    for t in range(T):
                        V.tensor_scalar(pick[:, t, :], C("slots"), slotid[:, t, col], None, ALU.is_equal)
                        last = V.tensor_scalar(pick_w[:, t, :], C("slots"), slotid[:, t, col], route[:, t, col],
                                               ALU.is_equal, ALU.mult)
                    last.then_inc(pick_ready, 1)

                def prepare(e):
                    g = g_prep(e)
                    dve.wait_ge(g_done, g0 + (g + 1))
                    V.tensor_copy(put_back[:, e, :], G[:, (n.g + g) % 2, 0:2 * P]).then_inc(g_read, 1)
                    for half in range(2):
                        dve.wait_ge(act_ready, a0 + a_prep(e, half))
                        at = e * 1024 + half * 512
                        V.tensor_tensor(ul[:, at:at + 512], G[:, (n.g + g + 1 + half) % 2, :],
                                        uh[:, at:at + 512].bitcast(F32), ALU.subtract).then_inc(g_read, 1)

                def add(t, k, banks):
                    dve.wait_ge(scat_done, i * 4 + k)
                    V.tensor_tensor(moe_sum[:, t, :], moe_sum[:, t, :],
                                    A[:, banks:banks + 2, :].rearrange("p h c -> p (h c)"), ALU.add) \
                        .then_inc(acc_free if t else scat_read, 1)

                dve.wait_ge(acc_free, i * 2 + n.free)
                one_hots(0)
                piece(0, 0, 0)
                piece(0, 0, 1)
                prepare(0)
                for c in range(PAIR):
                    piece(c, c, 2)
                    piece(c, c, 3)
                    if c:
                        piece(c - 1, c - 1, 4)
                        piece(c - 1, c - 1, 5)
                    if c < PAIR - 1:
                        piece(c + 1, c + 1, 0)
                        piece(c + 1, c + 1, 1)
                    dve.wait_ge(act_ready, a0 + a_silu(c))
                    V.tensor_tensor(hid[:, 0, 0, :], sgt[:, 0, :], G[:, (n.g + g_unit(c)) % 2, FU:2 * FU], ALU.mult) \
                        .then_inc(g_read, 1)
                    dve.wait_ge(act_ready, a0 + (a_silu(c) + 1))
                    V.tensor_tensor(htl[:, 0:2 * P], TB[:, (n.tg + c) % 2, 0:2 * P], hth[:, 0:2 * P].bitcast(F32),
                                    ALU.subtract).then_inc(t_evac, 1)
                    if c == PREP_AT - 1:
                        one_hots(1)
                    if c == PREP_AT:
                        prepare(1)
                    if c == NU + 1:
                        add(0, 1, 0)
                    if c == NU + 2:
                        add(1, 2, 0)
                piece(PAIR - 1, PAIR - 1, 4)
                piece(PAIR - 1, PAIR - 1, 5)
                dve.wait_ge(scat_read, i * 2 + 1)
                add(0, 3, 2)
                dve.wait_ge(acc_free, i * 2 + (n.free + 1))
                add(1, 4, 0)

            def run(n, units, walk, past, route_of, drain_after, drained):
                piece = resters(n, units, past)

                def step(j, c):
                    if j == 0:
                        piece(0, c, 0)
                        piece(0, c, 1)
                    piece(j, c, 2)
                    piece(j, c, 3)
                    if j:
                        piece(j - 1, c - 1, 4)
                        piece(j - 1, c - 1, 5)
                    if j < units - 1:
                        piece(j + 1, c + 1, 0)
                        piece(j + 1, c + 1, 1)
                    for t in range(T):
                        dve.wait_ge(act_ready, (c + past) * 3 + (n.act + t + 1))
                        if route_of:
                            ins = V.scalar_tensor_tensor(out=hid[:, 0, t, :], in0=sgt[:, t, :], scalar=route_of(j, t),
                                                         in1=G[:, t, FU:2 * FU], op0=ALU.mult, op1=ALU.mult)
                        else:
                            ins = V.tensor_tensor(hid[:, 0, t, :], sgt[:, t, :], G[:, t, FU:2 * FU], ALU.mult)
                        ins.then_inc(g_read, 1)
                    dve.wait_ge(act_ready, (c + past) * 3 + (n.act + 3))
                    V.tensor_tensor(htl[:, :], TB[:, (n.tg + j) % 2, :], hth[:, :].bitcast(F32), ALU.subtract) \
                        .then_inc(t_evac, 1)
                    if j - 1 in drain_after:
                        drain(j - 1, c - 1)

                def drain(j, c):
                    dve.wait_ge(down_used, (c + past) + (n.d + 1))
                    dve.wait_ge(acc_free, drained(j))
                    for t in range(T):
                        acc = A[:, 2 * t:2 * t + 2, :].rearrange("p h c -> p (h c)")
                        last = V.tensor_tensor(moe_sum[:, t, :], moe_sum[:, t, :], acc, ALU.add)
                    last.then_inc(acc_free, 1)

                walk(dve, units, step)
                piece(units - 1, units - 1, 4)
                piece(units - 1, units - 1, 5)
                if units - 1 in drain_after:
                    drain(units - 1, units - 1)

            for kind, arg, n, before in steps:
                if kind == "start":
                    dve.wait_ge(s_con, 16)
                    dve.wait_ge(act_ready, 1)
                    V.tensor_copy(condB, condT.unsqueeze(2).to_broadcast([P, KD, P])).then_inc(dve_ready, 1)
                    dve.wait_ge(s_x, 16)
                elif kind == "ada":
                    if arg:
                        V.tensor_copy(condB, condT.unsqueeze(2).to_broadcast([P, KD, P])).then_inc(cond_again, 1)
                    dve.wait_ge(s_ada, 16 * (arg + 1))
                    for c in range(12):
                        g = n.g + c
                        dst = mod[:, c // 2, (c % 2) * 512:(c % 2 + 1) * 512]
                        dve.wait_ge(g_done, g + 1)
                        V.tensor_tensor(dst, G[:, g % 2, :], dst, ALU.add).then_inc(g_read, 1)
                    dve.wait_ge(g_read, n.g + 12)
                elif kind == "mod":
                    for t in range(T):
                        link(V.scalar_tensor_tensor(out=src[:, t, :], in0=mod[:, arg + 1, :], scalar=1.0, in1=x[:, t, :],
                                                    op0=ALU.add, op1=ALU.mult))
                        last = V.tensor_tensor(src[:, t, :], src[:, t, :], mod[:, arg, :], ALU.add)
                    last.then_inc(src_ready, 1)
                elif kind == "gla":
                    for c in range(6):
                        for t in range(T):
                            copy_out(n.g + 2 * c + t, proj[:, t, c * 512:(c + 1) * 512], 512)
                    dve.wait_ge(g_read, n.g + 12)
                    dve.wait_ge(s_gla, 64 * (arg + 1))
                    for t in range(T):
                        zc = proj[:, t, C_C:C_C + CONV]
                        link(V.tensor_tensor(zc, zc, proj[:, t, C_H:C_H + CONV], ALU.mult))
                        link(V.tensor_tensor(proj[:, t, C_H:C_H + CONV], zc, convw[:, 0, :], ALU.mult))
                        link(V.tensor_tensor(z1[:, t, :], zc, convw[:, 1, :], ALU.mult))
                        last = V.tensor_tensor(zc, zc, convw[:, 2, :], ALU.mult)
                    last.then_inc(dve_ready, 1)
                    for t in range(T):
                        log_sigmoid(n.g + 12 + t, lsg[:, t, :], KW, n.act + 1 + t)
                        V.tensor_scalar(gk[:, t, :], lsg[:, t, :], 1.0 / 16.0, -1.0, ALU.mult, ALU.max) \
                            .then_inc(dve_ready, 1)
                    for t in range(T):
                        g = n.g + 14 + t
                        dve.wait_ge(g_done, g + 1)
                        V.tensor_tensor(src[:, t, 0:CONV], G[:, g % 2, :], proj[:, t, C_B:C_B + CONV], ALU.mult) \
                            .then_inc(g_read, 1)
                    for t in range(T):
                        g = n.g + 16 + t
                        dve.wait_ge(act_ready, n.act + 3 + t)
                        q, k = proj[:, t, C_Q:C_Q + KW], proj[:, t, C_K:C_K + KW]
                        V.scalar_tensor_tensor(out=q, in0=q, scalar=DK ** -0.5, in1=e3[:, t, 0:KW],
                                               op0=ALU.mult, op1=ALU.mult)
                        link(V.tensor_tensor(proj[:, t, C_C:C_C + KW], k, e3[:, t, 2 * KW:3 * KW], ALU.mult))
                        V.tensor_tensor(k, k, e3[:, t, KW:2 * KW], ALU.mult).then_inc(g_read, 1)
                    dve.wait_ge(g_read, n.g + 18)
                    link(V.memset(state, 0.0))
                    dve.wait_ge(acc_done, n.acc + 1)
                    dve.wait_ge(t_evac, n.tg + 2)
                    for c in range(3):
                        for f in range(2):
                            r = slice(DK * f, DK * f + DK)
                            for a in range(2):
                                kv = A[r, c, a * KW + f * DV:a * KW + (f + 1) * DV]
                                if c == 0:
                                    last = V.tensor_copy(state[r, 0, a, f * DV:(f + 1) * DV], kv)
                                else:
                                    last = V.scalar_tensor_tensor(out=state[r, c, a, f * DV:(f + 1) * DV],
                                                                  in0=state[r, c - 1, a, f * DV:(f + 1) * DV],
                                                                  scalar=dec[r, c // 2, a, c % 2:c % 2 + 1], in1=kv,
                                                                  op0=ALU.mult, op1=ALU.add)
                        if c < 2:
                            link(last)
                    last.then_inc(dve_ready, 1)
                    V.tensor_copy(ve[0:1, 0, 0:1], A[0:1, 0, 0:1]).then_inc(acc_free, 1)
                    for f in range(2):
                        g = n.g + 18 + f
                        dve.wait_ge(g_done, g + 1)
                        V.tensor_tensor(stm[:, f], G[:, g % 2, :].rearrange("p (h i) -> p h i", h=HEADS),
                                        C("cum").unsqueeze(1).to_broadcast([P, HEADS, P]), ALU.mult).then_inc(g_read, 1)
                    dve.wait_ge(acc_free, n.free + 1)
                    for t in range(T):
                        mean_eps(t, HEADS, DV, n.act + 7 + t)
                    for t in range(T):
                        g = n.g + 20 + t
                        dve.wait_ge(pool_ready, n.pool + t + 1)
                        y = src[:, t, CONV:CONV + VW]
                        for h in range(HEADS):
                            last = V.scalar_tensor_tensor(out=y[:, h * DV:(h + 1) * DV], in0=G[:, g % 2, h * DV:(h + 1) * DV],
                                                          scalar=rstd[:, t, h:h + 1], in1=gnw, op0=ALU.mult, op1=ALU.mult)
                        last.then_inc(g_read, 1)
                        dve.wait_ge(g_read, g + 1)
                        last = V.tensor_tensor(y, y, proj[:, t, C_H:C_H + VW], ALU.mult)
                    last.then_inc(src_ready, 1)
                elif kind == "ln":
                    how, which = arg
                    if before == "moe":
                        dve.wait_ge(acc_free, n.free)
                    elif before == "ffn":
                        dve.wait_ge(down_used, n.d)
                    else:
                        dve.wait_ge(acc_done, n.acc)
                    for t in range(T):
                        acc = A[:, 2 * t:2 * t + 2, :].rearrange("p h c -> p (h c)")
                        if before == "moe":
                            acc = moe_sum[:, t, :]
                        xt = x[:, t, :]
                        if how in ("mod", "gate"):
                            delta = src[:, t, :]
                            if how == "mod":
                                link(V.scalar_tensor_tensor(out=delta, in0=mod[:, which, :], scalar=1.0, in1=acc,
                                                            op0=ALU.add, op1=ALU.mult))
                            else:
                                dve.wait_ge(act_ready, n.act - 1 + t)
                                link(V.tensor_tensor(delta, gt[:, t, :], acc, ALU.mult))
                            link(V.scalar_tensor_tensor(out=xt, in0=xt, scalar=ALPHA, in1=delta, op0=ALU.mult, op1=ALU.add))
                        elif how == "half":
                            link(V.tensor_scalar(xt, xt, ALPHA, None, ALU.mult))
                            link(V.scalar_tensor_tensor(out=xt, in0=acc, scalar=0.5, in1=xt, op0=ALU.mult, op1=ALU.add))
                        else:
                            link(V.scalar_tensor_tensor(out=xt, in0=xt, scalar=ALPHA, in1=acc, op0=ALU.mult, op1=ALU.add))
                        for half in range(2):
                            last = V.bn_stats(stats[:, t, half, :], x[:, t, half * 512:(half + 1) * 512])
                        link(last)
                        link(V.bn_aggr(mv[:, t, :], stats[:, t].rearrange("p c s -> p (c s)")))
                        V.tensor_scalar(ve[:, t, 0:1], mv[:, t, 1:2], LN_EPS, None, ALU.add).then_inc(dve_ready, 1)
                    V.tensor_copy(nmax[0:1, 0:1], mv[0:1, 0, 0:1]).then_inc(acc_free, 1)
                    dve.wait_ge(s_ln, 32 * (n.ln + 1))
                    for t in range(T):
                        xt = x[:, t, :]
                        link(V.scalar_tensor_tensor(out=xt, in0=xt, scalar=mv[:, t, 0:1], in1=lnp[:, 0:D],
                                                    op0=ALU.subtract, op1=ALU.mult))
                        dve.wait_ge(pool_ready, n.pool + t + 1)
                        last = V.scalar_tensor_tensor(out=xt, in0=xt, scalar=rstd[:, t, 0:1], in1=lnp[:, D:2 * D],
                                                      op0=ALU.mult, op1=ALU.add)
                    last.then_inc(src_ready, 1)
                    dve.wait_ge(src_ready, n.src + 1)
                elif kind == "ffn":
                    run(n, NU, roll, 0, None, (), None)
                elif kind == "moe":
                    link(V.memset(moe_sum, 0.0))
                    dve.wait_ge(dve_ready, n.dve)
                    full = dve.value_load(crowded[0:1, 0:1], min_val=0, max_val=1)
                    with dve.If(full == 0):
                        with dve.Fori(0, EXPERTS // 2) as i:
                            run_packed(n, i)
                        dve.drain().then_inc(g_read, 2 * NU * EXPERTS - G_PAIR * (EXPERTS // 2))
                    with dve.Else():
                      with dve.Fori(0, EXPERTS // 2) as i:
                        run(n, PAIR, straight, i * PAIR, lambda j, t: route[:, t, bass.ds(i * 2 + j // NU, 1)],
                            (NU - 1, PAIR - 1), lambda j: i * 2 + (n.free + j // NU))
                elif kind == "trs8":
                    for j in range(4):
                        dve.wait_ge(act_ready, n.act + j + 1)
                        V.tensor_tensor(ul[:, j * 512:(j + 1) * 512], TB[:, (n.tg + j) % 2, :],
                                        uh[:, j * 512:(j + 1) * 512].bitcast(F32), ALU.subtract).then_inc(t_evac, 1)
                elif kind == "router":
                    for t in range(T):
                        copy_out(n.g + t, logit[:, t, :], EXPERTS)
                    dve.wait_ge(g_read, n.g + 2)
                    for t in range(T):
                        link(V.max(top8[:, t, :], logit[:, t, :]))
                        link(V.max_index(idx8[:, t * 8:(t + 1) * 8], top8[:, t, :], logit[:, t, :]))
                        link(V.tensor_copy(idxf[:, t, :], idx8[:, t * 8:(t + 1) * 8]))
                        last = V.tensor_tensor(gap[:, t:t + 1], top8[:, t, 1:2], top8[:, t, 0:1], ALU.subtract)
                    last.then_inc(dve_ready, 1)
                    dve.wait_ge(act_ready, n.act + 1)
                    link(V.tensor_scalar(w1, e2, 1.0, None, ALU.add))
                    link(V.reciprocal(w1, w1))
                    link(V.tensor_tensor(w2, e2, w1, ALU.mult))
                    for t in range(T):
                        link(V.tensor_scalar(rtmp[:, t, :], C("experts"), idxf[:, t, 1:2], None, ALU.is_equal))
                        link(V.scalar_tensor_tensor(out=member[:, t, :], in0=C("experts"), scalar=idxf[:, t, 0:1],
                                                    in1=rtmp[:, t, :], op0=ALU.is_equal, op1=ALU.add))
                    V.tensor_copy(nmax[0:1, 0:1], w1[0:1, 0:1]).then_inc(dve_ready, 1)
                    for t in range(T):
                        link(V.tensor_scalar(rtmp[:, t, :], C("experts"), idxf[:, t, 0:1], w1[:, t:t + 1],
                                             ALU.is_equal, ALU.mult))
                        link(V.tensor_scalar(route[:, t, :], C("experts"), idxf[:, t, 1:2], w2[:, t:t + 1],
                                             ALU.is_equal, ALU.mult))
                        link(V.tensor_tensor(route[:, t, :], route[:, t, :], rtmp[:, t, :], ALU.add))
                    for t in range(T):
                        g = n.g + 2 + t
                        dve.wait_ge(g_done, g + 1)
                        link(V.tensor_tensor(slotid[:, t, :], G[:, g % 2, 0:EXPERTS], member[:, t, :], ALU.mult))
                        if t:
                            link(V.tensor_reduce(gap[:, 0:1], G[:, g % 2, EXPERTS:2 * EXPERTS], AX.X, ALU.max))
                        link(V.tensor_scalar(slotid[:, t, :], slotid[:, t, :], -1.0, None, ALU.add))
                        V.tensor_copy(nmax[0:1, 0:1], G[0:1, g % 2, 0:1]).then_inc(g_read, 1)
                    V.tensor_scalar(crowded[:, :], gap[:, 0:1], float(P), None, ALU.is_gt).then_inc(dve_ready, 1)
                elif kind == "kvdown":
                    dve.wait_ge(s_attn, 48)
                    for t in range(T):
                        mean_eps(t, 1, KVLORA, n.act + 1 + t)
                    half = ROPE // 2
                    for t in range(T):
                        g = n.g + t
                        cos = C("cos").rearrange("p (t c) -> p t c", t=T)[:, t, :]
                        sin = C("sin").rearrange("p (t c) -> p t c", t=T)[:, t, :]
                        link(rope((krd[:, t, 0:half], krd[:, t, half:ROPE]), G[:, g % 2, KVLORA:KVLORA + half],
                                  G[:, g % 2, KVLORA + half:KVLORA + ROPE], cos, sin, rinv[:, :, :].rearrange("p a b -> p (a b)")))
                        link(V.tensor_copy(krd[:, t, ROPE:2 * ROPE], krd[:, t, 0:ROPE]))
                        dve.wait_ge(pool_ready, n.pool + t + 1)
                        V.scalar_tensor_tensor(out=ckv[:, t, :], in0=G[:, g % 2, 0:KVLORA], scalar=rstd[:, t, 0:1], in1=kvnw,
                                               op0=ALU.mult, op1=ALU.mult).then_inc(g_read, 1)
                    V.tensor_copy(nmax[0:1, 0:1], rstd[0:1, 0, 0:1]).then_inc(dve_ready, 1)
                elif kind == "fox":
                    for c in range(4):
                        for f in range(4):
                            dst = fqT if c < 2 else fkT
                            copy_out(n.g + 4 * c + f, dst[:, 4 * (c % 2) + f, :], S, FOX_D ** -0.5 if c < 2 else None)
                    for c in range(2):
                        for t in range(T):
                            copy_out(n.g + 16 + 2 * c + t, fv[:, t, c * 512:(c + 1) * 512], 512)
                    for t in range(T):
                        log_sigmoid(n.g + 20 + t, flt[:, t, :], FOX_H, n.act + 1 + t)
                        V.tensor_copy(fls[:, t, :], flt[:, t, :]).then_inc(dve_ready, 1)
                    for t in range(T):
                        copy_out(n.g + 22 + t, cumf[:, t, :], FOX_H)
                    dve.wait_ge(g_read, n.g + 24)
                    attention(n, n.g + 24, True)
                    V.tensor_copy(nmax[0:1, 0:1], rinv[0:1, 0, 0:1]).then_inc(src_ready, 1)
                elif kind == "mla":
                    for t in range(T):
                        mean_eps(t, 1, QLORA, n.act + 1 + t)
                    for t in range(T):
                        g = n.g + t
                        dve.wait_ge(pool_ready, n.pool + t + 1)
                        V.scalar_tensor_tensor(out=cq[:, t, :], in0=G[:, g % 2, 0:QLORA], scalar=rstd[:, t, 0:1], in1=qnw,
                                               op0=ALU.mult, op1=ALU.mult).then_inc(g_read, 1)
                    for c in range(4):
                        g = n.g + 2 + 6 * c
                        for h in range(4):
                            copy_out(g + h, qnT[:, 4 * c + h, :], S)
                        for t in range(T):
                            copy_out(g + 4 + t, qr_raw[:, t, 4 * c:4 * c + 4, :], 4 * ROPE)
                    dve.wait_ge(g_read, n.g + 26)
                    half = ROPE // 2
                    for t in range(T):
                        cos = C("cos").rearrange("p (t c) -> p t c", t=T)[:, t:t + 1, :].to_broadcast([P, MLA_H, half])
                        sin = C("sin").rearrange("p (t c) -> p t c", t=T)[:, t:t + 1, :].to_broadcast([P, MLA_H, half])
                        link(rope((qr_rot[:, t, :, 0:half], qr_rot[:, t, :, half:ROPE]), qr_raw[:, t, :, 0:half],
                                  qr_raw[:, t, :, half:ROPE], cos, sin, ropetmp))
                    V.tensor_copy(nmax[0:1, 0:1], rstd[0:1, 0, 0:1]).then_inc(dve_ready, 1)
                    for c in range(2):
                        g = n.g + 26 + 12 * c
                        for h in range(8):
                            copy_out(g + h, knT[:, 8 * c + h, :], S)
                        for q in range(2):
                            for t in range(T):
                                copy_out(g + 8 + 2 * q + t, vtok[:, t, (2 * c + q) * 512:(2 * c + q + 1) * 512], 512)
                    dve.wait_ge(g_read, n.g + 50)
                    attention(n, n.g + 50, False)
                    V.tensor_copy(nmax[0:1, 0:1], rinv[0:1, 0, 0:1]).then_inc(src_ready, 1)
                elif kind == "ple":
                    dve.wait_ge(s_ple, 32 * (arg + 1))
                    for c in range(2):
                        for t in range(T):
                            g = n.g + 2 * c + t
                            dve.wait_ge(g_done, g + 1)
                            V.tensor_tensor(gt[:, t, c * 512:(c + 1) * 512], G[:, g % 2, :], bgate[:, c * 512:(c + 1) * 512],
                                            ALU.add).then_inc(g_read, 1)


NAMES = ["x", "c", "ada_w", "ada_b", "w_in", "conv_w", "gk_w2", "gk_b", "gla_norm_w", "w_out", "ln1_g", "ln1_b",
         "ln2_g", "ln2_b", "ffn_w_gate", "ffn_w_up", "ffn_w_down", "router_w", "moe_w_gate", "moe_w_up",
         "moe_w_down", "p_2", "ffn1_w_in_2", "ffn1_w_out_2", "ffn2_w_in_2", "ffn2_w_out_2", "ln_g_2", "ln_b_2",
         "ple_w_gate_2", "ple_b_gate_2", "ple_w_proj_2", "fox_w_in_2", "fox_b_f_2", "fox_w_o_2", "mla_w_dq_2",
         "mla_q_norm_2", "mla_w_uq_2", "mla_w_o_2", "kv_w_down_2", "kv_norm_2", "kv_w_up_2"]


def kernel(**inputs):
    import concourse.bacc as bacc
    from concourse.bass_utils import run_bass_kernel_spmd

    nc = bacc.Bacc("TRN2", target_bir_lowering=False, num_devices=1)
    arrays, aps = {}, {}
    for name in NAMES:
        a = np.ascontiguousarray(inputs[name])
        arrays[f"in_{name}"] = a
        aps[name] = nc.dram_tensor(f"in_{name}", a.shape, mybir.dt.from_np(a.dtype), kind="ExternalInput").ap()
    arrays["in_con"] = constants()
    aps["con"] = nc.dram_tensor("in_con", (P, NCONST), F32, kind="ExternalInput").ap()
    out = nc.dram_tensor("out_x", (1, S, D), F32, kind="ExternalOutput").ap()
    build(nc, aps, out)
    r = run_bass_kernel_spmd(nc, [arrays], core_ids=[0])
    return r.results[0]["out_x"]
```

```python
from contextlib import ExitStack

import numpy as np

import concourse.bass as bass
from concourse import mybir

F32 = mybir.dt.float32
F32R = mybir.dt.float32r
U32 = mybir.dt.uint32
ALU = mybir.AluOpType
ACT = mybir.ActivationFunctionType
AX = mybir.AxisListType

P = 128
S = 256
T = S // P
D = 1024
KD = D // P
DEPTH = 2
CONV = 512
WIDTH = 3
HEADS = 4
DK = 64
DV = 128
CHUNK = 64
KW = HEADS * DK
VW = HEADS * DV
RANK = 16
C_B, C_C, C_H = 0, CONV, 2 * CONV
C_Q = 3 * CONV
C_K = C_Q + KW
C_V = C_K + KW
C_G = C_V + VW
C_LOW = C_G + VW
FF = 2816
FU = 256
NU = FF // FU
EXPERTS = 8
ALPHA = (2.0 * DEPTH) ** 0.25
LN_EPS = 1e-5
RMS_EPS = 1e-6
FOX_H = 16
FOX_D = 64
MLA_H = 16
NOPE = 128
ROPE = 64
VH = 128
QLORA = 384
KVLORA = 256
THETA = 10000.0
MASKED = -1e30

RW = 2
RD = 2
WSLOT = 4096
DSLOT = 2048
PAIR = 2 * NU
NEED_WIDE = 16

CONST_COLS = {}
_col = 0
for _name, _w in (("ident", P), ("shift1", P), ("shift2", P), ("cross1", P), ("cross2", P), ("cum", P),
                  ("suffix", P), ("tri", P), ("ones", P), ("causal", P), ("slots", P), ("chunks", 2), ("experts", EXPERTS),
                  ("cos", T * ROPE // 2), ("sin", T * ROPE // 2), ("minushalf", T * HEADS)):
    CONST_COLS[_name] = (_col, _col + _w)
    _col += _w
NCONST = _col


def constants():
    c = np.zeros((P, NCONST), np.float32)
    j, i = np.meshgrid(np.arange(P), np.arange(P), indexing="ij")
    same = j // CHUNK == i // CHUNK

    def put(name, value):
        a, b = CONST_COLS[name]
        c[:, a:b] = value

    put("ident", j == i)
    put("shift1", j == i - 1)
    put("shift2", j == i - 2)
    put("cross1", j == i - 1 + P)
    put("cross2", j == i - 2 + P)
    put("cum", same & (j <= i))
    put("suffix", same & (j > i))
    put("tri", j <= i)
    put("ones", 1.0)
    put("causal", np.where(i <= j, 0.0, MASKED))
    put("chunks", np.arange(P)[:, None] // CHUNK == np.arange(2)[None, :])
    put("slots", np.arange(P)[None, :])
    put("experts", np.arange(EXPERTS)[None, :])
    half = ROPE // 2
    inv = np.float32(THETA) ** (-np.arange(half, dtype=np.float32) * np.float32(2.0 / ROPE))
    ang = np.arange(S, dtype=np.float32)[:, None] * inv[None, :].astype(np.float32)
    put("cos", np.cos(ang).reshape(T, P, half).transpose(1, 0, 2).reshape(P, T * half))
    put("sin", np.sin(ang).reshape(T, P, half).transpose(1, 0, 2).reshape(P, T * half))
    put("minushalf", -0.5)
    return c


class Tally:
    DELTA = {
        "start": dict(),
        "ada": dict(g=12, w=12, lo=48, lin=36),
        "mod": dict(src=2),
        "tr8": dict(tg=4),
        "gla": dict(g=22, tg=4, w=7, act=8, dve=6, pool=2, acc=1, free=1, src=2, lo=24, lin=18),
        "out1": dict(w=2, acc=2, lo=8, lin=6),
        "out2": dict(w=4, acc=4, lo=16, lin=12),
        "ln": dict(dve=2, pool=2, free=1, src=2, ln=1),
        "trs8": dict(tg=4, act=4),
        "trs16": dict(tg=8, act=8),
        "ffn": dict(g=2 * NU, tg=NU, w=NU, d=NU, act=3 * NU, lo=6 * NU),
        "moe": dict(g=2 * NU * EXPERTS, tg=NU * EXPERTS, w=NU * EXPERTS, d=NU * EXPERTS, act=3 * NU * EXPERTS,
                    lo=6 * NU * EXPERTS, free=EXPERTS),
        "router": dict(g=4, act=1, dve=3),
        "kvdown": dict(g=2, tg=2, w=1, act=2, dve=3, pool=2),
        "fox": dict(g=16 + 32, tg=1 + 32, w=7, act=2 + 32, dve=2, acc=1, free=1, src=2, lo=24, lin=18),
        "mla": dict(g=2 + 24 + 24 + 32, tg=2 + 4 + 32, w=7, act=2 + 32, dve=3, pool=2, acc=2, free=2, src=2),
        "ple": dict(g=4, tg=1, w=3, act=2, acc=1, lo=8, lin=6),
    }
    def __init__(self):
        self.g = self.tg = self.w = self.d = self.act = self.dve = 0
        self.pool = self.acc = self.free = self.src = self.ln = self.lo = self.lin = 0

    def after(self, kind):
        new = Tally()
        e = self.DELTA[kind]
        new.g, new.tg = self.g + e.get("g", 0), self.tg + e.get("tg", 0)
        new.w, new.d = self.w + e.get("w", 0), self.d + e.get("d", 0)
        new.act, new.dve = self.act + e.get("act", 0), self.dve + e.get("dve", 0)
        new.pool, new.acc = self.pool + e.get("pool", 0), self.acc + e.get("acc", 0)
        new.free, new.src = self.free + e.get("free", 0), self.src + e.get("src", 0)
        new.ln, new.lo = self.ln + e.get("ln", 0), self.lo + e.get("lo", 0)
        new.lin = self.lin + e.get("lin", 0)
        return new


def stages():
    plan = [("start", 0)]
    for l in range(DEPTH):
        plan += [("ada", l), ("mod", 0), ("trs8", "src"), ("gla", l), ("trs8", "src"), ("out1", ("w_out", l)),
                 ("ln", ("mod", 2)), ("mod", 3), ("trs8", "src")]
        plan += [("ffn", "dense")] if l % 2 == 0 else [("router", 0), ("moe", 0)]
        plan += [("ln", ("mod", 5))]
    for i in range(DEPTH):
        if i:
            plan += [("tr8", "x"), ("kvdown", 0)]
        plan += [("trs8", "x"), ("ffn", ("ffn1", i)), ("ln", ("half", 0))]
        plan += [("tr8", "x"), ("mla", 0), ("trs16", "src"), ("out2", ("mla", 0))] if i else \
                [("trs8", "x"), ("fox", 0), ("trs8", "src"), ("out1", ("fox", 0))]
        plan += [("ln", ("plain", 0)), ("trs8", "x"), ("ffn", ("ffn2", i)), ("ln", ("half", 0)),
                 ("trs8", "x"), ("ple", i), ("ln", ("gate", 0))]
    return plan


def build(nc, I, out):
    plan = stages()
    tallies = [Tally()]
    for kind, _ in plan:
        tallies.append(tallies[-1].after(kind))
    steps = [(kind, arg, t, plan[max(i - 1, 0)][0]) for i, ((kind, arg), t) in enumerate(zip(plan, tallies))]

    def split_early(i):
        kind, _, n, _ = steps[i + 1]
        if kind in ("gla", "fox", "out1", "out2", "ple") or kind == "ffn" and steps[i - 1][0] != "mod":
            return kind, n
        return None, None

    with ExitStack() as ctx:
        def sb(name, cols, dt=F32, rows=P):
            return ctx.enter_context(nc.sbuf_tensor(name, [rows, cols], dt))

        def sem(name):
            return ctx.enter_context(nc.semaphore(name))

        G = ctx.enter_context(nc.psum_tensor("G", [P, 2, 512], F32))
        TB = ctx.enter_context(nc.psum_tensor("TB", [P, 2, 512], F32))
        A = ctx.enter_context(nc.psum_tensor("A", [P, 4, 512], F32))

        wide = [sb(f"wide{i}", WSLOT) for i in range(RW)]
        down = [sb(f"down{i}", DSLOT) for i in range(RD)]
        xs = sb("x_tok", T * D)
        x = xs[:, :].rearrange("p (t c) -> p t c", t=T)
        lnp = sb("ln_params", 2 * D)
        con = sb("con", NCONST)
        sg = sb("silu_gate", T * FU)
        hbuf = sb("hidden", 2 * T * FU)
        hT = sb("hidden_T", 2 * 2 * S)
        hT_at = nc.sbuf_base - 4 * 4 * S
        small = sb("small", 256)
        idx8 = sb("expert_idx", T * 8, U32)
        routw = sb("router_w", KD * EXPERTS)
        crowded = sb("crowded", 1, U32)
        pack = sb("pack", 2048)
        pick = pack[:, 0:256].rearrange("p (t s) -> p t s", t=T)
        pick_w = pack[:, 256:512].rearrange("p (t s) -> p t s", t=T)
        put_back = pack[:, 512:1024].rearrange("p (e s) -> p e s", e=2)
        packed_out = pack[:, 1024:2048]
        BIG = 2 * 4096
        ARENA = BIG + 15360 + 768
        arena = sb("arena", ARENA)
        arena_at = nc.sbuf_base - 4 * ARENA

        def split_tensor(name, cols, at):
            return nc.alloc_sbuf_tensor_at(name, [P, cols], F32R, offset=at)

        uh = split_tensor("u_hi", KD * S, arena_at)
        ul = split_tensor("u_lo", KD * S, arena_at + 4 * 2048)
        hth = split_tensor("hidden_hi", 2 * S, hT_at)
        htl = split_tensor("hidden_lo", 2 * S, hT_at + 4 * 2 * S)
        piece_at = [arena_at + 4 * (BIG + 1024 * j) for j in (0, 1, 2, 3, 4, 6, 7, 8, 9, 10, 11, 12)]
        w_hi = [split_tensor(f"w_hi{j}", 1024, piece_at[2 * j]) for j in range(6)]
        w_lo = [split_tensor(f"w_lo{j}", 1024, piece_at[2 * j + 1]) for j in range(6)]

        l_hi = [sb(f"l_hi{j}", 1024, F32R) for j in range(2)]
        l_lo = [sb(f"l_lo{j}", 1024, F32R) for j in range(2)]
        m_hi = [l_hi[0][:, :], l_hi[1][:, :], uh[:, KD * P:2 * KD * P]]
        m_lo = [l_lo[0][:, :], l_lo[1][:, :], ul[:, KD * P:2 * KD * P]]
        yh = split_tensor("y_hi", 2 * KD * S, arena_at)
        yl = split_tensor("y_lo", 2 * KD * S, arena_at + 4 * (BIG + 8192))

        def C(name):
            a, b = CONST_COLS[name]
            return con[:, a:b]

        ident, ones = C("ident"), C("ones")

        def area(at, *shape):
            size = 1
            for s in shape:
                size *= s
            v = arena[:, at:at + size]
            if len(shape) == 2:
                v = v.rearrange("p (a b) -> p a b", a=shape[0])
            if len(shape) == 3:
                v = v.rearrange("p (a b c) -> p a b c", a=shape[0], b=shape[1])
            return v

        uT = area(0, 16, S)
        src = area(4096, T, D)
        src2 = area(4096, T, 2 * D)
        z1 = area(2048, T, CONV)
        gqT = area(2048, 2, S)
        gkT = area(2560, 2, S)
        stm = area(3072, 2, 2 * T, P)
        e3 = area(6144, T, 3 * KW)
        lsg = area(6144, T, KW)
        state = area(6144, 3, 2, 2 * DV)
        gk = area(7680, T, KW)
        mod = area(BIG, 6, D)
        proj = area(BIG + 6144, T, 3088)
        convw = area(BIG + 12320, WIDTH, CONV)
        gnw = area(BIG + 13856, DV)
        glowT = area(BIG + 13984, S)
        gkw2 = area(BIG + 14240, KW)
        gkb = area(BIG + 14496, KW)
        cqT = area(2048, 3, S)
        ckvT = area(BIG + 15360, 2, S)
        krT = area(BIG + 15872, S)
        moe_sum = area(BIG + 13312, T, D)
        qnT = area(BIG, MLA_H, S)
        knT = area(BIG + 4096, MLA_H, S)
        vtok = area(BIG + 8192, T, 2 * D)
        qrT = area(BIG + 12288, MLA_H // 2, S)
        cq = area(BIG, T, QLORA)
        ckv = area(BIG, T, KVLORA)
        krd = area(BIG + 512, T, 2 * ROPE)
        qr_raw = area(4096, T, MLA_H, ROPE)
        qr_rot = area(6144, T, MLA_H, ROPE)
        ropetmp = area(BIG + 4096, MLA_H, ROPE // 2)
        fqT = area(BIG, KD, S)
        fkT = area(BIG + 2048, KD, S)
        fv = area(BIG + 4096, T, D)
        ncT = area(BIG + 14336, S)
        cumf = area(BIG + 14592, T, FOX_H)
        fls = area(BIG + 14624, T, FOX_H)
        flt = area(BIG + 14656, T, FOX_H)
        qnw = area(BIG + 14688, QLORA)
        kvnw = area(BIG + 15072, KVLORA)
        bfrow = area(BIG + 15328, FOX_H)
        gt = area(BIG, T, D)
        bgate = area(BIG + 2048, D)
        ptok = area(BIG + 3072, T, S)
        pT = area(BIG + 3584, 2, S)
        scores = hbuf[:, 0:2 * S].rearrange("p (b s) -> p b s", b=2)
        probs = hbuf[:, 2 * S:4 * S].rearrange("p (b s) -> p b s", b=2)
        pbT = hT[:, 0:4 * P].rearrange("p (b s q) -> p b s q", b=2, s=2)
        hid = hbuf[:, :].rearrange("p (b t f) -> p b t f", b=2, t=T)
        hidT = hT[:, :].rearrange("p (b f s) -> p b f s", b=2, f=2)
        sgt = sg[:, :].rearrange("p (t f) -> p t f", t=T)

        stats = small[:, 0:24].rearrange("p (t c s) -> p t c s", t=T, c=2)
        mv = small[:, 24:28].rearrange("p (t c) -> p t c", t=T)
        ve = small[:, 28:36].rearrange("p (t h) -> p t h", t=T)
        rstd = small[:, 36:44].rearrange("p (t h) -> p t h", t=T)
        ssq = small[:, 44:52].rearrange("p (t h) -> p t h", t=T)
        dec = small[:, 52:60].rearrange("p (t a c) -> p t a c", t=T, a=2)
        condT = small[:, 60:68]
        cT = small[:, 68:76]
        nmax = small[:, 76:78]
        rsum = small[:, 80:112].rearrange("p (t h) -> p t h", t=T)
        rinv = small[:, 112:144].rearrange("p (t h) -> p t h", t=T)
        logit = small[:, 144:160].rearrange("p (t e) -> p t e", t=T)
        top8 = small[:, 160:176].rearrange("p (t e) -> p t e", t=T)
        gap = small[:, 176:178]
        e2 = small[:, 178:180]
        w1 = small[:, 180:182]
        w2 = small[:, 182:184]
        idxf = small[:, 184:200].rearrange("p (t e) -> p t e", t=T)
        route = small[:, 200:216].rearrange("p (t e) -> p t e", t=T)
        rtmp = small[:, 216:232].rearrange("p (t e) -> p t e", t=T)
        slotid = rtmp
        member = small[:, 232:248].rearrange("p (t e) -> p t e", t=T)
        cond_hi = uh[:, 0:KD * P].rearrange("p (k s) -> p k s", k=KD)
        cond_lo = ul[:, 0:KD * P].rearrange("p (k s) -> p k s", k=KD)

        g_done = sem("g_done")
        g_read = sem("g_read")
        t_done = sem("t_done")
        t_evac = sem("t_evac")
        acc_done = sem("acc_done")
        acc_free = sem("acc_free")
        down_used = sem("down_used")
        act_ready = sem("act_ready")
        dve_ready = sem("dve_ready")
        pool_ready = sem("pool_ready")
        src_ready = sem("src_ready")
        dve_step = sem("dve_step")
        act_step = sem("act_step")
        wide_full = [sem(f"wide_full{i}") for i in range(RW)]
        wide_full2 = [sem(f"wide_full2_{i}") for i in range(RW)]
        down_full = [sem(f"down_full{i}") for i in range(RD)]
        s_con = sem("con_loaded")
        s_x = sem("x_loaded")
        s_c = sem("c_loaded")
        s_rout = sem("router_loaded")
        s_ada = [sem(f"ada_bias{row}_loaded") for row in range(6)]
        s_gla = sem("gla_params_loaded")
        s_ln = sem("ln_params_loaded")
        s_attn = sem("attn_params_loaded")
        s_ple = sem("ple_params_loaded")
        s_out = sem("out_stored")

        hi_ready = sem("hi_ready")
        lo_ready = sem("lo_ready")
        up_used = sem("up_used")
        down0_used = sem("down0_used")
        pick_ready = sem("pick_ready")
        scat_done = sem("scat_done")
        scat_read = sem("scat_read")
        lin_used = sem("lin_used")
        cond_rounded = sem("cond_rounded")
        cond_ready = sem("cond_ready")

        def ring_count(base, n, depth, need):
            return base * (need // depth) + need * (n // depth + 1)

        def up_pieces(c, j):
            if isinstance(c, int) and c == 0:
                return j + 1
            return c * 6 + (j - 1)

        def down_pieces(c, f, units):
            if isinstance(c, int) and c == units - 1:
                return 6 * units - 1 + f
            return c * 6 + (9 + f)

        def roll(eng, units, step):
            step(0, 0)
            step(1, 1)
            with eng.Fori(0, (units - 3) // 2) as i:
                for j in (2, 3):
                    step(j, i * 2 + j)
            step(units - 1, units - 1)

        def straight(eng, units, step):
            for c in range(units):
                step(c, c)

        PREP_AT = 4
        G_PAIR = PAIR + 6
        ACT_PAIR = 2 * PAIR + 6

        def g_unit(c):
            return c + 3 if c <= PREP_AT else c + 6

        def g_prep(e):
            return (PREP_AT + 4) * e

        def a_silu(c):
            return 2 * c + 3 + (2 if c > PREP_AT else 0) + (1 if c > NU else 0)

        def a_prep(e, half):
            return 1 + half + (2 + 2 * (PREP_AT + 1)) * e

        def a_out(e):
            return a_silu(NU) + 2 if e == 0 else ACT_PAIR

        def linear_bank(c, b):
            return (TB if c % 2 else G)[:, b, :]

        def flat(ap):
            return {2: lambda a: a, 3: lambda a: a.rearrange("p a b -> p (a b)")}[len(ap.shape)](ap)

        def swiglu(arg):
            if arg == "dense":
                return I["ffn_w_gate"][0], I["ffn_w_up"][0], I["ffn_w_down"][0]
            name, i = arg
            w = I[f"{name}_w_in_2"][i]
            return w[:, 0:FF], w[:, FF:2 * FF], I[f"{name}_w_out_2"][i]

        block = ctx.enter_context(nc.Block())

        @block.sync
        def _(sp):
            released = []
            state_w = {"w": 0}

            def wait_slot(half=1):
                w = state_w["w"]
                if w >= RW:
                    s, v = released[w - RW]
                    if s is lo_ready and half == 0:
                        v -= 2
                    sp.wait_ge(s, v)

            def fill(view_k, kt, cols, freed_by):
                w = state_w["w"]
                dst = wide[w % RW][:, 0:kt * cols].rearrange("p (k c) -> p k c", k=kt)
                cut = (kt + 1) // 2
                wait_slot(0)
                sp.dma_start(dst[:, 0:cut], view_k[:, 0:cut]).then_inc(wide_full[w % RW], 16)
                wait_slot()
                sp.dma_start(dst[:, cut:kt], view_k[:, cut:kt]).then_inc(wide_full2[w % RW], 16)
                released.append(freed_by)
                state_w["w"] = w + 1

            def kview(w_ap):
                return w_ap.rearrange("(k p) c -> p k c", p=P)

            def load_up(slot, gate, up, at):
                gv = wide[slot][:, :].rearrange("p (k h f) -> p k h f", k=KD, h=2)
                sp.dma_start(gv[:, :, 0], kview(gate)[:, :, bass.ds(at, FU)]).then_inc(wide_full[slot], 16)
                sp.dma_start(gv[:, :, 1], kview(up)[:, :, bass.ds(at, FU)]).then_inc(wide_full2[slot], 16)

            def load_down(dslot, dn, at):
                sp.dma_start(down[dslot][:, :].rearrange("p (f c) -> p f c", f=2),
                             dn[bass.ds(at, FU), :].rearrange("(f p) c -> p f c", p=P)).then_inc(down_full[dslot], 16)

            for kind, arg, n, _ in steps:
                if kind == "ada":
                    v = kview(I["ada_w"][arg])
                    for c in range(12):
                        fill(v[:, :, c * 512:(c + 1) * 512], KD, 512, (lo_ready, n.lo + 4 * c + 4))
                        if arg == 0 and c == RW:
                            sp.dma_start(con[:, :], I["con"]).then_inc(s_con, 16)
                elif kind == "gla":
                    v = kview(I["w_in"][arg])
                    for c in range(6):
                        fill(v[:, :, c * 512:(c + 1) * 512], KD, 512, (lo_ready, n.lo + 4 * c + 4))
                    fill(v[:, :, C_LOW:C_LOW + RANK], KD, RANK, (t_done, n.tg + 1))
                elif kind in ("out1", "out2"):
                    name, i = arg
                    w_ap = {"w_out": I["w_out"], "fox": I["fox_w_o_2"], "mla": I["mla_w_o_2"]}[name][i]
                    v, kt = kview(w_ap), (KD if kind == "out1" else 2 * KD)
                    cols = WSLOT // kt
                    for c in range(D // cols):
                        fill(v[:, :, c * cols:(c + 1) * cols], kt, cols, (lo_ready, n.lo + 4 * c + 4))
                elif kind == "ffn":
                    gate, up, dn = swiglu(arg)

                    def step_in(j, c):
                        if j >= RW:
                            sp.wait_ge(lo_ready, up_pieces(c - RW, 3) + n.lo)
                        load_up((n.w + j) % RW, gate, up, c * FU)
                        if j:
                            down_in(j - 1, c - 1)

                    def down_in(j, c):
                        if j >= RD:
                            sp.wait_ge(lo_ready, down_pieces(c - RD, 1, NU) + n.lo)
                        elif n.lo:
                            sp.wait_ge(lo_ready, n.lo)
                        load_down((n.d + j) % RD, dn, c * FU)

                    for c in range(3):
                        if c < RW:
                            wait_slot()
                            state_w["w"] += 1
                            released.append((lo_ready, n.lo + up_pieces(c, 3)))
                        step_in(c, c)
                    with sp.Fori(0, (NU - 3) // 2) as i:
                        for j in (3, 4):
                            step_in(j, i * 2 + j)
                    down_in(NU - 1, NU - 1)
                    for c in range(RW, NU):
                        released.append((lo_ready, n.lo + up_pieces(c, 3)))
                    state_w["w"] += NU - RW
                elif kind == "moe":
                    gates, ups, dns = I["moe_w_gate"][0], I["moe_w_up"][0], I["moe_w_down"][0]
                    for _ in range(RW):
                        wait_slot()
                        state_w["w"] += 1
                        released.append(None)
                    with sp.Fori(0, EXPERTS // 2) as i:
                        lo0 = i * (6 * PAIR) + n.lo
                        for c in range(PAIR):
                            sp.wait_ge(lo_ready, lo0 + up_pieces(c - RW, 3) if c >= RW else lo0)
                            gate = gates[bass.ds(i * 2 + c // NU, 1)].rearrange("e d f -> (e d) f")
                            up = ups[bass.ds(i * 2 + c // NU, 1)].rearrange("e d f -> (e d) f")
                            load_up((n.w + c) % RW, gate, up, (c % NU) * FU)
                            for b in ([c - 1] if c else []) + ([c] if c == PAIR - 1 else []):
                                if b >= RD:
                                    sp.wait_ge(lo_ready, lo0 + down_pieces(b - RD, 1, PAIR))
                                dn = dns[bass.ds(i * 2 + b // NU, 1)].rearrange("e d f -> (e d) f")
                                load_down((n.d + b) % RD, dn, (b % NU) * FU)
                    for c in range(RW, NU * EXPERTS):
                        in_last = c - (EXPERTS // 2 - 1) * PAIR
                        released.append((lo_ready, n.lo + (EXPERTS // 2 - 1) * 6 * PAIR + up_pieces(in_last, 3))
                                        if in_last >= 0 else None)
                    state_w["w"] += NU * EXPERTS - RW
                elif kind == "kvdown":
                    fill(kview(I["kv_w_down_2"]), KD, KVLORA + ROPE, (g_done, n.g + 2))
                elif kind == "fox":
                    v = kview(I["fox_w_in_2"][0])
                    for c in range(6):
                        fill(v[:, :, c * 512:(c + 1) * 512], KD, 512, (lo_ready, n.lo + 4 * c + 4))
                    fill(v[:, :, 3 * D:3 * D + FOX_H], KD, FOX_H, (g_done, n.g + 14))
                elif kind == "mla":
                    fill(kview(I["mla_w_dq_2"][0]), KD, QLORA, (g_done, n.g + 2))
                    v = I["mla_w_uq_2"][0].rearrange("(k p) h d -> p k (h d)", p=P)
                    cols = 4 * (NOPE + ROPE)
                    for c in range(4):
                        fill(v[:, :, c * cols:(c + 1) * cols], 3, cols, (g_done, n.g + 2 + 6 * c + 6))
                    v = I["kv_w_up_2"].rearrange("(k p) h d -> p k (h d)", p=P)
                    for c in range(2):
                        fill(v[:, :, c * 2048:(c + 1) * 2048], 2, 2048, (g_done, n.g + 26 + 12 * c + 12))
                elif kind == "ple":
                    v = kview(I["ple_w_gate_2"][arg])
                    for c in range(2):
                        fill(v[:, :, c * 512:(c + 1) * 512], KD, 512, (lo_ready, n.lo + 4 * c + 4))
                    fill(kview(I["ple_w_proj_2"][arg]), 2, D, (acc_done, n.acc + 1))
            sp.wait_ge(src_ready, tallies[-1].src)
            sp.dma_start(out[0].rearrange("(t p) c -> p t c", p=P), x).then_inc(s_out, 16)
            sp.wait_ge(s_out, 16)

        @block.tensor
        def _(pe):
            def open_g(g):
                if not isinstance(g, int) or g >= 2:
                    pe.wait_ge(g_read, g - 1)

            def open_t(tg):
                if not isinstance(tg, int) or tg >= 2:
                    pe.wait_ge(t_evac, tg - 1)

            def wide_ready(w):
                pe.wait_ge(wide_full[w % RW], NEED_WIDE * (w // RW + 1))
                pe.wait_ge(wide_full2[w % RW], NEED_WIDE * (w // RW + 1))

            def slot(w, kt, cols):
                return wide[w % RW][:, 0:kt * cols].rearrange("p (k c) -> p k c", k=kt)

            def mm(o, lhsT, rhs, start, stop):
                return nc.tensor.matmul(o, lhsT, rhs, start=start, stop=stop, skip_group_check=True)

            def tok(t):
                return slice(t * P, (t + 1) * P)

            def project(g, t, aT, kt, rhs_of, cols):
                open_g(g)
                for k in range(kt):
                    last = mm(G[:, g % 2, 0:cols], aT[:, k, tok(t)], rhs_of(k), k == 0, k == kt - 1)
                return last.then_inc(g_done, 1)

            def project_T(g, lhs_of, aT, kt):
                open_g(g)
                for k in range(kt):
                    last = mm(G[:, g % 2, 0:S], lhs_of(k), aT[:, k, :], k == 0, k == kt - 1)
                return last.then_inc(g_done, 1)

            def transposes(tg, blocks):
                open_t(tg)
                for b, block_in in enumerate(blocks):
                    last = nc.tensor.transpose(TB[:, tg % 2, b * P:(b + 1) * P], block_in, ident)
                return last.then_inc(t_done, 1)

            def attention(n, g0, tg0, act0, heads, rows, scores_of, vcols, free0):
                todo = [(t, h) for t in range(T) for h in range(heads)]
                per_t = len(todo) // T
                for i in range(len(todo) + 2):
                    if i < len(todo):
                        t, h = todo[i]
                        open_g(g0 + i)
                        scores_of(G[:, (g0 + i) % 2, 0:P * (t + 1)], t, h).then_inc(g_done, 1)
                    if 1 <= i <= len(todo):
                        t, h = todo[i - 1]
                        pe.wait_ge(act_ready, act0 + i)
                        transposes(tg0 + i - 1, [probs[:, (i - 1) % 2, tok(b)] for b in range(t + 1)])
                    if i >= 2:
                        t, h = todo[i - 2]
                        pe.wait_ge(t_evac, tg0 + i - 1)
                        if i == 2:
                            pe.wait_ge(acc_free, free0)
                        if vcols == VH and t and h == 0:
                            pe.wait_ge(acc_free, free0 + 1)
                        if vcols == VH:
                            o = A[:, h // 4, (h % 4) * VH:(h % 4 + 1) * VH]
                            v = vtok
                        else:
                            o = A[:, 2 * t + h // 8, (h % 8) * FOX_D:(h % 8 + 1) * FOX_D]
                            v = fv
                        for b in range(t + 1):
                            last = mm(o, pbT[:, i % 2, b, :], v[:, b, h * vcols:(h + 1) * vcols], b == 0, b == t)
                        if (i - 2) % per_t == per_t - 1 and (vcols == VH or t == T - 1):
                            last.then_inc(acc_done, 1)

            uhv = uh[:, :].rearrange("p (k s) -> p k s", k=KD)
            ulv = ul[:, :].rearrange("p (k s) -> p k s", k=KD)
            hthv = hth[:, :].rearrange("p (f s) -> p f s", f=2)
            htlv = htl[:, :].rearrange("p (f s) -> p f s", f=2)

            def mm3(o, a_hi, a_lo, b_hi, b_lo, start, stop):
                mm(o, a_hi, b_hi, start, False)
                mm(o, a_hi, b_lo, False, False)
                return mm(o, a_lo, b_hi, False, stop)

            def linear(n, chunks, act_hi, act_lo, kpp, open_chunk, out_of, done, per_bank, turned=()):
                for c in range(chunks):
                    for q in range(4):
                        pe.wait_ge(lo_ready, n.lo + 4 * c + q + 1)
                        if q == 0:
                            open_chunk(c)
                        hi = l_hi[q % 2][:, :].rearrange("p (k c) -> p k c", k=kpp)
                        lo = l_lo[q % 2][:, :].rearrange("p (k c) -> p k c", k=kpp)
                        for kk in range(kpp):
                            k = kpp * q + kk
                            for b in range(2):
                                o = out_of(c, b)
                                start, stop = k == 0, k == 4 * kpp - 1
                                if c in turned:
                                    for f in range(2):
                                        at = slice((2 * b + f) * P, (2 * b + f + 1) * P)
                                        last = mm3(o[:, f * S:(f + 1) * S], hi[:, kk, at], lo[:, kk, at],
                                                   act_hi[:, k, :], act_lo[:, k, :], start and f == 0, stop)
                                else:
                                    last = mm3(o, act_hi[:, k, tok(b)], act_lo[:, k, tok(b)], hi[:, kk, :], lo[:, kk, :],
                                               start, stop)
                                if stop and (per_bank or b):
                                    last.then_inc(done, 1)
                        if q < 3:
                            last.then_inc(lin_used, 1)

            def open_banks(n):
                def open_chunk(c):
                    pe.wait_ge(g_read, n.g if c < 2 else n.g + 2 * c - 2) if n.g or c > 1 else None
                return open_chunk

            def run(n, units, walk, past, first_of, last_of, fresh_acc):
                def up(j, c):
                    for q in range(4):
                        pe.wait_ge(lo_ready, past * 6 + up_pieces(c, q) + n.lo)
                        if q == 0:
                            open_g((c + past) * 2 + (n.g + 1))
                        hi = w_hi[q][:, :].rearrange("p (k c) -> p k c", k=2)
                        lo = w_lo[q][:, :].rearrange("p (k c) -> p k c", k=2)
                        for kk in range(2):
                            k = 2 * q + kk
                            for t in range(T):
                                last = mm3(G[:, t, :], uhv[:, k, tok(t)], ulv[:, k, tok(t)], hi[:, kk, :], lo[:, kk, :],
                                           k == 0, k == KD - 1)
                                if k == KD - 1:
                                    last.then_inc(g_done, 1)
                        if q < 3:
                            last.then_inc(up_used, 1)

                def down_product(j, c):
                    if j in first_of:
                        pe.wait_ge(acc_free, fresh_acc(j))
                    for f in range(2):
                        pe.wait_ge(lo_ready, past * 6 + down_pieces(c, f, units) + n.lo)
                        hi, lo = w_hi[4 + f], w_lo[4 + f]
                        for t in range(T):
                            for half in range(2):
                                cols = slice(half * 512, half * 512 + 512)
                                last = mm3(A[:, 2 * t + half, :], hthv[:, f, tok(t)], htlv[:, f, tok(t)],
                                           hi[:, cols], lo[:, cols], j in first_of and f == 0, j in last_of and f == 1)
                        last.then_inc(down_used if f else down0_used, 1)

                def last_down_product():
                    for f in range(2):
                        pe.wait_ge(lo_ready, past * 6 + down_pieces(units - 1, f, units) + n.lo)
                    for t in range(T):
                        for f in range(2):
                            for half in range(2):
                                cols = slice(half * 512, half * 512 + 512)
                                last = mm3(A[:, 2 * t + half, :], hthv[:, f, tok(t)], htlv[:, f, tok(t)],
                                           w_hi[4 + f][:, cols], w_lo[4 + f][:, cols], False, f == 1)
                        last.then_inc(down_used if t else down0_used, 1)

                def turn(j, c):
                    tg = (c + past) + n.tg
                    pe.wait_ge(g_read, (c + past) * 2 + (n.g + 2))
                    open_t(tg)
                    for f in range(2):
                        for t in range(T):
                            last = nc.tensor.transpose(TB[:, (n.tg + j) % 2, f * S + t * P:f * S + (t + 1) * P],
                                                       hid[:, 0, t, tok(f)], ident)
                    last.then_inc(t_done, 1)

                def step(j, c):
                    up(j, c)
                    if j:
                        pe.wait_ge(t_evac, (c + past) + n.tg)
                        down_product(j - 1, c - 1)
                    turn(j, c)

                walk(pe, units, step)
                pe.wait_ge(t_evac, past + (n.tg + units))
                last_down_product()

            def run_packed(n, i):
                past = i * PAIR
                g0, a0 = i * G_PAIR + n.g, i * ACT_PAIR + n.act

                def prepare(e):
                    pe.wait_ge(pick_ready, i * 2 + (e + 1))
                    b = (n.g + g_prep(e)) % 2
                    pe.wait_ge(g_read, g0 + (g_prep(e) - 1))
                    for t in range(T):
                        last = nc.tensor.transpose(G[:, b, tok(t)], pick_w[:, t, :], ident)
                    last.then_inc(g_done, 1)
                    for half in range(2):
                        b = (n.g + g_prep(e) + 1 + half) % 2
                        pe.wait_ge(g_read, g0 + (g_prep(e) + half))
                        for kk in range(4):
                            for t in range(T):
                                last = mm(G[:, b, tok(kk)], src[:, t, tok(4 * half + kk)], pick[:, t, :], t == 0, t == 1)
                        last.then_inc(g_done, 1)

                def up(c):
                    e, b = c // NU, (n.g + g_unit(c)) % 2
                    if c % NU == 0:
                        pe.wait_ge(g_read, g0 + (g_prep(e) + 3))
                    for q in range(4):
                        pe.wait_ge(lo_ready, past * 6 + (up_pieces(c, q) + n.lo))
                        if q == 0:
                            pe.wait_ge(g_read, g0 + (g_unit(c) - 1))
                        for kk in range(2):
                            k = 2 * q + kk
                            at = e * 1024 + k * P
                            last = mm3(G[:, b, :], uh[:, at:at + P], ul[:, at:at + P],
                                       w_hi[q][:, kk * 512:(kk + 1) * 512], w_lo[q][:, kk * 512:(kk + 1) * 512],
                                       k == 0, k == KD - 1)
                        last.then_inc(up_used if q < 3 else g_done, 1)

                def down_product(c):
                    e = c // NU
                    if c == 0:
                        pe.wait_ge(acc_free, i * 2 + n.free)
                    for f in range(2):
                        pe.wait_ge(lo_ready, past * 6 + (down_pieces(c, f, PAIR) + n.lo))
                        for half in range(2):
                            cols = slice(half * 512, half * 512 + 512)
                            last = mm3(A[:, 2 * e + half, :], hth[:, tok(f)], htl[:, tok(f)], w_hi[4 + f][:, cols],
                                       w_lo[4 + f][:, cols], c % NU == 0 and f == 0, c % NU == NU - 1 and f == 1)
                        last.then_inc(down_used if f else down0_used, 1)

                def turn(c):
                    pe.wait_ge(g_read, g0 + (g_unit(c) + 1))
                    tg = past + (c + n.tg)
                    open_t(tg)
                    for f in range(2):
                        last = nc.tensor.transpose(TB[:, (n.tg + c) % 2, tok(f)], hid[:, 0, 0, tok(f)], ident)
                    last.then_inc(t_done, 1)

                def scatter(e, t, banks):
                    for half in range(2):
                        last = mm(A[:, banks + half, :], put_back[:, e, tok(t)],
                                  packed_out[:, half * 512:(half + 1) * 512], True, True)
                    last.then_inc(scat_done, 1)

                prepare(0)
                for c in range(PAIR):
                    up(c)
                    if c:
                        pe.wait_ge(t_evac, past + (c + n.tg))
                        down_product(c - 1)
                    turn(c)
                    if c == PREP_AT:
                        prepare(1)
                    if c == NU + 1:
                        pe.wait_ge(act_ready, a0 + a_out(0))
                        scatter(0, 0, 0)
                    if c == NU + 2:
                        pe.wait_ge(scat_read, i * 2 + 1)
                        scatter(0, 1, 0)
                pe.wait_ge(t_evac, past + (n.tg + PAIR))
                down_product(PAIR - 1)
                pe.wait_ge(act_ready, a0 + a_out(1))
                scatter(1, 0, 2)
                pe.wait_ge(acc_free, i * 2 + (n.free + 1))
                scatter(1, 1, 0)

            for kind, arg, n, before in steps:
                if kind == "ada":
                    pe.wait_ge(cond_ready, arg + 1)
                    for c in range(12):
                        g = n.g + c
                        for q in range(4):
                            pe.wait_ge(lo_ready, n.lo + 4 * c + q + 1)
                            if q == 0:
                                open_g(g)
                            for kk in range(2):
                                k, cols = 2 * q + kk, slice(kk * 512, kk * 512 + 512)
                                at = (4 * c + q) % 3
                                last = mm3(G[:, g % 2, :], cond_hi[:, k, :], cond_lo[:, k, :], m_hi[at][:, cols],
                                           m_lo[at][:, cols], k == 0, k == KD - 1)
                            last.then_inc(lin_used if q < 3 else g_done, 1)
                    if arg == 0:
                        pe.wait_ge(s_con, 16)
                elif kind == "tr8":
                    pe.wait_ge(src_ready, n.src)
                    for j in range(KD // 2):
                        transposes(n.tg + j, [x[:, t, tok(2 * j + k)] for k in range(2) for t in range(T)])
                elif kind in ("trs8", "trs16"):
                    pe.wait_ge(t_evac, n.tg)
                    groups = 4 if kind == "trs16" else 2
                    view = x if arg == "x" else (src if kind == "trs8" else src2)
                    for t in range(T):
                        pe.wait_ge(src_ready, n.src - 1 + t)
                        for j in range(groups):
                            transposes(n.tg + groups * t + j, [view[:, t, tok(4 * j + k)] for k in range(4)])
                elif kind == "gla":
                    pe.wait_ge(t_evac, n.tg)
                    linear(n, 6, uhv, ulv, 2, open_banks(n), linear_bank, g_done, True)
                    wide_ready(n.w + 6)
                    wv6 = slot(n.w + 6, KD, RANK)
                    pe.wait_ge(g_read, n.g + 12)
                    for k in range(KD):
                        o = TB[0:RANK, n.tg % 2, 0:S]
                        mm(o, wv6[:, k, :], uhv[:, k, :].bitcast(F32), k == 0, False)
                        last = mm(o, wv6[:, k, :], ulv[:, k, :].bitcast(F32), False, k == KD - 1)
                    last.then_inc(t_done, 1)
                    pe.wait_ge(s_gla, 64 * (arg + 1))
                    pe.wait_ge(t_evac, n.tg + 1)
                    for t in range(T):
                        g = n.g + 12 + t
                        open_g(g)
                        mm(G[:, g % 2, 0:KW], ones[0:1, :], gkb[0:1, :], True, False)
                        mm(G[:, g % 2, 0:KW], glowT[0:RANK, tok(t)], gkw2[0:RANK, :], False, True) \
                            .then_inc(g_done, 1)
                    pe.wait_ge(dve_ready, n.dve + 1)
                    for t in range(T):
                        g = n.g + 14 + t
                        open_g(g)
                        o = G[:, g % 2, :]
                        mm(o, ident, proj[:, t, C_C:C_C + CONV], True, False)
                        mm(o, C("shift1"), z1[:, t, :], False, False)
                        if t:
                            mm(o, C("cross1"), z1[:, t - 1, :], False, False)
                            mm(o, C("cross2"), proj[:, t - 1, C_H:C_H + CONV], False, False)
                        mm(o, C("shift2"), proj[:, t, C_H:C_H + CONV], False, True).then_inc(g_done, 1)
                    for t in range(T):
                        g = n.g + 16 + t
                        pe.wait_ge(dve_ready, n.dve + 2 + t)
                        open_g(g)
                        mm(G[:, g % 2, 0:KW], C("cum"), gk[:, t, :], True, True)
                        mm(G[:, g % 2, KW:2 * KW], C("suffix"), gk[:, t, :], True, True).then_inc(g_done, 1)
                    open_t(n.tg + 1)
                    for t in range(T):
                        for a in range(2):
                            last = mm(TB[:, (n.tg + 1) % 2, t * 4 + a * 2:t * 4 + a * 2 + 2],
                                      gk[:, t, tok(a)], C("chunks"), True, True)
                    last.then_inc(t_done, 1)
                    pe.wait_ge(g_read, n.g + 18)
                    transposes(n.tg + 2, [proj[:, t, C_Q + a * P:C_Q + (a + 1) * P] for a in range(2)
                                          for t in range(T)])
                    transposes(n.tg + 3, [proj[:, t, C_C + a * P:C_C + (a + 1) * P] for a in range(2)
                                          for t in range(T)])
                    pe.wait_ge(acc_free, n.free) if n.free else None
                    for c in range(3):
                        t, r = c // 2, slice(CHUNK * (c % 2), CHUNK * (c % 2) + CHUNK)
                        for a in range(2):
                            last = mm(A[:, c, a * KW:(a + 1) * KW], proj[r, t, C_K + a * P:C_K + (a + 1) * P],
                                      proj[r, t, C_V + a * KW:C_V + (a + 1) * KW], True, True)
                    last.then_inc(acc_done, 1)
                    pe.wait_ge(t_evac, n.tg + 4)
                    for f in range(2):
                        g = n.g + 18 + f
                        r = slice(DK * f, DK * f + DK)
                        open_g(g)
                        for j in range(2 * T):
                            a, t = divmod(j, T)
                            last = mm(G[:, g % 2, tok(j)], gkT[r, a, tok(t)], gqT[r, a, tok(t)], True, True)
                        last.then_inc(g_done, 1)
                    pe.wait_ge(g_read, n.g + 20)
                    pe.wait_ge(dve_ready, n.dve + 4)
                    for t in range(T):
                        g = n.g + 20 + t
                        open_g(g)
                        for h in range(HEADS):
                            mm(G[:, g % 2, tok(h)], stm[:, h % 2, T * (h // 2) + t, :],
                               proj[:, t, C_V + h * DV:C_V + (h + 1) * DV], h == 0, False)
                        for f in range(2):
                            c = 2 * t + f
                            if c:
                                q = slice(CHUNK * f, CHUNK * f + CHUNK)
                                for a in range(2):
                                    last = mm(G[q, g % 2, a * KW:(a + 1) * KW],
                                              gqT[:, a, t * P + CHUNK * f:t * P + CHUNK * f + CHUNK],
                                              state[:, c - 1, a, :], False, True)
                        last.then_inc(g_done, 1)
                elif kind in ("out1", "out2"):
                    pe.wait_ge(t_evac, n.tg)
                    pe.wait_ge(acc_free, n.free)
                    if kind == "out1":
                        linear(n, 2, uhv, ulv, 2, lambda c: None, lambda c, b: A[:, 2 * b + c, :], acc_done, False)
                    else:
                        linear(n, 4, yh[:, :].rearrange("p (k s) -> p k s", k=2 * KD),
                               yl[:, :].rearrange("p (k s) -> p k s", k=2 * KD), 4, lambda c: None,
                               lambda c, b: A[:, 2 * b + c // 2, (c % 2) * 256:(c % 2 + 1) * 256], acc_done, False)
                elif kind == "ffn":
                    pe.wait_ge(t_evac, n.tg)
                    run(n, NU, roll, 0, (0,), (NU - 1,), lambda j: n.free)
                elif kind == "moe":
                    pe.wait_ge(t_evac, n.tg)
                    pe.wait_ge(dve_ready, n.dve)
                    full = pe.value_load(crowded[0:1, 0:1], min_val=0, max_val=1)
                    with pe.If(full == 0):
                        with pe.Fori(0, EXPERTS // 2) as i:
                            run_packed(n, i)
                        pe.drain().then_inc(g_done, 2 * NU * EXPERTS - G_PAIR * (EXPERTS // 2))
                    with pe.Else():
                        with pe.Fori(0, EXPERTS // 2) as i:
                            run(n, PAIR, straight, i * PAIR, (0, NU), (NU - 1, PAIR - 1),
                                lambda j: i * 2 + (n.free + j // NU))
                elif kind == "router":
                    pe.wait_ge(t_evac, n.tg)
                    pe.wait_ge(s_rout, 16)
                    rv = routw[:, :].rearrange("p (k e) -> p k e", k=KD)
                    for t in range(T):
                        g = n.g + t
                        open_g(g)
                        for k in range(KD):
                            mm(G[:, g % 2, 0:EXPERTS], uhv[:, k, tok(t)].bitcast(F32), rv[:, k, :], k == 0, False)
                            last = mm(G[:, g % 2, 0:EXPERTS], ulv[:, k, tok(t)].bitcast(F32), rv[:, k, :],
                                      False, k == KD - 1)
                        last.then_inc(g_done, 1)
                    pe.wait_ge(dve_ready, n.dve + 2)
                    for t in range(T):
                        g = n.g + 2 + t
                        open_g(g)
                        last = mm(G[:, g % 2, 0:EXPERTS], C("tri"), member[:, t, :], True, t == 0)
                        if t:
                            mm(G[:, g % 2, 0:EXPERTS], ones, member[:, 0, :], False, True)
                            mm(G[:, g % 2, EXPERTS:2 * EXPERTS], ones, member[:, 0, :], True, False)
                            last = mm(G[:, g % 2, EXPERTS:2 * EXPERTS], ones, member[:, 1, :], False, True)
                        last.then_inc(g_done, 1)
                elif kind == "kvdown":
                    pe.wait_ge(t_evac, n.tg)
                    wide_ready(n.w)
                    wv = slot(n.w, KD, KVLORA + ROPE)
                    for t in range(T):
                        project(n.g + t, t, uT, KD, lambda k: wv[:, k, :], KVLORA + ROPE)
                    pe.wait_ge(dve_ready, n.dve + 3)
                    transposes(n.tg, [ckv[:, t, tok(k)] for k in range(2) for t in range(T)])
                    transposes(n.tg + 1, [krd[:, t, :] for t in range(T)])
                elif kind == "fox":
                    pe.wait_ge(t_evac, n.tg)
                    linear(n, 6, uhv, ulv, 2, open_banks(n), linear_bank, g_done, True, turned=(0, 1, 2, 3))
                    wide_ready(n.w + 6)
                    pe.wait_ge(s_attn, 48)
                    wv6 = slot(n.w + 6, KD, FOX_H)
                    for t in range(T):
                        g = n.g + 12 + t
                        open_g(g)
                        mm(G[:, g % 2, 0:FOX_H], ones[0:1, :], bfrow[0:1, :], True, False)
                        for k in range(KD):
                            mm(G[:, g % 2, 0:FOX_H], uhv[:, k, tok(t)].bitcast(F32), wv6[:, k, :], False, False)
                            last = mm(G[:, g % 2, 0:FOX_H], ulv[:, k, tok(t)].bitcast(F32), wv6[:, k, :], False, k == KD - 1)
                        last.then_inc(g_done, 1)
                    pe.wait_ge(dve_ready, n.dve + 2)
                    for t in range(T):
                        g = n.g + 14 + t
                        open_g(g)
                        last = mm(G[:, g % 2, 0:FOX_H], C("tri"), fls[:, t, :], True, t == 0)
                        if t:
                            last = mm(G[:, g % 2, 0:FOX_H], ones, fls[:, 0, :], False, True)
                        last.then_inc(g_done, 1)
                    pe.wait_ge(g_read, n.g + 12)
                    for t in range(T):
                        o = TB[0:FOX_H, n.tg % 2, tok(t)]
                        last = mm(o, fls[:, t, :], C("tri"), True, t == 0)
                        if t:
                            last = mm(o, fls[:, 0, :], ones, False, True)
                    last.then_inc(t_done, 1)
                    pe.wait_ge(t_evac, n.tg + 1)
                    pe.wait_ge(g_read, n.g + 16)

                    def fox_scores(o, t, h):
                        r = slice(FOX_D * (h % 2), FOX_D * (h % 2) + FOX_D)
                        mm(o, fqT[r, h // 2, tok(t)], fkT[r, h // 2, 0:P * (t + 1)], True, False)
                        return mm(o, ident[0:FOX_H, h:h + 1].to_broadcast([FOX_H, P]), ncT[0:FOX_H, 0:P * (t + 1)],
                                  False, True)

                    attention(n, n.g + 16, n.tg + 1, n.act + 2, FOX_H, None, fox_scores, FOX_D, n.free)
                elif kind == "mla":
                    pe.wait_ge(t_evac, n.tg)
                    wide_ready(n.w)
                    wv = slot(n.w, KD, QLORA)
                    for t in range(T):
                        project(n.g + t, t, uT, KD, lambda k: wv[:, k, :], QLORA)
                    pe.wait_ge(g_read, n.g + 2)
                    transposes(n.tg, [cq[:, t, tok(k)] for k in range(2) for t in range(T)])
                    transposes(n.tg + 1, [cq[:, t, tok(2)] for t in range(T)])
                    pe.wait_ge(t_evac, n.tg + 2)
                    for c in range(4):
                        wide_ready(n.w + 1 + c)
                        wv = slot(n.w + 1 + c, 3, 4 * (NOPE + ROPE))
                        wr = wide[(n.w + 1 + c) % RW][:, 0:12 * (NOPE + ROPE)].rearrange(
                            "p (k h d) -> p k h d", k=3, h=4)
                        g = n.g + 2 + 6 * c
                        for h in range(4):
                            project_T(g + h, lambda k: wr[:, k, h, 0:NOPE], cqT, 3)
                        for t in range(T):
                            project(g + 4 + t, t, cqT, 3, lambda k: wr[:, k, :, NOPE:NOPE + ROPE], 4 * ROPE)
                    pe.wait_ge(dve_ready, n.dve + 3)
                    for j in range(4):
                        transposes(n.tg + 2 + j, [qr_rot[:, t, 4 * j + 2 * a:4 * j + 2 * a + 2, :].rearrange(
                            "p h d -> p (h d)") for a in range(2) for t in range(T)])
                    for c in range(2):
                        wide_ready(n.w + 5 + c)
                        wr2 = wide[(n.w + 5 + c) % RW][:, :].rearrange("p (k h d) -> p k h d", k=2, h=8)
                        g = n.g + 26 + 12 * c
                        for h in range(8):
                            project_T(g + h, lambda k: wr2[:, k, h, 0:NOPE], ckvT, 2)
                        for q in range(2):
                            for t in range(T):
                                project(g + 8 + 2 * q + t, t, ckvT, 2,
                                        lambda k: wr2[:, k, 4 * q:4 * q + 4, NOPE:NOPE + VH], 4 * VH)
                    pe.wait_ge(t_evac, n.tg + 6)
                    pe.wait_ge(g_read, n.g + 50)

                    def mla_scores(o, t, h):
                        r = slice(ROPE * (h % 2), ROPE * (h % 2) + ROPE)
                        mm(o, qnT[:, h, tok(t)], knT[:, h, 0:P * (t + 1)], True, False)
                        return mm(o, qrT[r, h // 2, tok(t)], krT[r, 0:P * (t + 1)], False, True)

                    attention(n, n.g + 50, n.tg + 6, n.act + 2, MLA_H, None, mla_scores, VH, n.free)
                elif kind == "ple":
                    pe.wait_ge(t_evac, n.tg)
                    linear(n, 2, uhv, ulv, 2, open_banks(n), linear_bank, g_done, True)
                    pe.wait_ge(s_ple, 32 * (arg + 1))
                    pe.wait_ge(g_read, n.g + 4)
                    transposes(n.tg, [ptok[:, t, tok(k)] for k in range(2) for t in range(T)])
                    pe.wait_ge(t_evac, n.tg + 1)
                    pe.wait_ge(acc_free, n.free)
                    wide_ready(n.w + 2)
                    wv = slot(n.w + 2, 2, D)
                    for t in range(T):
                        for half in range(2):
                            for k in range(2):
                                last = mm(A[:, 2 * t + half, :], pT[:, k, tok(t)],
                                          wv[:, k, half * 512:(half + 1) * 512], k == 0, k == 1)
                    last.then_inc(acc_done, 1)

        @block.scalar
        def _(act):
            act.dma_start(cT, I["c"].rearrange("a (k p) -> p (a k)", p=P),
                          allow_slow_non_contiguous=True).then_inc(s_c, 16)
            step = [0]

            def link(ins):
                step[0] += 1
                ins.then_inc(act_step, 1)
                act.wait_ge(act_step, step[0])

            def evac(tg, dst, cols=4 * P, rows=P, func=ACT.Copy, scale=1.0):
                act.wait_ge(t_done, tg + 1)
                nc.scalar.activation(flat(dst), TB[0:rows, tg % 2, 0:cols], func, scale=scale).then_inc(t_evac, 1)

            def log_gate(g, dst, cols):
                act.wait_ge(g_done, g + 1)
                link(nc.scalar.activation(dst, G[:, g % 2, 0:cols], ACT.Abs))
                link(nc.scalar.activation(dst, dst, ACT.Exp, scale=-1.0))
                nc.scalar.activation(dst, dst, ACT.Ln, bias=1.0).then_inc(act_ready, 1)

            def sum_squares(g, t, h, cols, junk, signal):
                ins = nc.scalar.activation(junk, G[:, g % 2, h * cols:(h + 1) * cols], ACT.Square,
                                           accum_out=ssq[:, t, h:h + 1])
                if signal:
                    ins.then_inc(act_ready, 1)

            def attention(n, g0, tg0, act0):
                for i in range(33):
                    if i < 32:
                        t, h = divmod(i, 16)
                        act.wait_ge(g_read, g0 + i + 1)
                        nc.scalar.activation(probs[:, i % 2, 0:P * (t + 1)], scores[:, i % 2, 0:P * (t + 1)], ACT.Exp,
                                             bias=nmax[:, i % 2:i % 2 + 1], accum_out=rsum[:, t, h:h + 1]) \
                            .then_inc(act_ready, 1)
                    if i >= 1:
                        t = (i - 1) // 16
                        evac(tg0 + i - 1, pbT[:, (i - 1) % 2, 0:t + 1, :], P * (t + 1))

            def linear(n, pieces, done=None, done_of=None, ring=(l_hi[0][:, :], l_hi[1][:, :])):
                for p in pieces:
                    c, q = divmod(p, 4)
                    w = n.w + c
                    if q % 2 == 0:
                        half = wide_full2 if q else wide_full
                        act.wait_ge(half[w % RW], NEED_WIDE * (w // RW + 1))
                    depth = len(ring)
                    if p >= depth:
                        last_c, last_q = divmod(p - depth, 4)
                        if last_q == 3:
                            act.wait_ge(done, done_of(last_c))
                        else:
                            act.wait_ge(lin_used, n.lin + 3 * last_c + last_q + 1)
                    nc.scalar.activation(ring[p % depth], wide[w % RW][:, q * 1024:(q + 1) * 1024], ACT.Copy) \
                        .then_inc(hi_ready, 1)

            def rounder(n, past, third_free):
                def piece(j, c, q):
                    if q < 4:
                        w = n.w + j
                        act.wait_ge(wide_full[w % RW], ring_count((c - j) + past, w, RW, NEED_WIDE))
                        act.wait_ge(wide_full2[w % RW], ring_count((c - j) + past, w, RW, NEED_WIDE))
                        raw = wide[w % RW][:, q * 1024:(q + 1) * 1024]
                        if q < 3:
                            act.wait_ge(up_used, (c + past) * 3 + (3 * n.d - 2 + q)) if j or n.d else None
                        else:
                            third_free(j, c)
                    else:
                        d = n.d + j
                        act.wait_ge(down_full[d % RD], ring_count((c - j) + past, d, RD, 16))
                        raw = down[d % RD][:, (q - 4) * 1024:(q - 3) * 1024]
                        if n.d or j:
                            act.wait_ge(down_used if q == 5 else down0_used, (c + past) + n.d)
                    nc.scalar.activation(w_hi[q][:, :], raw, ACT.Copy).then_inc(hi_ready, 1)

                return piece

            def run_packed(n, i):
                past = i * PAIR
                g0 = i * G_PAIR + n.g

                def third_free(j, c):
                    act.wait_ge(g_done, g0 + (g_unit(j - 1) + 1 if j else 0))

                piece = rounder(n, past, third_free)

                def prepare(e):
                    for half in range(2):
                        g = g_prep(e) + 1 + half
                        act.wait_ge(g_done, g0 + (g + 1))
                        at = e * 1024 + half * 512
                        nc.scalar.activation(uh[:, at:at + 512], G[:, (n.g + g) % 2, :], ACT.Copy).then_inc(act_ready, 1)

                def outputs(e, c):
                    act.wait_ge(down_used, past + (n.d + c + 1))
                    if e:
                        act.wait_ge(scat_done, i * 4 + 2)
                    nc.scalar.activation(packed_out, A[:, 2 * e:2 * e + 2, :].rearrange("p h c -> p (h c)"), ACT.Copy) \
                        .then_inc(act_ready, 1)

                piece(0, 0, 0)
                piece(0, 0, 1)
                prepare(0)
                for c in range(PAIR):
                    piece(c, c, 2)
                    piece(c, c, 3)
                    if c:
                        piece(c - 1, c - 1, 4)
                        piece(c - 1, c - 1, 5)
                    if c < PAIR - 1:
                        piece(c + 1, c + 1, 0)
                        piece(c + 1, c + 1, 1)
                    act.wait_ge(g_done, g0 + (g_unit(c) + 1))
                    nc.scalar.activation(sgt[:, 0, :], G[:, (n.g + g_unit(c)) % 2, 0:FU], ACT.Silu).then_inc(act_ready, 1)
                    act.wait_ge(t_done, past + (c + n.tg + 1))
                    nc.scalar.activation(hth[:, 0:2 * P], TB[:, (n.tg + c) % 2, 0:2 * P], ACT.Copy).then_inc(act_ready, 1)
                    if c == PREP_AT:
                        prepare(1)
                    if c == NU:
                        outputs(0, NU - 1)
                piece(PAIR - 1, PAIR - 1, 4)
                piece(PAIR - 1, PAIR - 1, 5)
                outputs(1, PAIR - 1)

            def run(n, units, walk, past, early):
                piece = rounder(n, past, lambda j, c: act.wait_ge(g_done, (c + past) * 2 + n.g))

                def step(j, c):
                    if j == 0 and not early:
                        piece(0, c, 0)
                        piece(0, c, 1)
                    piece(j, c, 2)
                    piece(j, c, 3)
                    if j:
                        piece(j - 1, c - 1, 4)
                        piece(j - 1, c - 1, 5)
                    if j < units - 1:
                        piece(j + 1, c + 1, 0)
                        piece(j + 1, c + 1, 1)
                    for t in range(T):
                        act.wait_ge(g_done, (c + past) * 2 + (n.g + t + 1))
                        nc.scalar.activation(sgt[:, t, :], G[:, t, 0:FU], ACT.Silu).then_inc(act_ready, 1)
                    act.wait_ge(t_done, (c + past) + (n.tg + 1))
                    nc.scalar.activation(hth[:, :], TB[:, (n.tg + j) % 2, :], ACT.Copy).then_inc(act_ready, 1)

                walk(act, units, step)
                piece(units - 1, units - 1, 4)
                piece(units - 1, units - 1, 5)

            for index, (kind, arg, n, before) in enumerate(steps):
                if kind == "start":
                    act.wait_ge(s_c, 16)
                    link(nc.scalar.activation(condT, cT, ACT.Silu))
                elif kind == "ada":
                    if arg:
                        act.wait_ge(down_used, n.d)
                    nc.scalar.activation(cond_hi, condT.unsqueeze(2).to_broadcast([P, KD, P]), ACT.Copy) \
                        .then_inc(cond_rounded, 1)
                    linear(n, range(RW * 4), g_done, lambda c: n.g + c + 1, m_hi)
                    if arg == 0:
                        act.dma_start(x, I["x"][0].rearrange("(t p) c -> p t c", p=P)).then_inc(s_x, 16)
                    linear(n, range(RW * 4, 48), g_done, lambda c: n.g + c + 1, m_hi)
                elif kind in ("trs8", "trs16"):
                    next_kind, m = split_early(index)
                    if next_kind == "ffn":
                        for q in range(2):
                            rounder(m, 0, None)(0, 0, q)
                    elif next_kind:
                        if next_kind == "gla":
                            act.wait_ge(g_done, m.g)
                        linear(m, range(2))
                    groups = 4 if kind == "trs16" else 2
                    dst = (yh if kind == "trs16" else uh)[:, :].rearrange("p (k s) -> p k s", k=4 * groups)
                    for i in range(T * groups):
                        t, j = divmod(i, groups)
                        act.wait_ge(t_done, n.tg + i + 1)
                        nc.scalar.activation(dst[:, 4 * j:4 * j + 4, t * P:(t + 1) * P],
                                             TB[:, (n.tg + i) % 2, :].rearrange("p (k s) -> p k s", k=4), ACT.Copy) \
                            .then_inc(act_ready, 1)
                elif kind in ("out1", "out2"):
                    linear(n, range(2, 8 if kind == "out1" else 16), acc_done, lambda c: n.acc + c + 1)
                elif kind == "tr8":
                    for j in range(4):
                        evac(n.tg + j, uT[:, 2 * j:2 * j + 2, :])
                elif kind == "gla":
                    linear(n, range(2, 24), g_done, lambda c: n.g + 2 * c + 2)
                    evac(n.tg, glowT[0:RANK, :], S, RANK)
                    for t in range(T):
                        log_gate(n.g + 12 + t, lsg[:, t, :], KW)
                    evac(n.tg + 1, small[:, 52:60], 8, P, ACT.Exp)
                    act.wait_ge(dve_ready, n.dve + 3)
                    for t in range(T):
                        g = n.g + 16 + t
                        act.wait_ge(g_done, g + 1)
                        nc.scalar.activation(e3[:, t, 0:2 * KW], G[:, g % 2, 0:2 * KW], ACT.Exp)
                        nc.scalar.activation(e3[:, t, 2 * KW:3 * KW], G[:, g % 2, 0:KW], ACT.Exp, scale=-1.0) \
                            .then_inc(act_ready, 1)
                    evac(n.tg + 2, gqT)
                    evac(n.tg + 3, gkT)
                    for t in range(T):
                        act.wait_ge(g_read, n.g + 16)
                        nc.scalar.activation(proj[:, t, C_H:C_H + VW], proj[:, t, C_G:C_G + VW], ACT.Silu) \
                            .then_inc(act_ready, 1)
                    for t in range(T):
                        g = n.g + 20 + t
                        act.wait_ge(g_done, g + 1)
                        for h in range(HEADS):
                            sum_squares(g, t, h, DV, hbuf[:, t * VW + h * DV:t * VW + (h + 1) * DV], h == HEADS - 1)
                elif kind == "ffn":
                    run(n, NU, roll, 0, split_early(index - 1)[0])
                elif kind == "moe":
                    act.wait_ge(dve_ready, n.dve)
                    full = act.value_load(crowded[0:1, 0:1], min_val=0, max_val=1)
                    with act.If(full == 0):
                        with act.Fori(0, EXPERTS // 2) as i:
                            run_packed(n, i)
                        act.drain().then_inc(act_ready, 3 * NU * EXPERTS - ACT_PAIR * (EXPERTS // 2))
                    with act.Else():
                        with act.Fori(0, EXPERTS // 2) as i:
                            run(n, PAIR, straight, i * PAIR, None)
                elif kind == "router":
                    act.wait_ge(dve_ready, n.dve + 1)
                    nc.scalar.activation(e2, gap, ACT.Exp).then_inc(act_ready, 1)
                elif kind == "kvdown":
                    for t in range(T):
                        act.wait_ge(g_done, n.g + t + 1)
                        sum_squares(n.g + t, t, 0, KVLORA, sg[:, t * KVLORA:(t + 1) * KVLORA], True)
                    evac(n.tg, ckvT)
                    evac(n.tg + 1, krT, S)
                elif kind == "fox":
                    linear(n, range(2, 24), g_done, lambda c: n.g + 2 * c + 2)
                    for t in range(T):
                        log_gate(n.g + 12 + t, flt[:, t, :], FOX_H)
                    evac(n.tg, ncT[0:FOX_H, :], S, FOX_H, ACT.Copy, -1.0)
                    attention(n, n.g + 16, n.tg + 1, n.act + 2)
                elif kind == "mla":
                    for t in range(T):
                        act.wait_ge(g_done, n.g + t + 1)
                        sum_squares(n.g + t, t, 0, QLORA, hbuf[:, t * QLORA:(t + 1) * QLORA], True)
                    evac(n.tg, cqT[:, 0:2, :])
                    evac(n.tg + 1, cqT[:, 2, :], S)
                    for j in range(4):
                        evac(n.tg + 2 + j, qrT[:, 2 * j:2 * j + 2, :])
                    attention(n, n.g + 50, n.tg + 6, n.act + 2)
                elif kind == "ple":
                    linear(n, range(2, 8), g_done, lambda c: n.g + 2 * c + 2)
                    evac(n.tg, pT)
                    for t in range(T):
                        act.wait_ge(g_read, n.g + 3 + t)
                        nc.scalar.activation(gt[:, t, :], gt[:, t, :], ACT.Sigmoid).then_inc(act_ready, 1)

        @block.gpsimd
        def _(pool):
            def bc(row):
                return row.partition_broadcast(P)

            def load_ln(s):
                if s < 2 * DEPTH:
                    name = ("ln1", "ln2")[s % 2]
                    rows = I[f"{name}_g"][s // 2], I[f"{name}_b"][s // 2]
                elif s < 6 * DEPTH:
                    i, j = divmod(s - 2 * DEPTH, 4)
                    rows = I["ln_g_2"][i, j], I["ln_b_2"][i, j]
                else:
                    return
                for half, row in enumerate(rows):
                    pool.dma_start(lnp[:, half * D:(half + 1) * D], bc(row)).then_inc(s_ln, 16)

            def load_gla(l):
                pool.dma_start(convw, bc(I["conv_w"][l])).then_inc(s_gla, 16)
                pool.dma_start(gnw, bc(I["gla_norm_w"][l])).then_inc(s_gla, 16)
                pool.dma_start(gkw2[0:RANK, :], I["gk_w2"][l]).then_inc(s_gla, 16)
                pool.dma_start(gkb[0:1, :], I["gk_b"][l:l + 1]).then_inc(s_gla, 16)

            def load_ada(l):
                for row in range(6):
                    pool.dma_start(mod[:, row, :], bc(I["ada_b"][l, row * D:(row + 1) * D])).then_inc(s_ada[row], 16)

            def load_ple(i):
                pool.dma_start(bgate, bc(I["ple_b_gate_2"][i])).then_inc(s_ple, 16)
                pool.dma_start(ptok, I["p_2"][i, 0].rearrange("(t p) c -> p t c", p=P)).then_inc(s_ple, 16)

            def root(dve, width):
                a = CONST_COLS["minushalf"][0]
                for t in range(T):
                    pool.wait_ge(dve_ready, dve + t + 1)
                    nc.gpsimd.tensor_tensor(rstd[:, t, 0:width], ve[:, t, 0:width], con[:, a:a + width],
                                            ALU.pow).then_inc(pool_ready, 1)

            load_ada(0)
            pool.wait_ge(g_done, 2)
            load_gla(0)
            load_ln(0)
            pool.dma_start(routw[:, :].rearrange("p (k e) -> p k e", k=KD),
                           I["router_w"][0].rearrange("(k p) e -> p k e", p=P)).then_inc(s_rout, 16)
            pool.wait_ge(s_con, 16)
            for kind, arg, n, _ in steps:
                if kind == "gla":
                    root(n.dve + 4, HEADS)
                elif kind in ("kvdown", "mla"):
                    root(n.dve, 1)
                elif kind == "ln":
                    root(n.dve, 1)
                    pool.wait_ge(src_ready, n.src + 2)
                    load_ln(n.ln + 1)
                    if n.ln == 1:
                        load_gla(1)
                        load_ada(1)
                    if n.ln == 2 * DEPTH - 1:
                        pool.dma_start(qnw, bc(I["mla_q_norm_2"][0])).then_inc(s_attn, 16)
                        pool.dma_start(kvnw, bc(I["kv_norm_2"])).then_inc(s_attn, 16)
                        pool.dma_start(bfrow[0:1, :], I["fox_b_f_2"]).then_inc(s_attn, 16)
                    if n.ln >= 2 * DEPTH and n.ln % 4 == 2:
                        load_ple((n.ln - 2 * DEPTH) // 4)

        @block.vector
        def _(dve):
            V = nc.vector
            step = [0]

            def link(ins):
                step[0] += 1
                ins.then_inc(dve_step, 1)
                dve.wait_ge(dve_step, step[0])

            def copy_out(g, dst, cols, scale=None):
                dve.wait_ge(g_done, g + 1)
                if scale is None:
                    V.tensor_copy(flat(dst), G[:, g % 2, 0:cols]).then_inc(g_read, 1)
                else:
                    V.tensor_scalar(dst, G[:, g % 2, 0:cols], scale, None, ALU.mult).then_inc(g_read, 1)

            def log_sigmoid(g, scratch, cols, a):
                dve.wait_ge(act_ready, a)
                V.scalar_tensor_tensor(out=scratch, in0=G[:, g % 2, 0:cols], scalar=0.0, in1=scratch,
                                       op0=ALU.min, op1=ALU.subtract).then_inc(g_read, 1)
                dve.wait_ge(g_read, g + 1)

            def mean_eps(t, width, size, a):
                dve.wait_ge(act_ready, a)
                V.tensor_scalar(ve[:, t, 0:width], ssq[:, t, 0:width], 1.0 / size, RMS_EPS,
                                ALU.mult, ALU.add).then_inc(dve_ready, 1)

            def rope(dst, lo, hi, cos, sin, t1):
                half = ROPE // 2
                link(V.tensor_tensor(t1, hi, sin, ALU.mult))
                link(V.tensor_tensor(dst[0], lo, cos, ALU.mult))
                link(V.tensor_tensor(dst[0], dst[0], t1, ALU.subtract))
                link(V.tensor_tensor(t1, lo, sin, ALU.mult))
                link(V.tensor_tensor(dst[1], hi, cos, ALU.mult))
                return V.tensor_tensor(dst[1], dst[1], t1, ALU.add)

            def attention(n, g0, fox):
                for i in range(32):
                    t, h = divmod(i, 16)
                    g, cols = g0 + i, P * (t + 1)
                    dve.wait_ge(g_done, g + 1)
                    sc = scores[:, i % 2, 0:cols]
                    if i >= 2:
                        dve.wait_ge(act_ready, n.act + 2 + i - 1)
                    if fox:
                        scalar, op = cumf[:, t, h:h + 1], ALU.add
                    else:
                        scalar, op = float((NOPE + ROPE) ** -0.5), ALU.mult
                    if t:
                        link(V.tensor_scalar(sc[:, 0:P], G[:, g % 2, 0:P], scalar, None, op))
                    link(V.scalar_tensor_tensor(out=sc[:, t * P:cols], in0=G[:, g % 2, t * P:cols], scalar=scalar,
                                                in1=C("causal"), op0=op, op1=ALU.add))
                    V.tensor_reduce(nmax[:, i % 2:i % 2 + 1], sc, AX.X, ALU.max, negate=True).then_inc(g_read, 1)
                    if i == 31:
                        weighted(n, 1, fox)
                    elif i == 17 and not fox:
                        weighted(n, 0, fox)

            def weighted(n, t, fox):
                dve.wait_ge(acc_done, n.acc + (1 if fox or t == 0 else 2))
                dve.wait_ge(act_ready, n.act + 2 + 16 * (t + 1))
                if fox:
                    link(V.reciprocal(rinv[:, :, :], rsum[:, :, :]))
                    for b in range(4):
                        tt, half = divmod(b, 2)
                        last = V.tensor_tensor(
                            src[:, tt, half * 512:(half + 1) * 512].rearrange("p (h d) -> p h d", h=8),
                            A[:, b, :].rearrange("p (h d) -> p h d", h=8),
                            rinv[:, tt, half * 8:half * 8 + 8].unsqueeze(2).to_broadcast([P, 8, FOX_D]), ALU.mult)
                    last.then_inc(acc_free, 1)
                    dve.wait_ge(acc_free, n.free + 1)
                else:
                    link(V.reciprocal(rinv[:, t, :], rsum[:, t, :]))
                    for b in range(4):
                        last = V.tensor_tensor(
                            src2[:, t, b * 512:(b + 1) * 512].rearrange("p (h d) -> p h d", h=4),
                            A[:, b, :].rearrange("p (h d) -> p h d", h=4),
                            rinv[:, t, b * 4:b * 4 + 4].unsqueeze(2).to_broadcast([P, 4, VH]), ALU.mult)
                    last.then_inc(acc_free, 1)
                    dve.wait_ge(acc_free, n.free + 1 + t)

            def linear_rest(n, c, q, hi=(l_hi[0][:, :], l_hi[1][:, :]), lo=(l_lo[0][:, :], l_lo[1][:, :])):
                at = (4 * c + q) % len(hi)
                dve.wait_ge(hi_ready, n.lo + 4 * c + q + 1)
                V.tensor_tensor(lo[at], wide[(n.w + c) % RW][:, q * 1024:(q + 1) * 1024], hi[at].bitcast(F32),
                                ALU.subtract).then_inc(lo_ready, 1)

            def linear(n, chunks, evac):
                for c in range(chunks + 1):
                    for q in range(4):
                        if c < chunks and (c or q >= 2):
                            linear_rest(n, c, q)
                        if q == 1 and c and evac:
                            for b in range(2):
                                dve.wait_ge(g_done, n.g + 2 * (c - 1) + b + 1)
                                evac(c - 1, b).then_inc(g_read, 1)

            def resters(n, units, past):
                def piece(j, c, q):
                    if q < 4:
                        raw = wide[(n.w + j) % RW][:, q * 1024:(q + 1) * 1024]
                        count = up_pieces(c, q)
                    else:
                        raw = down[(n.d + j) % RD][:, (q - 4) * 1024:(q - 3) * 1024]
                        count = down_pieces(c, q - 4, units)
                    dve.wait_ge(hi_ready, past * 6 + count + n.lo)
                    V.tensor_tensor(w_lo[q][:, :], raw, w_hi[q][:, :].bitcast(F32), ALU.subtract).then_inc(lo_ready, 1)

                return piece

            def run_packed(n, i):
                past = i * PAIR
                g0, a0 = i * G_PAIR + n.g, i * ACT_PAIR + n.act
                piece = resters(n, PAIR, past)

                def one_hots(e):
                    col = bass.ds(i * 2 + e, 1)
                    for t in range(T):
                        V.tensor_scalar(pick[:, t, :], C("slots"), slotid[:, t, col], None, ALU.is_equal)
                        last = V.tensor_scalar(pick_w[:, t, :], C("slots"), slotid[:, t, col], route[:, t, col],
                                               ALU.is_equal, ALU.mult)
                    last.then_inc(pick_ready, 1)

                def prepare(e):
                    g = g_prep(e)
                    dve.wait_ge(g_done, g0 + (g + 1))
                    V.tensor_copy(put_back[:, e, :], G[:, (n.g + g) % 2, 0:2 * P]).then_inc(g_read, 1)
                    for half in range(2):
                        dve.wait_ge(act_ready, a0 + a_prep(e, half))
                        at = e * 1024 + half * 512
                        V.tensor_tensor(ul[:, at:at + 512], G[:, (n.g + g + 1 + half) % 2, :],
                                        uh[:, at:at + 512].bitcast(F32), ALU.subtract).then_inc(g_read, 1)

                def add(t, k, banks):
                    dve.wait_ge(scat_done, i * 4 + k)
                    V.tensor_tensor(moe_sum[:, t, :], moe_sum[:, t, :],
                                    A[:, banks:banks + 2, :].rearrange("p h c -> p (h c)"), ALU.add) \
                        .then_inc(acc_free if t else scat_read, 1)

                dve.wait_ge(acc_free, i * 2 + n.free)
                one_hots(0)
                piece(0, 0, 0)
                piece(0, 0, 1)
                prepare(0)
                for c in range(PAIR):
                    piece(c, c, 2)
                    piece(c, c, 3)
                    if c:
                        piece(c - 1, c - 1, 4)
                        piece(c - 1, c - 1, 5)
                    if c < PAIR - 1:
                        piece(c + 1, c + 1, 0)
                        piece(c + 1, c + 1, 1)
                    dve.wait_ge(act_ready, a0 + a_silu(c))
                    V.tensor_tensor(hid[:, 0, 0, :], sgt[:, 0, :], G[:, (n.g + g_unit(c)) % 2, FU:2 * FU], ALU.mult) \
                        .then_inc(g_read, 1)
                    dve.wait_ge(act_ready, a0 + (a_silu(c) + 1))
                    V.tensor_tensor(htl[:, 0:2 * P], TB[:, (n.tg + c) % 2, 0:2 * P], hth[:, 0:2 * P].bitcast(F32),
                                    ALU.subtract).then_inc(t_evac, 1)
                    if c == PREP_AT - 1:
                        one_hots(1)
                    if c == PREP_AT:
                        prepare(1)
                    if c == NU + 1:
                        add(0, 1, 0)
                    if c == NU + 2:
                        add(1, 2, 0)
                piece(PAIR - 1, PAIR - 1, 4)
                piece(PAIR - 1, PAIR - 1, 5)
                dve.wait_ge(scat_read, i * 2 + 1)
                add(0, 3, 2)
                dve.wait_ge(acc_free, i * 2 + (n.free + 1))
                add(1, 4, 0)

            def run(n, units, walk, past, route_of, drain_after, drained, early):
                piece = resters(n, units, past)

                def step(j, c):
                    if j == 0 and not early:
                        piece(0, c, 0)
                        piece(0, c, 1)
                    piece(j, c, 2)
                    piece(j, c, 3)
                    if j:
                        piece(j - 1, c - 1, 4)
                        piece(j - 1, c - 1, 5)
                    if j < units - 1:
                        piece(j + 1, c + 1, 0)
                        piece(j + 1, c + 1, 1)
                    for t in range(T):
                        dve.wait_ge(act_ready, (c + past) * 3 + (n.act + t + 1))
                        if route_of:
                            ins = V.scalar_tensor_tensor(out=hid[:, 0, t, :], in0=sgt[:, t, :], scalar=route_of(j, t),
                                                         in1=G[:, t, FU:2 * FU], op0=ALU.mult, op1=ALU.mult)
                        else:
                            ins = V.tensor_tensor(hid[:, 0, t, :], sgt[:, t, :], G[:, t, FU:2 * FU], ALU.mult)
                        ins.then_inc(g_read, 1)
                    dve.wait_ge(act_ready, (c + past) * 3 + (n.act + 3))
                    V.tensor_tensor(htl[:, :], TB[:, (n.tg + j) % 2, :], hth[:, :].bitcast(F32), ALU.subtract) \
                        .then_inc(t_evac, 1)
                    if j - 1 in drain_after:
                        drain(j - 1, c - 1)

                def drain(j, c):
                    dve.wait_ge(down_used, (c + past) + (n.d + 1))
                    dve.wait_ge(acc_free, drained(j))
                    for t in range(T):
                        acc = A[:, 2 * t:2 * t + 2, :].rearrange("p h c -> p (h c)")
                        last = V.tensor_tensor(moe_sum[:, t, :], moe_sum[:, t, :], acc, ALU.add)
                    last.then_inc(acc_free, 1)

                walk(dve, units, step)
                piece(units - 1, units - 1, 4)
                piece(units - 1, units - 1, 5)
                if units - 1 in drain_after:
                    drain(units - 1, units - 1)

            for index, (kind, arg, n, before) in enumerate(steps):
                if kind == "start":
                    pass
                elif kind == "ada":
                    dve.wait_ge(cond_rounded, arg + 1)
                    V.tensor_tensor(cond_lo, condT.unsqueeze(2).to_broadcast([P, KD, P]), cond_hi.bitcast(F32),
                                    ALU.subtract).then_inc(cond_ready, 1)
                    for c in range(13):
                        for q in range(4):
                            if c < 12:
                                linear_rest(n, c, q, m_hi, m_lo)
                            if q == 1 and c:
                                b = c - 1
                                dst = mod[:, b // 2, (b % 2) * 512:(b % 2 + 1) * 512]
                                dve.wait_ge(s_ada[b // 2], 16 * (arg + 1))
                                dve.wait_ge(g_done, n.g + b + 1)
                                V.tensor_tensor(dst, G[:, (n.g + b) % 2, :], dst, ALU.add).then_inc(g_read, 1)
                    dve.wait_ge(g_read, n.g + 12)
                    if arg == 0:
                        dve.wait_ge(s_con, 16)
                        dve.wait_ge(s_x, 16)
                elif kind == "mod":
                    for t in range(T):
                        link(V.scalar_tensor_tensor(out=src[:, t, :], in0=mod[:, arg + 1, :], scalar=1.0, in1=x[:, t, :],
                                                    op0=ALU.add, op1=ALU.mult))
                        V.tensor_tensor(src[:, t, :], src[:, t, :], mod[:, arg, :], ALU.add).then_inc(src_ready, 1)
                elif kind == "gla":
                    linear(n, 6, lambda c, b: V.tensor_copy(proj[:, b, c * 512:(c + 1) * 512], linear_bank(c, b)))
                    dve.wait_ge(g_read, n.g + 12)
                    dve.wait_ge(t_done, n.tg + 1)
                    dve.wait_ge(s_gla, 64 * (arg + 1))
                    for t in range(T):
                        zc = proj[:, t, C_C:C_C + CONV]
                        link(V.tensor_tensor(zc, zc, proj[:, t, C_H:C_H + CONV], ALU.mult))
                        link(V.tensor_tensor(proj[:, t, C_H:C_H + CONV], zc, convw[:, 0, :], ALU.mult))
                        link(V.tensor_tensor(z1[:, t, :], zc, convw[:, 1, :], ALU.mult))
                        last = V.tensor_tensor(zc, zc, convw[:, 2, :], ALU.mult)
                    last.then_inc(dve_ready, 1)
                    for t in range(T):
                        log_sigmoid(n.g + 12 + t, lsg[:, t, :], KW, n.act + 1 + t)
                        V.tensor_scalar(gk[:, t, :], lsg[:, t, :], 1.0 / 16.0, -1.0, ALU.mult, ALU.max) \
                            .then_inc(dve_ready, 1)
                    for t in range(T):
                        g = n.g + 14 + t
                        dve.wait_ge(g_done, g + 1)
                        V.tensor_tensor(src[:, t, 0:CONV], G[:, g % 2, :], proj[:, t, C_B:C_B + CONV], ALU.mult) \
                            .then_inc(g_read, 1)
                    for t in range(T):
                        g = n.g + 16 + t
                        dve.wait_ge(act_ready, n.act + 3 + t)
                        q, k = proj[:, t, C_Q:C_Q + KW], proj[:, t, C_K:C_K + KW]
                        V.scalar_tensor_tensor(out=q, in0=q, scalar=DK ** -0.5, in1=e3[:, t, 0:KW],
                                               op0=ALU.mult, op1=ALU.mult)
                        link(V.tensor_tensor(proj[:, t, C_C:C_C + KW], k, e3[:, t, 2 * KW:3 * KW], ALU.mult))
                        V.tensor_tensor(k, k, e3[:, t, KW:2 * KW], ALU.mult).then_inc(g_read, 1)
                    dve.wait_ge(g_read, n.g + 18)
                    link(V.memset(state, 0.0))
                    dve.wait_ge(acc_done, n.acc + 1)
                    dve.wait_ge(t_evac, n.tg + 2)
                    for c in range(3):
                        for f in range(2):
                            r = slice(DK * f, DK * f + DK)
                            for a in range(2):
                                kv = A[r, c, a * KW + f * DV:a * KW + (f + 1) * DV]
                                if c == 0:
                                    last = V.tensor_copy(state[r, 0, a, f * DV:(f + 1) * DV], kv)
                                else:
                                    last = V.scalar_tensor_tensor(out=state[r, c, a, f * DV:(f + 1) * DV],
                                                                  in0=state[r, c - 1, a, f * DV:(f + 1) * DV],
                                                                  scalar=dec[r, c // 2, a, c % 2:c % 2 + 1], in1=kv,
                                                                  op0=ALU.mult, op1=ALU.add)
                        if c < 2:
                            link(last)
                    last.then_inc(dve_ready, 1)
                    V.tensor_copy(ve[0:1, 0, 0:1], A[0:1, 0, 0:1]).then_inc(acc_free, 1)
                    for f in range(2):
                        g = n.g + 18 + f
                        dve.wait_ge(g_done, g + 1)
                        V.tensor_tensor(stm[:, f], G[:, g % 2, :].rearrange("p (h i) -> p h i", h=HEADS),
                                        C("cum").unsqueeze(1).to_broadcast([P, HEADS, P]), ALU.mult).then_inc(g_read, 1)
                    dve.wait_ge(acc_free, n.free + 1)
                    for t in range(T):
                        mean_eps(t, HEADS, DV, n.act + 7 + t)
                    for t in range(T):
                        g = n.g + 20 + t
                        dve.wait_ge(pool_ready, n.pool + t + 1)
                        y = src[:, t, CONV:CONV + VW]
                        for h in range(HEADS):
                            last = V.scalar_tensor_tensor(out=y[:, h * DV:(h + 1) * DV], in0=G[:, g % 2, h * DV:(h + 1) * DV],
                                                          scalar=rstd[:, t, h:h + 1], in1=gnw, op0=ALU.mult, op1=ALU.mult)
                        last.then_inc(g_read, 1)
                        dve.wait_ge(g_read, g + 1)
                        V.tensor_tensor(y, y, proj[:, t, C_H:C_H + VW], ALU.mult).then_inc(src_ready, 1)
                elif kind == "ln":
                    how, which = arg
                    if before == "moe":
                        dve.wait_ge(acc_free, n.free)
                    elif before != "ffn":
                        dve.wait_ge(acc_done, n.acc)
                    for t in range(T):
                        acc = A[:, 2 * t:2 * t + 2, :].rearrange("p h c -> p (h c)")
                        if before == "moe":
                            acc = moe_sum[:, t, :]
                        xt = x[:, t, :]
                        if before == "ffn":
                            dve.wait_ge(down_used if t else down0_used, n.d)
                        if how in ("mod", "gate"):
                            delta = src[:, t, :]
                            if how == "mod":
                                link(V.scalar_tensor_tensor(out=delta, in0=mod[:, which, :], scalar=1.0, in1=acc,
                                                            op0=ALU.add, op1=ALU.mult))
                            else:
                                dve.wait_ge(act_ready, n.act - 1 + t)
                                link(V.tensor_tensor(delta, gt[:, t, :], acc, ALU.mult))
                            link(V.scalar_tensor_tensor(out=xt, in0=xt, scalar=ALPHA, in1=delta, op0=ALU.mult, op1=ALU.add))
                        elif how == "half":
                            link(V.scalar_tensor_tensor(out=xt, in0=xt, scalar=2.0 * ALPHA, in1=acc, op0=ALU.mult,
                                                        op1=ALU.add))
                        else:
                            link(V.scalar_tensor_tensor(out=xt, in0=xt, scalar=ALPHA, in1=acc, op0=ALU.mult, op1=ALU.add))
                        for half in range(2):
                            last = V.bn_stats(stats[:, t, half, :], x[:, t, half * 512:(half + 1) * 512])
                        link(last)
                        link(V.bn_aggr(mv[:, t, :], stats[:, t].rearrange("p c s -> p (c s)")))
                        V.tensor_scalar(ve[:, t, 0:1], mv[:, t, 1:2], (4.0 if how == "half" else 1.0) * LN_EPS, None, ALU.add).then_inc(dve_ready, 1)
                    V.tensor_copy(nmax[0:1, 0:1], mv[0:1, 0, 0:1]).then_inc(acc_free, 1)
                    dve.wait_ge(s_ln, 32 * (n.ln + 1))
                    for t in range(T):
                        xt = x[:, t, :]
                        link(V.scalar_tensor_tensor(out=xt, in0=xt, scalar=mv[:, t, 0:1], in1=lnp[:, 0:D],
                                                    op0=ALU.subtract, op1=ALU.mult))
                        dve.wait_ge(pool_ready, n.pool + t + 1)
                        V.scalar_tensor_tensor(out=xt, in0=xt, scalar=rstd[:, t, 0:1], in1=lnp[:, D:2 * D],
                                               op0=ALU.mult, op1=ALU.add).then_inc(src_ready, 1)
                    dve.wait_ge(src_ready, n.src + 2)
                elif kind == "ffn":
                    run(n, NU, roll, 0, None, (), None, split_early(index - 1)[0])
                elif kind == "moe":
                    link(V.memset(moe_sum, 0.0))
                    dve.wait_ge(dve_ready, n.dve)
                    full = dve.value_load(crowded[0:1, 0:1], min_val=0, max_val=1)
                    with dve.If(full == 0):
                        with dve.Fori(0, EXPERTS // 2) as i:
                            run_packed(n, i)
                        dve.drain().then_inc(g_read, 2 * NU * EXPERTS - G_PAIR * (EXPERTS // 2))
                    with dve.Else():
                      with dve.Fori(0, EXPERTS // 2) as i:
                        run(n, PAIR, straight, i * PAIR, lambda j, t: route[:, t, bass.ds(i * 2 + j // NU, 1)],
                            (NU - 1, PAIR - 1), lambda j: i * 2 + (n.free + j // NU), None)
                elif kind in ("out1", "out2"):
                    linear(n, 2 if kind == "out1" else 4, None)
                elif kind in ("trs8", "trs16"):
                    next_kind, m = split_early(index)

                    def early_rest(q):
                        if next_kind == "ffn":
                            resters(m, NU, 0)(0, 0, q)
                        elif next_kind:
                            linear_rest(m, 0, q)

                    groups = 4 if kind == "trs16" else 2
                    hi, lo = (v[:, :].rearrange("p (k s) -> p k s", k=4 * groups)
                              for v in ((yh, yl) if kind == "trs16" else (uh, ul)))
                    for i in range(T * groups):
                        t, j = divmod(i, groups)
                        if i == groups:
                            early_rest(0)
                        at = (slice(None), slice(4 * j, 4 * j + 4), slice(t * P, (t + 1) * P))
                        dve.wait_ge(act_ready, n.act + i + 1)
                        V.tensor_tensor(lo[at], TB[:, (n.tg + i) % 2, :].rearrange("p (k s) -> p k s", k=4),
                                        hi[at].bitcast(F32), ALU.subtract).then_inc(t_evac, 1)
                    early_rest(1)
                elif kind == "router":
                    for t in range(T):
                        copy_out(n.g + t, logit[:, t, :], EXPERTS)
                    dve.wait_ge(g_read, n.g + 2)
                    for t in range(T):
                        link(V.max(top8[:, t, :], logit[:, t, :]))
                        link(V.max_index(idx8[:, t * 8:(t + 1) * 8], top8[:, t, :], logit[:, t, :]))
                        link(V.tensor_copy(idxf[:, t, :], idx8[:, t * 8:(t + 1) * 8]))
                        last = V.tensor_tensor(gap[:, t:t + 1], top8[:, t, 1:2], top8[:, t, 0:1], ALU.subtract)
                    last.then_inc(dve_ready, 1)
                    dve.wait_ge(act_ready, n.act + 1)
                    link(V.tensor_scalar(w1, e2, 1.0, None, ALU.add))
                    link(V.reciprocal(w1, w1))
                    link(V.tensor_tensor(w2, e2, w1, ALU.mult))
                    for t in range(T):
                        link(V.tensor_scalar(rtmp[:, t, :], C("experts"), idxf[:, t, 1:2], None, ALU.is_equal))
                        link(V.scalar_tensor_tensor(out=member[:, t, :], in0=C("experts"), scalar=idxf[:, t, 0:1],
                                                    in1=rtmp[:, t, :], op0=ALU.is_equal, op1=ALU.add))
                    V.tensor_copy(nmax[0:1, 0:1], w1[0:1, 0:1]).then_inc(dve_ready, 1)
                    for t in range(T):
                        link(V.tensor_scalar(rtmp[:, t, :], C("experts"), idxf[:, t, 0:1], w1[:, t:t + 1],
                                             ALU.is_equal, ALU.mult))
                        link(V.tensor_scalar(route[:, t, :], C("experts"), idxf[:, t, 1:2], w2[:, t:t + 1],
                                             ALU.is_equal, ALU.mult))
                        link(V.tensor_tensor(route[:, t, :], route[:, t, :], rtmp[:, t, :], ALU.add))
                    for t in range(T):
                        g = n.g + 2 + t
                        dve.wait_ge(g_done, g + 1)
                        link(V.tensor_tensor(slotid[:, t, :], G[:, g % 2, 0:EXPERTS], member[:, t, :], ALU.mult))
                        if t:
                            link(V.tensor_reduce(gap[:, 0:1], G[:, g % 2, EXPERTS:2 * EXPERTS], AX.X, ALU.max))
                        link(V.tensor_scalar(slotid[:, t, :], slotid[:, t, :], -1.0, None, ALU.add))
                        V.tensor_copy(nmax[0:1, 0:1], G[0:1, g % 2, 0:1]).then_inc(g_read, 1)
                    V.tensor_scalar(crowded[:, :], gap[:, 0:1], float(P), None, ALU.is_gt).then_inc(dve_ready, 1)
                elif kind == "kvdown":
                    dve.wait_ge(s_attn, 48)
                    for t in range(T):
                        mean_eps(t, 1, KVLORA, n.act + 1 + t)
                    half = ROPE // 2
                    for t in range(T):
                        g = n.g + t
                        cos = C("cos").rearrange("p (t c) -> p t c", t=T)[:, t, :]
                        sin = C("sin").rearrange("p (t c) -> p t c", t=T)[:, t, :]
                        link(rope((krd[:, t, 0:half], krd[:, t, half:ROPE]), G[:, g % 2, KVLORA:KVLORA + half],
                                  G[:, g % 2, KVLORA + half:KVLORA + ROPE], cos, sin, rinv[:, :, :].rearrange("p a b -> p (a b)")))
                        link(V.tensor_copy(krd[:, t, ROPE:2 * ROPE], krd[:, t, 0:ROPE]))
                        dve.wait_ge(pool_ready, n.pool + t + 1)
                        V.scalar_tensor_tensor(out=ckv[:, t, :], in0=G[:, g % 2, 0:KVLORA], scalar=rstd[:, t, 0:1], in1=kvnw,
                                               op0=ALU.mult, op1=ALU.mult).then_inc(g_read, 1)
                    V.tensor_copy(nmax[0:1, 0:1], rstd[0:1, 0, 0:1]).then_inc(dve_ready, 1)
                elif kind == "fox":
                    def read_out(c, b):
                        if c < 2:
                            at = 4 * c + 2 * b
                            return V.tensor_scalar(flat(fqT[:, at:at + 2, :]), linear_bank(c, b), FOX_D ** -0.5, None,
                                                   ALU.mult)
                        if c < 4:
                            at = 4 * (c - 2) + 2 * b
                            return V.tensor_copy(flat(fkT[:, at:at + 2, :]), linear_bank(c, b))
                        return V.tensor_copy(fv[:, b, (c - 4) * 512:(c - 3) * 512], linear_bank(c, b))

                    linear(n, 6, read_out)
                    for t in range(T):
                        log_sigmoid(n.g + 12 + t, flt[:, t, :], FOX_H, n.act + 1 + t)
                        V.tensor_copy(fls[:, t, :], flt[:, t, :]).then_inc(dve_ready, 1)
                    for t in range(T):
                        copy_out(n.g + 14 + t, cumf[:, t, :], FOX_H)
                    dve.wait_ge(g_read, n.g + 16)
                    attention(n, n.g + 16, True)
                    V.tensor_copy(nmax[0:1, 0:1], rinv[0:1, 0, 0:1]).then_inc(src_ready, T)
                elif kind == "mla":
                    for t in range(T):
                        mean_eps(t, 1, QLORA, n.act + 1 + t)
                    for t in range(T):
                        g = n.g + t
                        dve.wait_ge(pool_ready, n.pool + t + 1)
                        V.scalar_tensor_tensor(out=cq[:, t, :], in0=G[:, g % 2, 0:QLORA], scalar=rstd[:, t, 0:1], in1=qnw,
                                               op0=ALU.mult, op1=ALU.mult).then_inc(g_read, 1)
                    for c in range(4):
                        g = n.g + 2 + 6 * c
                        for h in range(4):
                            copy_out(g + h, qnT[:, 4 * c + h, :], S)
                        for t in range(T):
                            copy_out(g + 4 + t, qr_raw[:, t, 4 * c:4 * c + 4, :], 4 * ROPE)
                    dve.wait_ge(g_read, n.g + 26)
                    half = ROPE // 2
                    for t in range(T):
                        cos = C("cos").rearrange("p (t c) -> p t c", t=T)[:, t:t + 1, :].to_broadcast([P, MLA_H, half])
                        sin = C("sin").rearrange("p (t c) -> p t c", t=T)[:, t:t + 1, :].to_broadcast([P, MLA_H, half])
                        link(rope((qr_rot[:, t, :, 0:half], qr_rot[:, t, :, half:ROPE]), qr_raw[:, t, :, 0:half],
                                  qr_raw[:, t, :, half:ROPE], cos, sin, ropetmp))
                    V.tensor_copy(nmax[0:1, 0:1], rstd[0:1, 0, 0:1]).then_inc(dve_ready, 1)
                    for c in range(2):
                        g = n.g + 26 + 12 * c
                        for h in range(8):
                            copy_out(g + h, knT[:, 8 * c + h, :], S)
                        for q in range(2):
                            for t in range(T):
                                copy_out(g + 8 + 2 * q + t, vtok[:, t, (2 * c + q) * 512:(2 * c + q + 1) * 512], 512)
                    dve.wait_ge(g_read, n.g + 50)
                    attention(n, n.g + 50, False)
                    V.tensor_copy(nmax[0:1, 0:1], rinv[0:1, 0, 0:1]).then_inc(src_ready, T)
                elif kind == "ple":
                    dve.wait_ge(s_ple, 32 * (arg + 1))
                    linear(n, 2, lambda c, b: V.tensor_tensor(gt[:, b, c * 512:(c + 1) * 512], linear_bank(c, b),
                                                              bgate[:, c * 512:(c + 1) * 512], ALU.add))


NAMES = ["x", "c", "ada_w", "ada_b", "w_in", "conv_w", "gk_w2", "gk_b", "gla_norm_w", "w_out", "ln1_g", "ln1_b",
         "ln2_g", "ln2_b", "ffn_w_gate", "ffn_w_up", "ffn_w_down", "router_w", "moe_w_gate", "moe_w_up",
         "moe_w_down", "p_2", "ffn1_w_in_2", "ffn1_w_out_2", "ffn2_w_in_2", "ffn2_w_out_2", "ln_g_2", "ln_b_2",
         "ple_w_gate_2", "ple_b_gate_2", "ple_w_proj_2", "fox_w_in_2", "fox_b_f_2", "fox_w_o_2", "mla_w_dq_2",
         "mla_q_norm_2", "mla_w_uq_2", "mla_w_o_2", "kv_w_down_2", "kv_norm_2", "kv_w_up_2"]


def kernel(**inputs):
    import concourse.bacc as bacc
    from concourse.bass_utils import run_bass_kernel_spmd

    nc = bacc.Bacc("TRN2", target_bir_lowering=False, num_devices=1)
    arrays, aps = {}, {}
    for name in NAMES:
        a = np.ascontiguousarray(inputs[name])
        arrays[f"in_{name}"] = a
        aps[name] = nc.dram_tensor(f"in_{name}", a.shape, mybir.dt.from_np(a.dtype), kind="ExternalInput").ap()
    arrays["in_con"] = constants()
    aps["con"] = nc.dram_tensor("in_con", (P, NCONST), F32, kind="ExternalInput").ap()
    out = nc.dram_tensor("out_x", (1, S, D), F32, kind="ExternalOutput").ap()
    build(nc, aps, out)
    r = run_bass_kernel_spmd(nc, [arrays], core_ids=[0])
    return r.results[0]["out_x"]
```
